# Optimizing a Trainium2 kernel written in Bass

```python
import math
import jax, jax.numpy as jnp
from jax import lax
import numpy as np

D_MODEL = 1024
BATCH = 1
SEQ = 512
DEPTH = 4
DEC_BATCH = 8
DEC_SEQ = 1
PAST_LEN = 4096
PAGE_SIZE = 128

N_MIXERS = 3
N_SCONV_LAYERS = (DEPTH + 2) // 3
N_RWKV_LAYERS = (DEPTH + 1) // 3
N_GLA_LAYERS = DEPTH // 3
CONV_W = 3
RMS_EPS = 1e-6
N_MOD = 6
RWKV_HEAD = 64
RWKV_HEADS = D_MODEL // RWKV_HEAD
RWKV_DECAY_LORA = 64
RWKV_A_LORA = 64
RWKV_GATE_LORA = 128
RWKV_GN_EPS = 64e-5
GLA_HEADS = 4
GLA_DK_TOTAL = D_MODEL // 2
GLA_DV_TOTAL = D_MODEL
GLA_DK = GLA_DK_TOTAL // GLA_HEADS
GLA_DV = GLA_DV_TOTAL // GLA_HEADS
GLA_GATE_RANK = 16
GLA_GATE_NORMALIZER = 16.0
GLA_CHUNK = 64
D_FF = ((8 * D_MODEL // 3 + 127) // 128) * 128

kernel_name = 'hybrid_sconv_rwkv7_gla_convffn_adaln_step'

def rmsnorm(x, g, eps=RMS_EPS):
    xf = x.astype(jnp.float32)
    y = xf * lax.rsqrt(jnp.mean(xf * xf, axis=-1, keepdims=True) + eps)
    return (y * g.astype(jnp.float32)).astype(x.dtype)

def causal_dwconv(u, buf, w):
    T = u.shape[1]
    full = jnp.concatenate([buf.astype(u.dtype), u], axis=1)
    y = full[:, 0:T] * w[0]
    for j in range(1, CONV_W):
        y = y + full[:, j:j + T] * w[j]
    return y, full[:, T:]

def short_conv_mixer(x, buf, w_in, conv_w, w_out):
    b_gate, c_gate, xi = jnp.split(x @ w_in, 3, axis=-1)
    y, new_buf = causal_dwconv(c_gate * xi, buf, conv_w)
    return (b_gate * y) @ w_out, new_buf

def rwkv7_mixer(x, shift_buf, S0, mu, w_rkv, w0, w1, w2, a0, a1, a2, g1, g2, k_k, k_a, r_k,
                lnx_w, lnx_b, w_o):
    B, T, D = x.shape
    H, N = RWKV_HEADS, RWKV_HEAD
    prev = jnp.concatenate([shift_buf[:, None, :].astype(x.dtype), x[:, :-1]], axis=1)
    xx = prev - x
    xr, xw, xk, xv, xa, xg = [x + xx * mu[i] for i in range(6)]
    r = xr @ w_rkv[0]
    k = xk @ w_rkv[1]
    v = xv @ w_rkv[2]
    logw = -jax.nn.softplus(-(w0 + jnp.tanh(xw @ w1) @ w2)) - 0.5
    a = jax.nn.sigmoid(a0 + (xa @ a1) @ a2)
    g = jax.nn.sigmoid(xg @ g1) @ g2
    hd = lambda t: t.reshape(B, T, H, N).astype(jnp.float32)
    kk = hd(k * k_k)
    kk = kk / jnp.maximum(jnp.sqrt(jnp.sum(kk * kk, axis=-1, keepdims=True)), 1e-12)
    k = k * (1 + (a - 1) * k_a)
    rh, kh, vh, ah = hd(r), hd(k), hd(v), hd(a)
    decay = jnp.exp(-jnp.exp(hd(logw)))

    def step(S, inp):
        r_t, w_t, k_t, v_t, kk_t, a_t = inp
        sa = jnp.einsum('bhvk,bhk->bhv', S, -kk_t)
        S = (S * w_t[:, :, None, :] + sa[..., None] * (kk_t * a_t)[:, :, None, :]
             + v_t[..., None] * k_t[:, :, None, :])
        return S, jnp.einsum('bhvk,bhk->bhv', S, r_t)

    tm = lambda t: jnp.moveaxis(t, 1, 0)
    S, y = lax.scan(step, S0.astype(jnp.float32), (tm(rh), tm(decay), tm(kh), tm(vh), tm(kk), tm(ah)))
    y = jnp.moveaxis(y, 0, 1)
    mean = jnp.mean(y, axis=-1, keepdims=True)
    var = jnp.mean(jnp.square(y - mean), axis=-1, keepdims=True)
    y = ((y - mean) * lax.rsqrt(var + RWKV_GN_EPS)).reshape(B, T, D)
    y = y * lnx_w.astype(jnp.float32) + lnx_b.astype(jnp.float32)
    bonus = jnp.sum(rh * kh * r_k.astype(jnp.float32), axis=-1, keepdims=True) * vh
    y = y + bonus.reshape(B, T, D)
    out = (y.astype(x.dtype) * g) @ w_o
    return out, x[:, -1], S.astype(S0.dtype)

def gla_chunked(q, k, v, lg, S0):
    B, T, H, dk = q.shape
    dv = v.shape[-1]
    L = math.gcd(T, GLA_CHUNK)
    n = T // L

    def blk(t):
        return t.reshape(B, n, L, H, t.shape[-1]).transpose(1, 0, 3, 2, 4).astype(jnp.float32)

    qc, kc, vc = blk(q), blk(k), blk(v)
    G = jnp.cumsum(blk(lg), axis=-2)
    causal = jnp.tril(jnp.ones((L, L), dtype=bool))[:, :, None]

    def step(S, inp):
        qb, kb, vb, Gb = inp
        diff = jnp.where(causal, Gb[:, :, :, None, :] - Gb[:, :, None, :, :], -jnp.inf)
        A = jnp.sum(qb[:, :, :, None, :] * kb[:, :, None, :, :] * jnp.exp(diff), axis=-1)
        o = (jnp.einsum('bhij,bhjv->bhiv', A, vb)
             + jnp.einsum('bhik,bhkv->bhiv', qb * jnp.exp(Gb), S))
        GL = Gb[:, :, -1:, :]
        S = (jnp.exp(GL[:, :, 0, :])[..., None] * S
             + jnp.einsum('bhjk,bhjv->bhkv', kb * jnp.exp(GL - Gb), vb))
        return S, o

    S, o = lax.scan(step, S0.astype(jnp.float32), (qc, kc, vc, G))
    o = o.transpose(1, 0, 3, 2, 4).reshape(B, T, H, dv)
    return o, S

def gla_mixer(x, S0, w_in, wa1, wa2, ba, onorm_g, w_o):
    B, T, _ = x.shape
    H = GLA_HEADS
    q, k, v, og = jnp.split(x @ w_in, [GLA_DK_TOTAL, 2 * GLA_DK_TOTAL, 2 * GLA_DK_TOTAL + GLA_DV_TOTAL], axis=-1)
    lg = jax.nn.log_sigmoid(((x @ wa1) @ wa2 + ba).astype(jnp.float32)) / GLA_GATE_NORMALIZER
    hk = lambda t: t.reshape(B, T, H, GLA_DK)
    o, S = gla_chunked(hk(q) * GLA_DK ** -0.5, hk(k), v.reshape(B, T, H, GLA_DV), hk(lg), S0)
    o = rmsnorm(o, onorm_g).astype(x.dtype) * jax.nn.silu(og).reshape(B, T, H, GLA_DV)
    return o.reshape(B, T, GLA_DV_TOTAL) @ w_o, S.astype(S0.dtype)

def conv_ffn(x, buf, w_up, conv_w, conv_b, w_down):
    h_gate, h_val = jnp.split(x @ w_up, 2, axis=-1)
    hc, new_buf = causal_dwconv(h_gate, buf, conv_w)
    return (jax.nn.silu(hc + conv_b) * h_val) @ w_down, new_buf

def trunk(x, c, st_conv_a, st_shift_b, st_wkv_b, st_gla_c, st_conv_f, p):
    mod = jnp.einsum('bd,lde->lbe', jax.nn.silu(c), p['ada_w']) + p['ada_b'][:, None, :]
    new_a, new_sb, new_wb, new_gc, new_f = [], [], [], [], []
    h = x
    for l in range(DEPTH):
        sh_m, sc_m, gt_m, sh_f, sc_f, gt_f = jnp.split(mod[l][:, None, :], N_MOD, axis=-1)
        u = rmsnorm(h, p['norm_g'][l, 0]) * (1 + sc_m) + sh_m
        kind, j = l % N_MIXERS, l // N_MIXERS
        if kind == 0:
            out, nb = short_conv_mixer(u, st_conv_a[j], p['sconv_w_in'][j], p['sconv_conv_w'][j],
                                       p['sconv_w_out'][j])
            new_a.append(nb)
        elif kind == 1:
            out, nsh, nS = rwkv7_mixer(u, st_shift_b[j], st_wkv_b[j], p['rwkv_mu'][j], p['rwkv_w_rkv'][j],
                                       p['rwkv_w0'][j], p['rwkv_w1'][j], p['rwkv_w2'][j], p['rwkv_a0'][j],
                                       p['rwkv_a1'][j], p['rwkv_a2'][j], p['rwkv_g1'][j], p['rwkv_g2'][j],
                                       p['rwkv_k_k'][j], p['rwkv_k_a'][j], p['rwkv_r_k'][j],
                                       p['rwkv_lnx_w'][j], p['rwkv_lnx_b'][j], p['rwkv_w_o'][j])
            new_sb.append(nsh)
            new_wb.append(nS)
        else:
            out, nS = gla_mixer(u, st_gla_c[j], p['gla_w_in'][j], p['gla_wa1'][j], p['gla_wa2'][j],
                                p['gla_ba'][j], p['gla_onorm_g'][j], p['gla_w_o'][j])
            new_gc.append(nS)
        h = h + gt_m * rmsnorm(out, p['norm_g'][l, 1])
        u = rmsnorm(h, p['norm_g'][l, 2]) * (1 + sc_f) + sh_f
        out, nb = conv_ffn(u, st_conv_f[l], p['ffn_w_up'][l], p['ffn_conv_w'][l], p['ffn_conv_b'][l],
                           p['ffn_w_down'][l])
        new_f.append(nb)
        h = h + gt_f * rmsnorm(out, p['norm_g'][l, 3])
    return (h, jnp.stack(new_a), jnp.stack(new_sb), jnp.stack(new_wb), jnp.stack(new_gc), jnp.stack(new_f))

def setup_inputs(seed: int = 0) -> dict:
    key = jax.random.key(seed)
    ks = iter(jax.random.split(key, 64))

    def nrm(shape, scale=1.0):
        return jax.random.normal(next(ks), shape, jnp.float32) * scale

    def unif(shape, lo, hi):
        return jax.random.uniform(next(ks), shape, jnp.float32, lo, hi)

    D = D_MODEL
    NA, NB, NC = N_SCONV_LAYERS, N_RWKV_LAYERS, N_GLA_LAYERS
    H, N = RWKV_HEADS, RWKV_HEAD
    return {
        'x_prompt': nrm((BATCH, SEQ, D)),
        'x_sample': nrm((DEC_BATCH, DEC_SEQ, D)),
        'state_conv_a': nrm((NA, DEC_BATCH, CONV_W - 1, D)),
        'state_shift_b': nrm((NB, DEC_BATCH, D)),
        'state_wkv_b': nrm((NB, DEC_BATCH, H, N, N)),
        'state_gla_c': nrm((NC, DEC_BATCH, GLA_HEADS, GLA_DK, GLA_DV)),
        'state_conv_ffn': nrm((DEPTH, DEC_BATCH, CONV_W - 1, D_FF)),
        'c_prompt': nrm((BATCH, D)),
        'c_sample': nrm((DEC_BATCH, D)),
        'ada_w': nrm((DEPTH, D, N_MOD * D), D ** -0.5),
        'ada_b': nrm((DEPTH, N_MOD * D), 0.02),
        'norm_g': 1.0 + nrm((DEPTH, 4, D), 0.05),
        'sconv_w_in': nrm((NA, D, 3 * D), D ** -0.5),
        'sconv_conv_w': nrm((NA, CONV_W, D), CONV_W ** -0.5),
        'sconv_w_out': nrm((NA, D, D), D ** -0.5),
        'rwkv_mu': unif((NB, 6, D), 0.0, 1.0),
        'rwkv_w_rkv': nrm((NB, 3, D, D), D ** -0.5),
        'rwkv_w0': unif((NB, D), -4.0, 1.0),
        'rwkv_w1': nrm((NB, D, RWKV_DECAY_LORA), D ** -0.5),
        'rwkv_w2': nrm((NB, RWKV_DECAY_LORA, D), 0.5 * RWKV_DECAY_LORA ** -0.5),
        'rwkv_a0': nrm((NB, D), 0.1),
        'rwkv_a1': nrm((NB, D, RWKV_A_LORA), D ** -0.5),
        'rwkv_a2': nrm((NB, RWKV_A_LORA, D), RWKV_A_LORA ** -0.5),
        'rwkv_g1': nrm((NB, D, RWKV_GATE_LORA), D ** -0.5),
        'rwkv_g2': nrm((NB, RWKV_GATE_LORA, D), RWKV_GATE_LORA ** -0.5),
        'rwkv_k_k': 0.85 + nrm((NB, D), 0.05),
        'rwkv_k_a': 1.0 + nrm((NB, D), 0.05),
        'rwkv_r_k': nrm((NB, H, N), 0.1),
        'rwkv_lnx_w': 1.0 + nrm((NB, D), 0.05),
        'rwkv_lnx_b': nrm((NB, D), 0.02),
        'rwkv_w_o': nrm((NB, D, D), D ** -0.5),
        'gla_w_in': nrm((NC, D, 2 * GLA_DK_TOTAL + 2 * GLA_DV_TOTAL), D ** -0.5),
        'gla_wa1': nrm((NC, D, GLA_GATE_RANK), D ** -0.5),
        'gla_wa2': nrm((NC, GLA_GATE_RANK, GLA_DK_TOTAL), GLA_GATE_RANK ** -0.5),
        'gla_ba': nrm((NC, GLA_DK_TOTAL), 0.1),
        'gla_onorm_g': 1.0 + nrm((NC, GLA_DV), 0.05),
        'gla_w_o': nrm((NC, GLA_DV_TOTAL, D), GLA_DV_TOTAL ** -0.5),
        'ffn_w_up': nrm((DEPTH, D, 2 * D_FF), D ** -0.5),
        'ffn_conv_w': nrm((DEPTH, CONV_W, D_FF), CONV_W ** -0.5),
        'ffn_conv_b': nrm((DEPTH, D_FF), 0.02),
        'ffn_w_down': nrm((DEPTH, D_FF, D), D_FF ** -0.5),
    }

def reference(x_prompt, x_sample, state_conv_a, state_shift_b, state_wkv_b, state_gla_c, state_conv_ffn,
              c_prompt, c_sample, ada_w, ada_b, norm_g, sconv_w_in, sconv_conv_w, sconv_w_out,
              rwkv_mu, rwkv_w_rkv, rwkv_w0, rwkv_w1, rwkv_w2, rwkv_a0, rwkv_a1, rwkv_a2, rwkv_g1, rwkv_g2,
              rwkv_k_k, rwkv_k_a, rwkv_r_k, rwkv_lnx_w, rwkv_lnx_b, rwkv_w_o,
              gla_w_in, gla_wa1, gla_wa2, gla_ba, gla_onorm_g, gla_w_o,
              ffn_w_up, ffn_conv_w, ffn_conv_b, ffn_w_down):
    p = dict(ada_w=ada_w, ada_b=ada_b, norm_g=norm_g,
             sconv_w_in=sconv_w_in, sconv_conv_w=sconv_conv_w, sconv_w_out=sconv_w_out,
             rwkv_mu=rwkv_mu, rwkv_w_rkv=rwkv_w_rkv, rwkv_w0=rwkv_w0, rwkv_w1=rwkv_w1, rwkv_w2=rwkv_w2,
             rwkv_a0=rwkv_a0, rwkv_a1=rwkv_a1, rwkv_a2=rwkv_a2, rwkv_g1=rwkv_g1, rwkv_g2=rwkv_g2,
             rwkv_k_k=rwkv_k_k, rwkv_k_a=rwkv_k_a, rwkv_r_k=rwkv_r_k, rwkv_lnx_w=rwkv_lnx_w,
             rwkv_lnx_b=rwkv_lnx_b, rwkv_w_o=rwkv_w_o,
             gla_w_in=gla_w_in, gla_wa1=gla_wa1, gla_wa2=gla_wa2, gla_ba=gla_ba,
             gla_onorm_g=gla_onorm_g, gla_w_o=gla_w_o,
             ffn_w_up=ffn_w_up, ffn_conv_w=ffn_conv_w, ffn_conv_b=ffn_conv_b, ffn_w_down=ffn_w_down)
    bp = x_prompt.shape[0]
    zeros = lambda s: jnp.zeros((s.shape[0], bp) + s.shape[2:], x_prompt.dtype)
    y_p, ca_p, sb_p, wb_p, gc_p, cf_p = trunk(x_prompt, c_prompt, zeros(state_conv_a), zeros(state_shift_b),
                                              zeros(state_wkv_b), zeros(state_gla_c), zeros(state_conv_ffn), p)
    y_s, ca_s, sb_s, wb_s, gc_s, cf_s = trunk(x_sample, c_sample, state_conv_a, state_shift_b, state_wkv_b,
                                              state_gla_c, state_conv_ffn, p)
    return (y_p, y_s, ca_p, ca_s, sb_p, sb_s, wb_p, wb_s, gc_p, gc_s, cf_p, cf_s)


_drawn_inputs = setup_inputs


def setup_inputs(seed=0):
    import zlib

    import numpy as np

    out = dict(_drawn_inputs(seed))
    spreads = {}
    factors = {'rwkv_lnx_b': 3.781, 'gla_onorm_g': 2.92, 'ffn_conv_b': 3.686}
    for name, (base, spread) in spreads.items():
        noise = np.random.default_rng([zlib.crc32(name.encode()), seed]).standard_normal(out[name].shape)
        drawn = base * np.exp(spread * noise) if base else spread * noise
        out[name] = __import__('jax').numpy.asarray(drawn.astype(out[name].dtype))
    for name, factor in factors.items():
        out[name] = (out[name] * factor).astype(out[name].dtype)
    return out
```

```python
import math
from contextlib import ExitStack

import concourse.bass as bass
from concourse import mybir

F32 = mybir.dt.float32
F32R = mybir.dt.float32r
ALU = mybir.AluOpType
ACT = mybir.ActivationFunctionType
AX = mybir.AxisListType

P = 128
D = 1024
TP = 512
NS = 8
T = TP + NS
HALF = T // 2
KT = D // P
DFF = 2816
FT = DFF // P
NSEQ = 1 + NS
MODT = 6 * KT
GT = 3 * KT
GW = 2 + TP + 3 * NS
CWD = GW - 2
EPS = 1e-6
HD = 64
NCH = TP // HD
RWKV_GN_EPS = 64e-5
DECAY = -math.exp(-0.5)
LEVELS = (2, 4, 8, 16, 32)
GH = 4
GDV = 256
GC = P
NGC = TP // GC
G_LEVELS = (64, 32, 16, 8, 4, 2, 1)
SCW = 512
DOWN_K = ((0, 8), (8, 7), (15, 7))


def ds(i, n):
    return bass.ds(i, n)


def trunk_kernel(nc, A, O, depth):
    ctx = ExitStack()
    with ctx:
        cursor = [(nc.sbuf_base + 63) // 64 * 64]

        def at(name, shape, dt, offset):
            return nc.alloc_sbuf_tensor_at(name, shape, dt, offset=offset)

        def sb(name, shape, dt=F32):
            n = 4
            for s in shape[1:]:
                n *= s
            off = cursor[0]
            cursor[0] = (off + n + 31) // 32 * 32
            return at(name, shape, dt, off)

        h = sb("h", [P, KT, T])
        u_off = cursor[0]
        u_hi = sb("u_hi", [P, KT, T], F32R)
        u_lo = sb("u_lo", [P, KT, T], F32R)
        proj = at("proj", [P, KT, T], F32, u_off)
        big_off = cursor[0]
        hid_hi = sb("hid_hi", [P, FT, T], F32R)
        hid_lo = sb("hid_lo", [P, FT, T], F32R)
        w_raw = sb("w_raw", [P, 2, KT, P])
        w_hi_at = cursor[0]
        w_hi = sb("w_hi", [P, 2, KT, P], F32R)
        w_lo = sb("w_lo", [P, 2, KT, P], F32R)
        ada_raw = sb("ada_raw", [P, 2, KT, P])
        vecs = sb("vecs", [P, 7 * P])
        mod_m = sb("mod_m", [P, GT, NSEQ])
        mod_f = sb("mod_f", [P, GT, NSEQ])
        cT = sb("cT", [P, KT, NSEQ])
        ident = sb("ident", [P, P])
        ones = sb("ones", [P, P])
        eps_col = sb("eps_col", [P, 1])
        std_at = cursor[0]
        std = sb("std", [P, T])
        rstd = sb("rstd", [P, T])
        gate_at = cursor[0]
        gate = sb("gate", [P, 2, GW])
        conv = sb("conv", [P, 2, GW])
        csb = sb("csb", [P, 2, T])
        prod = sb("prod", [P, 2, T])
        st_in = sb("st_in", [P, 2, P])
        tail = sb("tail", [P, 2, 2 + NS])
        rows = sb("rows", [2 + NS, 2, P])
        s8 = sb("s8", [P, 2, KT, NS])
        pair_ones = sb("pair_ones", [P, P])
        sc_mask = sb("sc_mask", [P, SCW])
        low_mask = sb("low_mask", [P, P])
        up_masks = sb("up_masks", [P, 1 + len(LEVELS), P])
        eps_gn = sb("eps_gn", [P, 1])
        prev_s = sb("prev_s", [P, KT, NS])
        one_less_ka = sb("one_less_ka", [P, KT])
        decay_s = sb("decay_s", [P, KT, NS])
        assert cursor[0] <= nc.sbuf_usable_end, cursor[0]
        slab_bytes = KT * T * 4

        def slab(name, i, dt=F32):
            return at(name, [P, KT, T], dt, big_off + i * slab_bytes)

        xb_hi, xb_lo = slab("xb_hi", 0, F32R), slab("xb_lo", 1, F32R)
        rw_G, rw_kk, rw_b = slab("rw_G", 0), slab("rw_kk", 1), slab("rw_b", 2)
        rw_u, rw_r, rw_k = slab("rw_u", 2), slab("rw_r", 3), slab("rw_k", 4)
        rw_y, proj_b = rw_kk, rw_G
        gate_off = gate_at
        rw_v = at("rw_v", [P, KT, T], F32, gate_off)
        rw_d = at("rw_d", [P, KT, T], F32, gate_off)
        half_off = big_off + 5 * slab_bytes
        t_lora = at("t_lora", [HD, 2, T], F32, half_off)
        rw_ST = at("rw_ST", [P, KT, P], F32, half_off)
        t_g = at("t_g", [HD, 2, T], F32, half_off + 2 * T * 4)
        xf = at("xf", [P, 2, T], F32, std_at)
        lora2 = at("lora2", [HD, 2, D], F32, u_off + slab_bytes)
        gn_tmp = slab("gn_tmp", 0)
        gated_sb = at("gated_sb", [P, 2, T], F32, big_off + 4 * T * 4)
        g2 = at("g2", [HD, 2, D], F32, big_off + 2 * slab_bytes)
        tmp8 = at("tmp8", [P, KT, T], F32, u_off)
        s_state = at("s_state", [P, HD, HD], F32, u_off)
        s_tmp = at("s_tmp", [P, HD, HD], F32, u_off + slab_bytes)
        s_rows = at("s_rows", [NS, 6, D], F32, w_hi_at)
        s_vec = at("s_vec", [P, 8, HD], F32, std_at)
        bd = []
        for q in range(2):
            o = u_off + q * slab_bytes
            names = ("Z", "B", "K", "Bh", "Kh", "Vf")
            d = {nm: at(f"bd_{nm}{q}", [P, 4, P], F32, o + i * 2048) for i, nm in enumerate(names)}
            d["R"] = at(f"bd_R{q}", [P, 4, HD], F32, o + 6 * 2048)
            d["Em"] = at(f"bd_Em{q}", [P, 4, HD], F32, o + 6 * 2048 + 1024)
            d["Ep"] = at(f"bd_Ep{q}", [P, 4, HD + 1], F32, o + 6 * 2048 + 2048)
            bd.append(d)
        sc = at("sc", [P, 4, SCW], F32, w_hi_at)
        mmt = at("mmt", [P, 4, 2 * P], F32, w_hi_at + 8192)
        ct = at("ct", [P, 4, P], F32, w_hi_at + 8192 + 4096)
        t1 = at("t1", [P, 4, P], F32, w_hi_at + 8192 + 6144)
        tok = at("tok", [P, 4, 3 * P], F32, w_hi_at + 16384)
        rhs_sb = at("rhs_sb", [P, 4, P], F32, w_hi_at + 16384 + 6144)
        uu = at("uu", [P, 4, P], F32, std_at)
        wkv_out = at("wkv_out", [P, KT, HD], F32, w_hi_at)
        g_in = at("g_in", [P, 3 * KT, T], F32, big_off)
        g_q, g_k, g_v, g_og = (g_in[:, 0:GH, :], g_in[:, GH:2 * GH, :], g_in[:, KT:2 * KT, :],
                               g_in[:, 2 * KT:3 * KT, :])
        g_o = at("g_o", [P, KT, T], F32, big_off + slab_bytes)
        g_sS = at("g_sS", [P, NS * GH, GDV], F32, big_off + 3 * slab_bytes)
        g_Kt = at("g_Kt", [P, NGC, GH, P], F32, half_off)
        g_AT = at("g_AT", [P, GH * NGC, P], F32, u_off)
        g_Vt = at("g_Vt", [P, NGC, D], F32, u_off + 8192)
        g_G = at("g_G", [P, GH, TP], F32, u_off + 8192 + 16384)
        g_Ql = at("g_Ql", [P, GH, TP], F32, gate_off)
        g_Kl = at("g_Kl", [P, GH, TP], F32, gate_off + 8192)
        g_z = at("g_z", [P, GH, T], F32, w_hi_at)
        g_e = at("g_e", [P, GH, T], F32, w_hi_at + GH * T * 4)
        g_S = at("g_S", [P, GH, GDV], F32, w_hi_at + 2 * GH * T * 4)
        g_end = at("g_end", [P, GH, NGC], F32, w_hi_at + 2 * GH * T * 4 + 4096)
        g_dec = at("g_dec", [P, GH, NS], F32, w_hi_at + 2 * GH * T * 4 + 4096 + 64)
        t_ga = at("t_ga", [8, 2, T], F32, half_off)
        wa2 = at("wa2", [8, 2, GH * P], F32, half_off + 2 * T * 4)
        g_sq = at("g_sq", [P, 2, T], F32, gate_off)
        g_vrow = at("g_vrow", [NS, D], F32, std_at)
        shift_rows = at("shift_rows", [NSEQ, D], F32, big_off + 3 * slab_bytes)
        shift_in = at("shift_in", [NS, D], F32, big_off + 3 * slab_bytes + 4096)
        normed = prod
        usb = conv
        sq = csb
        vec_rows = at("vec_rows", [P, 7, P], F32, big_off)
        x_rows = at("x_rows", [P, 4, D], F32, big_off + 4096)
        xs_rows = at("xs_rows", [NS, D], F32, big_off + 4096 + 16384)
        c_rows = at("c_rows", [NSEQ, D], F32, big_off + 8192 + 16384)
        y_rows = at("y_rows", [P, 5, D], F32, big_off)

        bank = [ctx.enter_context(nc.psum_tensor(f"bank{i}", [P, 512], F32)) for i in range(8)]
        tile_ps = [(bank[0], bank[1]), (bank[2], bank[3])]
        ss_ps = (bank[4], bank[5])
        st_ps, ada_ps, tail_ps = bank[4], bank[6], bank[7]

        def sem(name):
            return ctx.enter_context(nc.semaphore(name))

        consts_ready = sem("consts_ready")
        rows_loaded = sem("rows_loaded")
        c_silu = sem("c_silu")
        pro_turned = sem("pro_turned")
        x_copied = sem("x_copied")
        small_copied = sem("small_copied")
        w_loaded = [sem(f"w_loaded{i}") for i in range(2)]
        hi_done = sem("hi_done")
        lo_done = sem("lo_done")
        block_done = sem("block_done")
        tile_free = [sem(f"tile_free{i}") for i in range(2)]
        ada_loaded = [sem(f"ada_loaded{i}") for i in range(2)]
        ada_used = sem("ada_used")
        mod_ready = sem("mod_ready")
        st_loaded = [sem(f"st_loaded{i}") for i in range(2)]
        st_turned = sem("st_turned")
        st_zeroed = sem("st_zeroed")
        st_placed = sem("st_placed")
        gate_ready = sem("gate_ready")
        conv_done = sem("conv_done")
        silu_done = sem("silu_done")
        hid_ready = sem("hid_ready")
        tail_copied = sem("tail_copied")
        tail_turned = sem("tail_turned")
        rows_copied = sem("rows_copied")
        rows_out = [sem(f"rows_out{i}") for i in range(2)]
        sq_done = sem("sq_done")
        sq_used = sem("sq_used")
        ss_done = sem("ss_done")
        std_done = sem("std_done")
        norm_done = sem("norm_done")
        usb_done = sem("usb_done")
        uhi_done = sem("uhi_done")
        u_ready = sem("u_ready")
        h_ready = sem("h_ready")
        sum_ready = sem("sum_ready")
        y_turned = sem("y_turned")
        y_left = sem("y_left")
        y_right = sem("y_right")
        outs_done = sem("outs_done")
        dve_step = sem("dve_step")
        pool_step = sem("pool_step")
        masks_ready = sem("masks_ready")
        wa2_loaded, gz_mm, gz_done, gabs_done, gsoft_done, glg_done = (
            sem("wa2_loaded"), sem("gz_mm"), sem("gz_done"), sem("gabs_done"), sem("gsoft_done"), sem("glg_done"))
        gS_loaded, gdec_done, gG_done, gexp_done, gq_ready = (
            sem("gS_loaded"), sem("gdec_done"), sem("gG_done"), sem("gexp_done"), sem("gq_ready"))
        gtail_ready, gkhat_ready, gk_turned, gk_copied, gv_turned, gv_copied = (
            sem("gtail_ready"), sem("gkhat_ready"), sem("gk_turned"), sem("gk_copied"),
            sem("gv_turned"), sem("gv_copied"))
        gdiff_ready, glevel_ready, glevel_mm, glevel_put = (
            sem("gdiff_ready"), sem("glevel_ready"), sem("glevel_mm"), sem("glevel_put"))
        gvrow_turned, gvrow_copied, gvb_mm, gvb_used, gs_ready, gs_o_mm, gs_out = (
            sem("gvrow_turned"), sem("gvrow_copied"), sem("gvb_mm"), sem("gvb_used"), sem("gs_ready"),
            sem("gs_o_mm"), sem("gs_out"))
        go_mm, go_copied, gsu_mm, gS_ready, gS_out, gsilu_done = (
            sem("go_mm"), sem("go_copied"), sem("gsu_mm"), sem("gS_ready"), sem("gS_out"), sem("gsilu_done"))
        gsq_done, gss_mm, gon_std, gon_done, gyhi_done, gy_ready = (
            sem("gsq_done"), sem("gss_mm"), sem("gon_std"), sem("gon_done"), sem("gyhi_done"), sem("gy_ready"))
        shift_loaded, shift_turned = sem("shift_loaded"), sem("shift_turned")
        us_ready = sem("us_ready")
        urows_turned, urows_copied, shift_out = sem("urows_turned"), sem("urows_copied"), sem("shift_out")
        mixed, xhi_done, x_ready = sem("mixed"), sem("xhi_done"), sem("x_ready")
        lora_loaded, zw_done, za_done = sem("lora_loaded"), sem("zw_done"), sem("za_done")
        sig_w, sig_a = sem("sig_w"), sem("sig_a")
        ksq_done, ksum_done, knorm_done, kk_ready = (sem("ksq_done"), sem("ksum_done"), sem("knorm_done"),
                                                     sem("kk_ready"))
        prep_done = sem("prep_done")
        decay_done, srow_turned, srow_copied = sem("decay_done"), sem("srow_turned"), sem("srow_copied")
        svec_loaded, sstate_loaded, s_y_done = sem("svec_loaded"), sem("sstate_loaded"), sem("s_y_done")
        s_state_out, syrow_loaded, sy_turned, sy_placed = (sem("s_state_out"), sem("syrow_loaded"),
                                                           sem("sy_turned"), sem("sy_placed"))
        bd_zeroed = sem("bd_zeroed")
        exp_done, bd_ready, hat_ready, vf_ready = sem("exp_done"), sem("bd_ready"), sem("hat_ready"), sem("vf_ready")
        sc_done, tok_done, tok_ready = sem("sc_done"), sem("tok_done"), sem("tok_ready")
        ct_ready, t1_mm, t1_ready, d_mm, mmt_ready = (sem("ct_ready"), sem("t1_mm"), sem("t1_ready"), sem("d_mm"),
                                                      sem("mmt_ready"))
        rhs_mm, rhs_ready, u_mm, uu_ready = sem("rhs_mm"), sem("rhs_ready"), sem("u_mm"), sem("uu_ready")
        y_mm, y_ready, st_mm, st_updated = sem("y_mm"), sem("y_ready"), sem("st_mm"), sem("st_updated")
        wkv_turned, wkv_copied, wkv_out_done = sem("wkv_turned"), sem("wkv_copied"), sem("wkv_out_done")
        g2_loaded, mean_mm, centred, csq_done, var_mm, gstd_done, ynorm_done, yaff_done = (
            sem("g2_loaded"), sem("mean_mm"), sem("centred"), sem("csq_done"), sem("var_mm"), sem("gstd_done"),
            sem("ynorm_done"), sem("yaff_done"))
        rk_ready, bonus_mm, g_mm, gated, yhi_done, xy_ready = (sem("rk_ready"), sem("bonus_mm"), sem("g_mm"),
                                                               sem("gated"), sem("yhi_done"), sem("xy_ready"))

        col = {}
        pieces = []
        nrow = 0
        for name, ap in (
            ("norm_g", A["norm_g"].rearrange("l s (t p) -> (l s t) p", p=P)),
            ("ada_b", A["ada_b"].rearrange("l (t p) -> (l t) p", p=P)),
            ("ffn_conv_w", A["ffn_conv_w"].rearrange("l j (t p) -> (l j t) p", p=P)),
            ("ffn_conv_b", A["ffn_conv_b"].rearrange("l (t p) -> (l t) p", p=P)),
            ("sconv_conv_w", A["sconv_conv_w"].rearrange("l j (t p) -> (l j t) p", p=P)),
            ("rwkv_mu", A["rwkv_mu"].rearrange("l i (t p) -> (l i t) p", p=P)),
            ("rwkv_w0", A["rwkv_w0"].rearrange("l (t p) -> (l t) p", p=P)),
            ("rwkv_a0", A["rwkv_a0"].rearrange("l (t p) -> (l t) p", p=P)),
            ("rwkv_k_k", A["rwkv_k_k"].rearrange("l (t p) -> (l t) p", p=P)),
            ("rwkv_k_a", A["rwkv_k_a"].rearrange("l (t p) -> (l t) p", p=P)),
            ("rwkv_r_k", A["rwkv_r_k"].rearrange("l (t a) n -> (l t) (a n)", a=2)),
            ("rwkv_lnx_w", A["rwkv_lnx_w"].rearrange("l (t p) -> (l t) p", p=P)),
            ("rwkv_lnx_b", A["rwkv_lnx_b"].rearrange("l (t p) -> (l t) p", p=P)),
            ("gla_ba", A["gla_ba"].rearrange("l (t p) -> (l t) p", p=P)),
            ("gla_onorm_g", A["gla_onorm_g"].rearrange("l (t p) -> (l t) p", p=P)),
        ):
            col[name] = nrow
            done, n = 0, ap.shape[0]
            while done < n:
                k = min(n - done, P - nrow % P)
                pieces.append((nrow // P, nrow % P, k, ap[done:done + k, :]))
                done += k
                nrow += k
        NVG = (nrow + P - 1) // P
        NLOADS = len(pieces) + 4 + 1 + 2

        def vec(name, i):
            c = col[name] + i
            return vecs[:, ds(c, 1)]

        plan = []
        count = dict(blk=0, tile=0, unit=0, ada=GT, norm=0, split=0)

        def phase(kind, layer, iters, blk, tile, unit, ada, **more):
            plan.append(dict(kind=kind, l=layer, iters=iters, **{k: v for k, v in count.items()}, **more))
            count["blk"] += iters * blk
            count["tile"] += iters * tile
            count["unit"] += iters * unit
            count["ada"] += iters * ada

        def norm(kind, layer, **more):
            phase(kind, layer, 0, 0, 0, 0, 0, **more)
            count["norm"] += 1

        post = 0
        pre = 0
        for l in range(depth):
            mixer = l % 3
            norm("pre", l, mod=mod_m, group=2 * l, pre=pre, post=post, full=mixer == 1)
            count["split"] += mixer != 1
            pre += 1
            if mixer == 0:
                phase("sconv", l, KT // 2, 6, 6, 2, 6, pre=pre)
            elif mixer == 1:
                phase("rproj", l, 1, 28, 28, 0, GT, pre=pre)
                phase("rwkv", l, 0, 0, 0, 0, 0)
            else:
                phase("gproj", l, 1, 26, 26, 0, GT, pre=pre)
                phase("gla", l, 0, 0, 0, 0, 0)
            hid_x = mixer == 0
            phase("out", l, KT // 2, 2, 2, 0, 0, pre=pre,
                  x=(hid_hi, hid_lo, hid_ready, count["unit"] - KT) if hid_x else (u_hi, u_lo, (xy_ready, gy_ready)[mixer - 1], 0),
                  proj=proj if hid_x else proj_b)
            norm("post", l, mod=mod_m, sub=1, post=post, proj=proj if hid_x else proj_b)
            post += 1
            norm("pre", l, mod=mod_f, group=2 * l + 1, pre=pre, post=post, full=False)
            count["split"] += 1
            pre += 1
            phase("up", l, FT // 2, 4, 4, 2, 0, pre=pre, up_unit=l * FT)
            phase("down", l, KT // 2, 6, 2, 0, 6 if l + 1 < depth else 0, proj=proj)
            norm("post", l, mod=mod_f, sub=3, post=post, proj=proj)
            post += 1
        NBLK, NUNIT = count["blk"], count["unit"]
        for p in plan:
            p["last"] = p["kind"] == "down" and p["l"] == depth - 1

        def ada_group(p):
            return p["ada"] // GT

        block = ctx.enter_context(nc.Block())

        @block.sync
        def _(sp):
            for g, r, k, ap in pieces:
                sp.dma_start(vec_rows[r:r + k, g, :], ap).then_inc(rows_loaded, 16)
            sp.dma_start(c_rows[0:1, :], A["c_prompt"]).then_inc(rows_loaded, 16)
            sp.dma_start(c_rows[1:NSEQ, :], A["c_sample"]).then_inc(rows_loaded, 16)
            for t in range(4):
                sp.dma_start(x_rows[:, t, :], A["x_prompt"][0, t * P:(t + 1) * P, :]).then_inc(rows_loaded, 16)
            sp.dma_start(xs_rows[:, :], A["x_sample"].rearrange("b o d -> (b o) d")).then_inc(rows_loaded, 16)

            def load_block(n, s, src):
                sp.wait_ge(lo_done, n + 1)
                nk = src.shape[1]
                m = src.shape[2]
                sp.dma_start(w_raw[:, s, 0:nk, 0:m], src).then_inc(w_loaded[s], 16)

            def load_ada(a, s, l, t):
                sp.wait_ge(ada_used, a + 1)
                src = A["ada_w"][l].rearrange("(k p) c -> p k c", p=P)[:, :, ds(t * P, P)]
                sp.dma_start(ada_raw[:, s, :, :], src).then_inc(ada_loaded[s], 16)

            def load_state(q, src):
                sp.wait_ge(st_turned, q + 1)
                sp.dma_start(st_in[0:2 * NS, q_par, :], src).then_inc(st_loaded[q_par], 16)

            with sp.Fori(0, GT // 2) as it:
                for s in range(2):
                    load_ada(2 * it + s, s, 0, 2 * it + s)
            sp.wait_ge(st_zeroed, 1)
            for p in plan:
                l, n0, q0, a0 = p["l"], p["blk"], p["unit"], p["ada"]
                j = l // 3
                if p["kind"] == "sconv":
                    w = A["sconv_w_in"][j].rearrange("(k p) c -> p k c", p=P)
                    st = A["state_conv_a"][j].rearrange("b r c -> (b r) c")
                    with sp.Fori(0, p["iters"]) as it:
                        for e in range(2):
                            m = 2 * it + e
                            q_par = e
                            load_state(q0 + m, st[:, ds(m * P, P)])
                            for i, part in enumerate((1, 2, 0)):
                                k = 3 * e + i
                                load_block(n0 + 6 * it + k, k % 2, w[:, :, ds((part * KT + m) * P, P)])
                                load_ada(a0 + 6 * it + k, k % 2, l, GT + 6 * it + k)
                elif p["kind"] == "rproj":
                    for k, src in enumerate((A["rwkv_w1"][j], A["rwkv_a1"][j], A["rwkv_g1"][j][:, 0:HD],
                                             A["rwkv_g1"][j][:, HD:2 * HD])):
                        if k == 2:
                            sp.wait_ge(usb_done, KT * p["pre"])
                            sp.dma_start(shift_in[:, :], A["state_shift_b"][j]).then_inc(shift_loaded, 16)
                        load_block(n0 + k, k % 2, src.rearrange("(k p) c -> p k c", p=P))
                    for i in range(3):
                        w = A["rwkv_w_rkv"][j, i].rearrange("(k p) c -> p k c", p=P)
                        with sp.Fori(0, KT // 2) as it:
                            for e in range(2):
                                load_block(n0 + 4 + KT * i + 2 * it + e, e, w[:, :, ds((2 * it + e) * P, P)])
                                load_ada(a0 + KT * i + 2 * it + e, e, l, GT + KT * i + 2 * it + e)
                    sp.wait_ge(block_done, n0 + 28 + 2)
                    sp.dma_start(lora2[:, 0, :], A["rwkv_w2"][j]).then_inc(lora_loaded, 16)
                    sp.dma_start(lora2[:, 1, :], A["rwkv_a2"][j]).then_inc(lora_loaded, 16)
                elif p["kind"] == "gproj":
                    for k in range(2):
                        load_block(n0 + k, k % 2, A["gla_wa1"][0][:, 8 * k:8 * k + 8].rearrange("(k p) c -> p k c", p=P))
                    w = A["gla_w_in"][0].rearrange("(k p) c -> p k c", p=P)
                    with sp.Fori(0, GT // 2) as it:
                        for e in range(2):
                            load_block(n0 + 2 + 2 * it + e, e, w[:, :, ds((2 * it + e) * P, P)])
                            load_ada(a0 + 2 * it + e, e, l, GT + 2 * it + e)
                    sp.dma_start(wa2[:, :, :], A["gla_wa2"][0].rearrange("(i r) c -> r i c", i=2)).then_inc(wa2_loaded, 16)
                    st = A["state_gla_c"][0].rearrange("b h k v -> k (b h) v")
                    for half in range(2):
                        hs = slice(half * NS * GH // 2, (half + 1) * NS * GH // 2)
                        sp.dma_start(g_sS[:, hs, :], st[:, hs, :]).then_inc(gS_loaded, 16)
                elif p["kind"] == "out":
                    w = {0: A["sconv_w_out"][j], 1: A["rwkv_w_o"][j % 1], 2: A["gla_w_o"][j % 1]}[l % 3]
                    w = w.rearrange("(k p) c -> p k c", p=P)
                    with sp.Fori(0, p["iters"]) as it:
                        for e in range(2):
                            load_block(n0 + 2 * it + e, e, w[:, :, ds((2 * it + e) * P, P)])
                elif p["kind"] == "up":
                    w = A["ffn_w_up"][l].rearrange("(k p) c -> p k c", p=P)
                    st = A["state_conv_ffn"][l].rearrange("b r c -> (b r) c")
                    with sp.Fori(0, p["iters"]) as it:
                        for e in range(2):
                            m = 2 * it + e
                            q_par = e
                            load_state(q0 + m, st[:, ds(m * P, P)])
                            for part in range(2):
                                load_block(n0 + 4 * it + 2 * e + part, part, w[:, :, ds((part * FT + m) * P, P)])
                elif p["kind"] == "down":
                    w = A["ffn_w_down"][l].rearrange("(k p) c -> p k c", p=P)
                    with sp.Fori(0, p["iters"]) as it:
                        for e in range(2):
                            for i, (k0, nk) in enumerate(DOWN_K):
                                k = 3 * e + i
                                load_block(n0 + 6 * it + k, k % 2, w[:, k0:k0 + nk, ds((2 * it + e) * P, P)])
                                if l + 1 < depth:
                                    load_ada(a0 + 6 * it + k, k % 2, l + 1, 6 * it + k)
            for l in range(depth):
                sp.dma_start(O["conv_ffn_sample"][l, :, 0, :], A["state_conv_ffn"][l, :, 1, :]).then_inc(outs_done, 16)
            n_copies = depth
            if depth > 2:
                sp.wait_ge(gs_out, 32)
                sp.wait_ge(gS_out, 16)
            if depth > 1:
                sp.wait_ge(s_state_out, 16)
                sp.wait_ge(shift_out, 32)
                sp.wait_ge(wkv_out_done, 32)
            for j in range((depth + 2) // 3):
                sp.dma_start(O["conv_a_sample"][j, :, 0, :], A["state_conv_a"][j, :, 1, :]).then_inc(outs_done, 16)
                n_copies += 1
            sp.wait_ge(y_left, 5)
            sp.wait_ge(y_right, 5)
            for t in range(4):
                sp.dma_start(O["y_prompt"][0, t * P:(t + 1) * P, :], y_rows[:, t, :]).then_inc(outs_done, 16)
            sp.dma_start(O["y_sample"].rearrange("b o d -> (b o) d"), y_rows[0:NS, 4, :]).then_inc(outs_done, 16)
            sp.wait_ge(outs_done, 16 * (n_copies + 5))

        @block.gpsimd
        def _(pool):
            pool.memset(w_raw[:, :, :, :], 0.0).then_inc(lo_done, 2)
            pool.memset(ident[:, :], 0.0).then_inc(pool_step, 1)
            pool.memset(ones[:, :], 1.0).then_inc(consts_ready, 1)
            pool.wait_ge(pool_step, 1)
            pool.affine_select(out=ident[:, :], in_=ident[:, :], compare_op=ALU.not_equal, fill=1.0, base=0,
                               pattern=[[-1, P]], channel_multiplier=1).then_inc(consts_ready, 1)
            pool.memset(eps_col[:, :], EPS)
            pool.memset(tail[:, :, :], 0.0).then_inc(tail_copied, 2)
            pool.memset(st_in[:, :, :], 0.0).then_inc(st_zeroed, 1)

            pool.memset(pair_ones[:, :], 0.0).then_inc(pool_step, 1)
            pool.memset(sc_mask[:, :], 1.0).then_inc(pool_step, 1)
            pool.memset(up_masks[:, :, :], 0.0).then_inc(pool_step, 1)
            pool.memset(eps_gn[:, :], RWKV_GN_EPS).then_inc(pool_step, 1)
            pool.wait_ge(pool_step, 5)
            n_step = [5]

            def pstep(ins):
                n_step[0] += 1
                ins.then_inc(pool_step, 1)
                pool.wait_ge(pool_step, n_step[0])

            def select(view, pattern, base, mult, op=ALU.is_ge):
                pstep(pool.affine_select(out=view, in_=view, compare_op=op, fill=0.0, base=base,
                                         pattern=pattern, channel_multiplier=mult))

            for hh in range(2):
                pstep(pool.memset(pair_ones[hh * HD:(hh + 1) * HD, hh * HD:(hh + 1) * HD], 1.0))
            two = "p (a t) -> p a t"
            for c0, strict_low in ((0, True), (P, False), (2 * P + HD, False)):
                v = sc_mask[:, c0:c0 + P].rearrange(two, a=2)
                if strict_low:
                    select(v, [[-HD, 2], [-1, HD]], 0, 1, ALU.is_gt)
                    select(v, [[HD, 2], [0, HD]], HD - 1, -1)
                else:
                    select(v, [[HD, 2], [1, HD]], 0, -1, ALU.is_gt)
                    select(v, [[-HD, 2], [0, HD]], 0, 1)
            for c0 in (2 * P, 3 * P + HD):
                for hh in range(2):
                    select(sc_mask[hh * HD:(hh + 1) * HD, c0:c0 + HD], [[1, HD]], 0, -1)
            for i, z in enumerate((1,) + LEVELS):
                v = up_masks[:, i, :].rearrange("p (a two z) -> p a two z", two=2, z=z)[:, :, 1, :]
                pstep(pool.memset(v, 1.0))
                select(v, [[-2 * z, P // (2 * z)], [0, z]], 0, 1)
                select(v, [[2 * z, P // (2 * z)], [0, z]], z - 1, -1)
            pstep(pool.memset(low_mask[:, :], 0.0))
            v = low_mask[:, :].rearrange("p (a two) -> p a two", two=2)[:, :, 0]
            pstep(pool.memset(v, 1.0))
            select(v, [[-2, HD]], 0, 1, ALU.is_gt)
            select(v, [[2, HD]], 1, -1)
            pool.sem_inc(masks_ready, 1)

            def low(n, s):
                pool.wait_ge(hi_done, n + 1)
                pool.tensor_tensor(w_lo[:, s, :, :], w_raw[:, s, :, :], w_hi[:, s, :, :].bitcast(F32),
                                   ALU.subtract).then_inc(lo_done, 1)

            def tails(q, e, ready):
                pool.wait_ge(ready, q + 1)
                pool.wait_ge(tail_turned, q + 1)
                pool.tensor_tensor(tail[:, e, 0:2], gate[:, e, TP:TP + 2], ones[:, 0:2], ALU.mult).then_inc(pool_step, 1)
                pool.tensor_tensor(tail[:, e, 2:2 + NS], gate[:, e, TP + 4:GW:3], ones[:, 0:NS], ALU.mult).then_inc(tail_copied, 1)

            low(0, 0)
            for p in plan:
                n0, q0 = p["blk"], p["unit"]
                last = p["last"]
                if p["kind"] == "pre" and not p["full"]:
                    for k in range(KT):
                        pool.wait_ge(uhi_done, p["split"] * KT + k + 1)
                        pool.tensor_tensor(u_lo[:, k, :], usb[:, k % 2, 0:T], u_hi[:, k, :].bitcast(F32),
                                           ALU.subtract).then_inc(u_ready, 1)
                elif p["kind"] == "sconv":
                    with pool.Fori(0, p["iters"]) as it:
                        for e in range(2):
                            for i in range(3):
                                k = 3 * e + i
                                low(n0 + 6 * it + k + 1, (k + 1) % 2)
                            tails(q0 + 2 * it + e, e, gate_ready)
                elif p["kind"] == "rproj":
                    def mix_low(o):
                        lo, hi = (u_lo, u_hi) if o % 2 == 0 else (xb_lo, xb_hi)
                        for k in range(KT):
                            pool.wait_ge(xhi_done, KT * o + k + 1)
                            pool.tensor_tensor(lo[:, k, :], xf[:, k % 2, :], hi[:, k, :].bitcast(F32),
                                               ALU.subtract).then_inc(x_ready, 1)

                    mix_low(0)
                    mix_low(1)
                    low(n0 + 1, 1)
                    mix_low(2)
                    low(n0 + 2, 0)
                    mix_low(3)
                    low(n0 + 3, 1)
                    low(n0 + 4, 0)
                    for i in range(3):
                        if i < 2:
                            mix_low(4 + i)
                        iters = KT // 2 - (i == 2)
                        nb = n0 + 4 + KT * i
                        with pool.Fori(0, iters) as it:
                            for e in range(2):
                                low(nb + 2 * it + e + 1, (e + 1) % 2)
                    low(n0 + 27, 1)
                elif p["kind"] == "gproj":
                    low(n0 + 1, 1)
                    low(n0 + 2, 0)
                    with pool.Fori(0, GT // 2 - 1) as it:
                        for e in range(2):
                            low(n0 + 3 + 2 * it + e, 1 - e)
                    low(n0 + 25, 1)
                elif p["kind"] == "gla":
                    for k in range(KT):
                        pool.wait_ge(gyhi_done, k + 1)
                        pool.tensor_tensor(u_lo[:, k, :], prod[:, k % 2, :], u_hi[:, k, :].bitcast(F32),
                                           ALU.subtract).then_inc(gy_ready, 1)
                    low(p["blk"], p["blk"] % 2)
                elif p["kind"] == "rwkv":
                    def masked(w, g, lvl):
                        if lvl:
                            pool.wait_ge(t1_mm, 10 * w + 2 * lvl + g - 1)
                        m = up_masks[:, lvl + 1, :].unsqueeze(1).to_broadcast([P, 2, P])
                        pool.tensor_tensor(ct[:, 2 * g:2 * g + 2, :], sc[:, 2 * g:2 * g + 2, P:2 * P], m,
                                           ALU.mult).then_inc(ct_ready, 1)

                    with pool.Fori(0, NCH) as c:
                        for q in range(2):
                            w = 2 * c + q
                            for lvl in range(len(LEVELS)):
                                for g in range(2):
                                    if lvl == 0:
                                        pool.wait_ge(mmt_ready, 12 * w + g + 1)
                                    masked(w, g, lvl)
                    for k in range(KT):
                        pool.wait_ge(yhi_done, k + 1)
                        pool.tensor_tensor(u_lo[:, k, :], gated_sb[:, k % 2, :], u_hi[:, k, :].bitcast(F32),
                                           ALU.subtract).then_inc(xy_ready, 1)
                    low(p["blk"], p["blk"] % 2)
                elif p["kind"] == "out":
                    with pool.Fori(0, p["iters"]) as it:
                        for e in range(2):
                            low(n0 + 2 * it + e + 1, (e + 1) % 2)
                elif p["kind"] == "up":
                    with pool.Fori(0, p["iters"]) as it:
                        for e in range(2):
                            low(n0 + 4 * it + 2 * e + 1, 1)
                            tails(q0 + 2 * it + e, e, gate_ready)
                            low(n0 + 4 * it + 2 * e + 2, 0)
                elif p["kind"] == "down":
                    iters = p["iters"] - last
                    if iters:
                        with pool.Fori(0, iters) as it:
                            for k in range(6):
                                low(n0 + 6 * it + k + 1, (k + 1) % 2)
                    if last:
                        for k in range(5):
                            low(n0 + 6 * iters + k + 1, (k + 1) % 2)

        @block.scalar
        def _(act):
            act.wait_ge(rows_loaded, 16 * NLOADS)
            act.activation(c_rows[:, :], c_rows[:, :], ACT.Silu).then_inc(c_silu, 1)
            act.wait_ge(consts_ready, 2)
            act.activation(rows[:, 0, :], ones[0:2 + NS, :], ACT.Copy).then_inc(rows_out[0], 32)
            act.activation(rows[:, 1, :], ones[0:2 + NS, :], ACT.Copy).then_inc(rows_out[1], 32)
            for k in range(KT):
                act.wait_ge(pro_turned, k + 1)
                act.activation(h[:, k, 0:TP], bank[k][:, :], ACT.Copy).then_inc(x_copied, 1)

            def high(n, s):
                act.wait_ge(w_loaded[s], 16 * half_of(n) + 16)
                act.wait_ge(block_done, n + 1)
                act.activation(w_hi[:, s, :, :], w_raw[:, s, :, :], ACT.Copy).then_inc(hi_done, 1)

            def place_state(q, e):
                act.wait_ge(st_turned, q + 3)
                act.activation(gate[:, e, TP + 2:GW].rearrange("p (b r) -> p b r", r=3)[:, :, 0:2],
                               st_ps[:, 0:2 * NS].rearrange("p (b r) -> p b r", r=2), ACT.Copy)\
                   .then_inc(st_placed, 1)

            def rows_to_dram(q, qh, e, prompt, sample):
                act.wait_ge(tail_turned, q + 3)
                act.wait_ge(rows_out[e], 32 * qh + 32)
                act.activation(rows[:, e, :], tail_ps[0:2 + NS, 0:P], ACT.Copy).then_inc(rows_copied, 1)
                act.wait_ge(rows_copied, q + 2)
                act.dma_start(prompt, rows[0:2, e, :]).then_inc(rows_out[e], 16)
                act.dma_start(sample, rows[2:2 + NS, e, :]).then_inc(rows_out[e], 16)

            act.wait_ge(x_copied, KT)
            act.sem_inc(rows_copied, 1)
            act.sem_inc(st_placed, 1)
            half_of = lambda n: 0
            high(0, 0)

            def evacuate(t_half, s, n, dst):
                act.wait_ge(block_done, n + 3)
                act.activation(dst[:, 0:HALF], tile_ps[s][0][:, 0:HALF], ACT.Copy)
                return act.activation(dst[:, HALF:T], tile_ps[s][1][:, 0:HALF], ACT.Copy)

            for p in plan:
                l, n0, q0, t0 = p["l"], p["blk"], p["unit"], p["tile"]
                last = p["last"]
                if p["kind"] == "pre":
                    i, hs = p["pre"], KT * p["post"]
                    for k in range(KT):
                        act.wait_ge(h_ready, hs + k + 1)
                        if KT * i + k >= 2:
                            act.wait_ge(sq_used, KT * i + k - 1)
                        act.activation(sq[:, k % 2, :], h[:, k, :], ACT.Square).then_inc(sq_done, 1)
                    act.wait_ge(sq_used, KT * (i + 1))
                    act.activation(std[:, 0:HALF], ss_ps[0][:, 0:HALF], ACT.Sqrt, bias=eps_col[:, 0:1], scale=1.0 / D)
                    act.activation(std[:, HALF:T], ss_ps[1][:, 0:HALF], ACT.Sqrt, bias=eps_col[:, 0:1],
                                   scale=1.0 / D).then_inc(std_done, 1)
                    for k in range(KT):
                        act.wait_ge(norm_done, KT * i + k + 1)
                        dst = usb[:, k % 2, 0:TP]
                        if p["full"]:
                            dst = rw_u[:, k, 0:TP]
                        elif KT * p["split"] + k >= 2:
                            act.wait_ge(u_ready, KT * p["split"] + k - 1)
                        act.activation(dst, normed[:, k % 2, 0:TP], ACT.Identity,
                                       bias=p["mod"][:, k, 0:1], scale=p["mod"][:, KT + k, 0:1]).then_inc(usb_done, 1)
                elif p["kind"] == "post":
                    act.wait_ge(ss_done, p["post"] + 1)
                    act.activation(std[:, 0:HALF], ss_ps[0][:, 0:HALF], ACT.Sqrt, bias=eps_col[:, 0:1], scale=1.0 / D)
                    act.activation(std[:, HALF:T], ss_ps[1][:, 0:HALF], ACT.Sqrt, bias=eps_col[:, 0:1],
                                   scale=1.0 / D).then_inc(std_done, 1)
                elif p["kind"] == "sconv":
                    j = l // 3
                    with act.Fori(0, p["iters"]) as it:
                        for e in range(2):
                            n, q, m = n0 + 6 * it + 3 * e, q0 + 2 * it + e, 2 * it + e
                            k = 3 * e
                            half_of = lambda _n, k=k: n0 // 2 + 3 * it + (k + 1) // 2
                            high(n + 1, (k + 1) % 2)
                            act.wait_ge(conv_done, q + 1)
                            act.wait_ge(tail_copied, q + 1)
                            place_state(q, e)
                            evacuate(None, k % 2, n, csb[:, e, :]).then_inc(tile_free[k % 2], 1)
                            half_of = lambda _n, k=k: n0 // 2 + 3 * it + (k + 2) // 2
                            high(n + 2, (k + 2) % 2)
                            half_of = lambda _n, k=k: n0 // 2 + 3 * it + (k + 3) // 2
                            high(n + 3, (k + 3) % 2)
                            rows_to_dram(q, q0 // 2 + it, e,
                                         O["conv_a_prompt"][j, 0, :, ds(m * P, P)],
                                         O["conv_a_sample"][j, :, 1, ds(m * P, P)])
                elif p["kind"] == "rproj":
                    act.wait_ge(urows_turned, 1)
                    act.activation(shift_rows[:, 0:512], bank[6][0:NSEQ, :], ACT.Copy)
                    act.activation(shift_rows[:, 512:D], bank[7][0:NSEQ, :], ACT.Copy).then_inc(urows_copied, 1)
                    act.wait_ge(urows_copied, 1)
                    act.dma_start(O["shift_b_prompt"][0], shift_rows[0:1, :]).then_inc(shift_out, 16)
                    act.dma_start(O["shift_b_sample"][0], shift_rows[1:NSEQ, :]).then_inc(shift_out, 16)

                    def mix_high(o):
                        hi = u_hi if o % 2 == 0 else xb_hi
                        if o == 2:
                            act.wait_ge(block_done, n0 + 1 + 2)
                        elif o == 3:
                            act.wait_ge(block_done, n0 + 2 + 2)
                        elif o >= 4:
                            act.wait_ge(block_done, n0 + 4 + KT * (o - 4) + 2)
                        for k in range(KT):
                            act.wait_ge(mixed, KT * o + k + 1)
                            act.activation(hi[:, k, :], xf[:, k % 2, :], ACT.Copy).then_inc(xhi_done, 1)

                    def lora_tile(n, s, dst, func):
                        act.wait_ge(block_done, n + 3)
                        act.activation(dst[:, 0:HALF], tile_ps[s][0][0:HD, 0:HALF], func)
                        act.activation(dst[:, HALF:T], tile_ps[s][1][0:HD, 0:HALF], func).then_inc(tile_free[s], 1)

                    half_of = lambda _n: n0 // 2
                    mix_high(0)
                    mix_high(1)
                    high(n0 + 1, 1)
                    lora_tile(n0, 0, t_lora[:, 0, :], ACT.Tanh)
                    mix_high(2)
                    half_of = lambda _n: n0 // 2 + 1
                    high(n0 + 2, 0)
                    lora_tile(n0 + 1, 1, t_lora[:, 1, :], ACT.Copy)
                    mix_high(3)
                    high(n0 + 3, 1)
                    lora_tile(n0 + 2, 0, t_g[:, 0, :], ACT.Sigmoid)
                    half_of = lambda _n: n0 // 2 + 2
                    high(n0 + 4, 0)
                    lora_tile(n0 + 3, 1, t_g[:, 1, :], ACT.Sigmoid)
                    act.wait_ge(shift_out, 32)
                    for i, dst_slab in enumerate((rw_r, rw_k, rw_v)):
                        if i < 2:
                            mix_high(4 + i)
                        else:
                            act.wait_ge(mixed, KT * 6)
                        nb = n0 + 4 + KT * i

                        def proj_tile(it, e, ahead):
                            nonlocal half_of
                            n = nb + 2 * it + e
                            if ahead:
                                half_of = lambda _n: nb // 2 + it + (e + 1) // 2
                                high(n + 1, (e + 1) % 2)
                            dst = dst_slab[:, ds(2 * it + e, 1), :].rearrange("p a t -> p (a t)")
                            evacuate(None, e, n, dst).then_inc(tile_free[e], 1)

                        with act.Fori(0, KT // 2 - (i == 2)) as it:
                            proj_tile(it, 0, True)
                            proj_tile(it, 1, True)
                        if i == 2:
                            proj_tile(KT // 2 - 1, 0, True)
                            proj_tile(KT // 2 - 1, 1, False)
                elif p["kind"] == "gproj":
                    def gate_rank(n, s):
                        act.wait_ge(block_done, n + 3)
                        act.activation(t_ga[:, s, 0:HALF], tile_ps[s][0][0:8, 0:HALF], ACT.Copy)
                        act.activation(t_ga[:, s, HALF:T], tile_ps[s][1][0:8, 0:HALF], ACT.Copy)\
                           .then_inc(tile_free[s], 1)

                    half_of = lambda _n: n0 // 2
                    high(n0 + 1, 1)
                    gate_rank(n0, 0)
                    half_of = lambda _n: n0 // 2 + 1
                    high(n0 + 2, 0)
                    gate_rank(n0 + 1, 1)

                    def in_tile(it, e, ahead):
                        nonlocal half_of
                        n = n0 + 2 + 2 * it + e
                        if ahead:
                            half_of = lambda _n: n0 // 2 + 1 + it + (e + 1) // 2
                            high(n + 1, 1 - e)
                        dst = g_in[:, ds(2 * it + e, 1), :].rearrange("p a t -> p (a t)")
                        evacuate(None, e, n, dst).then_inc(tile_free[e], 1)

                    with act.Fori(0, GT // 2 - 1) as it:
                        in_tile(it, 0, True)
                        in_tile(it, 1, True)
                    in_tile(GT // 2 - 1, 0, True)
                    in_tile(GT // 2 - 1, 1, False)
                elif p["kind"] == "gla":
                    act.wait_ge(block_done, n0 + 2)
                    for k in range(GH):
                        act.wait_ge(gz_mm, k + 1)
                        for func, dst, done in ((ACT.Identity, g_z, gz_done), (ACT.Abs, g_e, gabs_done)):
                            for half in range(2):
                                ins = act.activation(dst[:, k, half * HALF:(half + 1) * HALF],
                                                     tile_ps[k % 2][half][:, 0:HALF], func, bias=vec("gla_ba", k))
                            ins.then_inc(done, 1)
                    act.wait_ge(gabs_done, GH)
                    act.activation(g_e[:, :, :], g_e[:, :, :], ACT.Exp, scale=-1.0).then_inc(gabs_done, 1)
                    act.wait_ge(gabs_done, GH + 1)
                    act.activation(g_e[:, :, :], g_e[:, :, :], ACT.Ln, bias=1.0).then_inc(gsoft_done, 1)
                    act.wait_ge(glg_done, 1)
                    act.activation(g_dec[:, :, :], g_z[:, :, TP:T], ACT.Exp).then_inc(gdec_done, 1)
                    act.wait_ge(gG_done, 1)
                    act.activation(g_end[:, :, :], g_G[:, :, GC - 1:TP:GC], ACT.Exp).then_inc(gexp_done, 1)
                    act.activation(g_e[:, :, 0:TP], g_G[:, :, :], ACT.Exp).then_inc(gexp_done, 1)
                    act.wait_ge(gtail_ready, 1)
                    act.activation(g_z[:, :, 0:TP], g_z[:, :, 0:TP], ACT.Exp).then_inc(gexp_done, 1)
                    act.activation(g_og[:, :, :], g_og[:, :, :], ACT.Silu).then_inc(gsilu_done, 1)
                    for c in range(NGC):
                        act.wait_ge(gk_turned, c + 1)
                        act.activation(g_Kt[:, c, :, :], bank[4 + c][:, :].rearrange("p (h k) -> p h k", h=GH), ACT.Copy)\
                           .then_inc(gk_copied, 1)
                    for n in range(2 * NGC):
                        act.wait_ge(gv_turned, n + 1)
                        act.activation(g_Vt[:, n // 2, (n % 2) * 512:(n % 2 + 1) * 512], bank[4 + n % 4][:, :],
                                       ACT.Copy).then_inc(gv_copied, 1)
                    for n in range(2):
                        act.wait_ge(gvrow_turned, n + 1)
                        act.activation(g_vrow[:, n * 512:(n + 1) * 512], bank[4 + n][0:NS, :], ACT.Copy)\
                           .then_inc(gvrow_copied, 1)
                    for lvl in range(len(G_LEVELS)):
                        act.wait_ge(gdiff_ready, lvl + 1)
                        act.activation(g_z[:, :, 0:TP], g_z[:, :, 0:TP], ACT.Exp).then_inc(gexp_done, 1)
                    act.wait_ge(gs_ready, NS)
                    for half in range(2):
                        hs = slice(half * NS * GH // 2, (half + 1) * NS * GH // 2)
                        act.dma_start(O["gla_c_sample"][0].rearrange("b h k v -> k (b h) v")[:, hs, :],
                                      g_sS[:, hs, :]).then_inc(gs_out, 16)
                    act.wait_ge(gs_o_mm, 1)
                    act.activation(g_o[:, :, TP:T], bank[7][:, 0:KT * NS].rearrange("p (k s) -> p k s", k=KT), ACT.Copy)
                    for c in range(NGC):
                        for g in range(2):
                            act.wait_ge(go_mm, 2 * c + g + 1)
                            ins = act.activation(g_o[:, 4 * g:4 * g + 4, c * GC:(c + 1) * GC],
                                                 bank[g + 2 * (c % 2)][:, :].rearrange("p (k t) -> p k t", k=4), ACT.Copy)
                            ins.then_inc(go_copied, 1)
                    act.wait_ge(gS_ready, NGC * GH + 1)
                    act.dma_start(O["gla_c_prompt"][0, 0].rearrange("h k v -> k h v"), g_S[:, :, :]).then_inc(gS_out, 16)
                    act.wait_ge(go_copied, 2 * NGC)
                    for hd in range(GH):
                        for i in range(2):
                            k = 2 * hd + i
                            if k >= 2:
                                act.wait_ge(gss_mm, hd)
                            act.activation(g_sq[:, k % 2, :], g_o[:, k, :], ACT.Square).then_inc(gsq_done, 1)
                        act.wait_ge(gss_mm, hd + 1)
                        if hd:
                            act.wait_ge(gon_done, hd)
                        for half in range(2):
                            ins = act.activation(std[:, half * HALF:(half + 1) * HALF], ss_ps[half][:, 0:HALF], ACT.Sqrt,
                                                 bias=eps_col[:, 0:1], scale=1.0 / GDV)
                        ins.then_inc(gon_std, 1)
                    act.wait_ge(gS_out, 16)
                    half_of = lambda _n: n0 // 2
                    high(n0, n0 % 2)
                elif p["kind"] == "rwkv":
                    for k in range(KT):
                        for slot, done, dst, bias, sig in ((0, zw_done, rw_G, "rwkv_w0", sig_w),
                                                           (1, za_done, rw_b, "rwkv_a0", sig_a)):
                            act.wait_ge(done, k + 1)
                            for half in range(2):
                                ins = act.activation(dst[:, k, half * HALF:(half + 1) * HALF],
                                                     tile_ps[slot][half][:, 0:HALF], ACT.Sigmoid, bias=vec(bias, k))
                            ins.then_inc(sig, 1)
                    for k in range(KT):
                        if k >= 2:
                            act.wait_ge(ksum_done, k - 1)
                        act.activation(tmp8[:, k % 2, :], rw_k[:, k, :], ACT.Square, scale=vec("rwkv_k_k", k))\
                           .then_inc(ksq_done, 1)
                        if k >= 2:
                            act.wait_ge(kk_ready, k - 1)
                        act.wait_ge(ksum_done, k + 1)
                        for half in range(2):
                            ins = act.activation(tmp8[:, 2 + k % 2, half * HALF:(half + 1) * HALF],
                                                 ss_ps[half][:, 0:HALF], ACT.Sqrt)
                        ins.then_inc(knorm_done, 1)
                    act.wait_ge(prep_done, 1)
                    act.activation(decay_s[:, :, :], rw_G[:, :, TP:T], ACT.Exp).then_inc(decay_done, 1)
                    for i in range(6):
                        act.wait_ge(srow_turned, i + 1)
                        act.activation(s_rows[:, i, 0:512], bank[2 * (i % 2)][0:NS, :], ACT.Copy)
                        act.activation(s_rows[:, i, 512:D], bank[2 * (i % 2) + 1][0:NS, :], ACT.Copy)\
                           .then_inc(srow_copied, 1)
                    act.wait_ge(srow_copied, 6)
                    act.dma_start(s_state[:, :, :], A["state_wkv_b"][0].rearrange("b h v k -> (b h) v k"))\
                       .then_inc(sstate_loaded, 16)
                    for i in range(6):
                        act.dma_start(s_vec[:, i, :], s_rows[:, i, :]).then_inc(svec_loaded, 16)
                    act.wait_ge(s_y_done, 1)
                    act.dma_start(O["wkv_b_sample"][0].rearrange("b h v k -> (b h) v k"), s_state[:, :, :])\
                       .then_inc(s_state_out, 16)
                    act.dma_start(s_rows[:, 0, :], s_vec[:, 7, :]).then_inc(syrow_loaded, 16)
                    act.wait_ge(sy_turned, 1)
                    act.activation(rw_y[:, :, TP:T], bank[0][:, 0:KT * NS].rearrange("p (k s) -> p k s", k=KT),
                                   ACT.Copy).then_inc(sy_placed, 1)
                    act.wait_ge(bd_zeroed, 2)
                    act.sem_inc(y_ready, 1)
                    with act.Fori(0, NCH) as c:
                        for q in range(2):
                            w, b = 2 * c + q, bd[q]
                            act.wait_ge(st_updated, w + 1)
                            src = rw_G[:, 4 * q:4 * q + 4, ds(HD * c, HD)]
                            act.activation(b["Ep"][:, :, 1:HD + 1], src, ACT.Exp)
                            act.activation(b["Em"][:, :, :], src, ACT.Exp, scale=-1.0).then_inc(exp_done, 1)
                            for hh in range(2):
                                rs = slice(hh * HD, (hh + 1) * HD)
                                ins = act.activation(b["Vf"][rs, :, rs], rw_v[rs, 4 * q:4 * q + 4, ds(HD * c, HD)],
                                                     ACT.Copy)
                            ins.then_inc(vf_ready, 1)
                            for i in range(4):
                                act.wait_ge(tok_done, 4 * w + i + 1)
                                act.activation(tok[:, i, :], bank[4 + i][:, 0:3 * P], ACT.Copy).then_inc(tok_ready, 1)
                            act.wait_ge(rhs_mm, w + 1)
                            act.activation(rhs_sb[:, :, :], bank[4][:, :].rearrange("p (i t) -> p i t", i=4),
                                           ACT.Copy).then_inc(rhs_ready, 1)
                            for lvl in range(len(LEVELS)):
                                for g in range(2):
                                    act.wait_ge(t1_mm, 10 * w + 2 * lvl + g + 1)
                                    act.activation(t1[:, 2 * g:2 * g + 2, :],
                                                   bank[2 * g][:, 0:2 * P].rearrange("p (i t) -> p i t", i=2),
                                                   ACT.Copy).then_inc(t1_ready, 1)
                            act.wait_ge(u_mm, w + 1)
                            act.activation(uu[:, :, :], bank[5][:, :].rearrange("p (i t) -> p i t", i=4), ACT.Copy)\
                               .then_inc(uu_ready, 1)
                            act.wait_ge(y_mm, w + 1)
                            act.activation(rw_y[:, 4 * q:4 * q + 4, ds(HD * c, HD)],
                                           bank[6][:, 0:4 * HD].rearrange("p (i t) -> p i t", i=4), ACT.Copy)\
                               .then_inc(y_ready, 1)
                    act.dma_start(g2[:, :, :], A["rwkv_g2"][0].rearrange("(i r) c -> r i c", i=2)).then_inc(g2_loaded, 16)
                    act.wait_ge(wkv_turned, 1)
                    for hh in range(2):
                        rs = slice(hh * HD, (hh + 1) * HD)
                        for i in range(2):
                            ins = act.activation(wkv_out[rs, 4 * i:4 * i + 4, :],
                                                 bank[i][rs, :].rearrange("p (i t) -> p i t", i=4)[:, :, rs], ACT.Copy)
                    ins.then_inc(wkv_copied, 1)
                    act.wait_ge(wkv_copied, 1)
                    for hh in range(2):
                        rs = slice(hh * HD, (hh + 1) * HD)
                        act.dma_start(O["wkv_b_prompt"][0, 0].rearrange("(j a) v k -> a v j k", a=2)[hh],
                                      wkv_out[rs, :, :]).then_inc(wkv_out_done, 16)
                    for k in range(KT):
                        act.wait_ge(centred, k + 1)
                        if k >= 2:
                            act.wait_ge(var_mm, k - 1)
                        act.activation(gn_tmp[:, k % 2, :], rw_y[:, k, :], ACT.Square).then_inc(csq_done, 1)
                        act.wait_ge(var_mm, k + 1)
                        if k >= 2:
                            act.wait_ge(ynorm_done, k - 1)
                        for half in range(2):
                            ins = act.activation(gn_tmp[:, 2 + k % 2, half * HALF:(half + 1) * HALF],
                                                 tile_ps[1][half][:, 0:HALF], ACT.Sqrt, bias=eps_gn[:, 0:1],
                                                 scale=1.0 / HD)
                        ins.then_inc(gstd_done, 1)
                        act.wait_ge(ynorm_done, k + 1)
                        act.activation(rw_y[:, k, :], rw_y[:, k, :], ACT.Identity, bias=vec("rwkv_lnx_b", k),
                                       scale=vec("rwkv_lnx_w", k)).then_inc(yaff_done, 1)
                    act.wait_ge(wkv_out_done, 32)
                    half_of = lambda _n: n0 // 2
                    high(n0, n0 % 2)
                elif p["kind"] == "out":
                    with act.Fori(0, p["iters"]) as it:
                        for e in range(2):
                            n = n0 + 2 * it + e
                            half_of = lambda _n, e=e: n0 // 2 + it + (e + 1) // 2
                            high(n + 1, (e + 1) % 2)
                            dst = p["proj"][:, ds(2 * it + e, 1), :].rearrange("p a t -> p (a t)")
                            evacuate(None, e, n, dst).then_inc(tile_free[e], 1)
                elif p["kind"] == "up":
                    with act.Fori(0, p["iters"]) as it:
                        for e in range(2):
                            n, q, m = n0 + 4 * it + 2 * e, q0 + 2 * it + e, 2 * it + e
                            half_of = lambda _n, e=e: n0 // 2 + 2 * it + e
                            high(n + 1, 1)
                            act.wait_ge(conv_done, q + 1)
                            act.wait_ge(tail_copied, q + 1)
                            place_state(q, e)
                            act.wait_ge(block_done, n + 3)
                            act.activation(gate[:, e, 2:2 + HALF], tile_ps[0][0][:, 0:HALF], ACT.Copy)
                            act.activation(gate[:, e, 2 + HALF:2 + TP], tile_ps[0][1][:, 0:TP - HALF], ACT.Copy)
                            act.activation(gate[:, e, TP + 4:GW:3], tile_ps[0][1][:, TP - HALF:HALF], ACT.Copy)\
                               .then_inc(gate_ready, 1)
                            act.wait_ge(gate_ready, q + 1)
                            act.sem_inc(tile_free[0], 1)
                            half_of = lambda _n, e=e: n0 // 2 + 2 * it + e + 1
                            high(n + 2, 0)
                            act.wait_ge(conv_done, q + 3)
                            act.activation(conv[:, e, 0:CWD], conv[:, e, 0:CWD], ACT.Silu,
                                           bias=vec("ffn_conv_b", l * FT + m)).then_inc(silu_done, 1)
                            rows_to_dram(q, q0 // 2 + it, e,
                                         O["conv_ffn_prompt"][l, 0, :, ds(m * P, P)],
                                         O["conv_ffn_sample"][l, :, 1, ds(m * P, P)])
                elif p["kind"] == "down":
                    def down(it, final):
                        for e in range(2):
                            for i in range(3):
                                k = 3 * e + i
                                nonlocal half_of
                                half_of = lambda _n, k=k: n0 // 2 + 3 * it + (k + 1) // 2
                                if not (final and k == 5):
                                    high(n0 + 6 * it + k + 1, (k + 1) % 2)
                            dst = p["proj"][:, ds(2 * it + e, 1), :].rearrange("p a t -> p (a t)")
                            evacuate(None, e, n0 + 6 * it + 3 * e + 2, dst).then_inc(tile_free[e], 1)
                    iters = p["iters"] - last
                    if iters:
                        with act.Fori(0, iters) as it:
                            down(it, False)
                    if last:
                        down(iters, True)
            for k in range(5):
                act.wait_ge(y_turned, 2 * k + 1)
                n = P if k < 4 else NS
                act.activation(y_rows[0:n, k, 0:512], bank[(2 * k) % 8][0:n, :], ACT.Copy).then_inc(y_left, 1)
            for e in range(2):
                act.wait_ge(rows_out[e], 32 * (NUNIT // 2) + 32)

        @block.tensor
        def _(pe):
            pe.wait_ge(consts_ready, 2)
            pe.wait_ge(rows_loaded, 16 * NLOADS)
            for k in range(KT):
                for t in range(4):
                    mm = pe.transpose(bank[k][:, t * P:(t + 1) * P], x_rows[:, t, k * P:(k + 1) * P], ident[:, :])
                mm.then_inc(pro_turned, 1)
            pe.wait_ge(x_copied, 1)
            for k in range(KT):
                mm = pe.transpose(bank[0][:, k * NS:(k + 1) * NS], xs_rows[:, k * P:(k + 1) * P], ident[0:NS, 0:NS])
            mm.then_inc(pro_turned, 1)
            pe.wait_ge(x_copied, 2)
            pe.wait_ge(c_silu, 1)
            for k in range(KT):
                mm = pe.transpose(bank[1][:, k * NSEQ:(k + 1) * NSEQ], c_rows[:, k * P:(k + 1) * P],
                                  ident[0:NSEQ, 0:NSEQ])
            mm.then_inc(pro_turned, 1)
            pe.wait_ge(x_copied, 4)
            for g in range(NVG):
                rws = min(P, nrow - g * P)
                mm = pe.transpose(bank[2 + g // 4][:, (g % 4) * P:(g % 4) * P + rws], vec_rows[0:rws, g, :],
                                  ident[0:rws, 0:rws])
            mm.then_inc(pro_turned, 1)
            pe.wait_ge(x_copied, KT)
            for s in (block_done, ada_used, st_turned, tail_turned):
                pe.sem_inc(s, 2)

            def ada_tile(a, ah, s, t):
                pe.wait_ge(ada_loaded[s], 16 * ah + 16)
                for k in range(KT):
                    mm = pe.matmul(ada_ps[:, ds(t * NSEQ, NSEQ)], ada_raw[:, s, k, :], cT[:, k, :],
                                   start=(k == 0), stop=(k == KT - 1))
                mm.then_inc(ada_used, 1)

            def gemm(n, s, slot, xh, xl, k0, nk, start, stop, ready=None, width=P):
                pe.wait_ge(hi_done, n + 1)
                pe.wait_ge(lo_done, n + 3)
                for k in range(nk):
                    if ready is not None:
                        pe.wait_ge(ready[0], ready[1] + k + 1)
                    first, final = start and k == 0, stop and k == nk - 1
                    for i, (w, x) in enumerate(((w_hi, xh), (w_hi, xl), (w_lo, xh))):
                        for half in range(2):
                            mm = pe.matmul(tile_ps[slot][half][0:width, 0:HALF], w[:, s, k, 0:width],
                                           x[:, k0 + k, half * HALF:(half + 1) * HALF],
                                           start=first and i == 0, stop=final and i == 2)
                return mm.then_inc(block_done, 1)

            def turn_state(q, qh, e):
                pe.wait_ge(st_loaded[e], 16 * qh + 16)
                pe.wait_ge(st_placed, q + 1)
                pe.transpose(st_ps[:, 0:P], st_in[:, e, :], ident[:, :]).then_inc(st_turned, 1)

            def turn_tail(q, e):
                pe.wait_ge(tail_copied, q + 3)
                pe.wait_ge(rows_copied, q + 1)
                pe.transpose(tail_ps[0:2 + NS, 0:P], tail[:, e, :], ident[:, :]).then_inc(tail_turned, 1)

            pe.wait_ge(small_copied, 3)
            with pe.Fori(0, GT // 2) as it:
                for s in range(2):
                    ada_tile(2 * it + s, it, s, 2 * it + s)
            for p in plan:
                l, n0, q0, a0, t0 = p["l"], p["blk"], p["unit"], p["ada"], p["tile"]
                if p["kind"] == "pre":
                    i = p["pre"]
                    for k in range(KT):
                        pe.wait_ge(sq_done, KT * i + k + 1)
                        if k == 0 and q0:
                            pe.wait_ge(st_placed, q0 + 1)
                        for half in range(2):
                            mm = pe.matmul(ss_ps[half][:, 0:HALF], ones[:, :], sq[:, k % 2, half * HALF:(half + 1) * HALF],
                                           start=(k == 0), stop=(k == KT - 1))
                        mm.then_inc(sq_used, 1)
                elif p["kind"] == "post":
                    pe.wait_ge(sum_ready, p["post"] + 1)
                    for half in range(2):
                        mm = pe.matmul(ss_ps[half][:, 0:HALF], ones[:, :], csb[:, 0, half * HALF:(half + 1) * HALF],
                                       start=True, stop=True)
                    mm.then_inc(ss_done, 1)
                elif p["kind"] == "sconv":
                    pe.wait_ge(mod_ready, ada_group(p))
                    pe.wait_ge(std_done, p["norm"])
                    with pe.Fori(0, p["iters"]) as it:
                        for e in range(2):
                            q = q0 + 2 * it + e
                            turn_state(q, q0 // 2 + it, e)
                            for i in range(3):
                                k = 3 * e + i
                                pe.wait_ge(tile_free[k % 2], t0 // 2 + 3 * it + k // 2 + 1)
                                gemm(n0 + 6 * it + k, k % 2, k % 2, u_hi, u_lo, 0, KT, True, True,
                                     (u_ready, KT * (p["split"] - 1)) if k == 0 else None)
                                ada_tile(a0 + 6 * it + k, a0 // 2 + 3 * it + k // 2, k % 2, 6 * it + k)
                            turn_tail(q, e)
                elif p["kind"] == "rproj":
                    pe.wait_ge(mod_ready, ada_group(p))
                    pe.wait_ge(shift_loaded, 16)
                    for k in range(KT):
                        mm = pe.transpose(bank[5][:, k * NS:(k + 1) * NS], shift_in[:, k * P:(k + 1) * P],
                                          ident[0:NS, 0:NS])
                    mm.then_inc(shift_turned, 1)
                    pe.wait_ge(usb_done, KT * p["pre"])
                    pe.wait_ge(us_ready, 1)
                    for k in range(KT):
                        mm = pe.transpose(bank[6 + k // 4][0:NSEQ, (k % 4) * P:(k % 4 + 1) * P],
                                          rw_u[:, k, TP - 1:T], ident[:, :])
                    mm.then_inc(urows_turned, 1)
                    for o, (k, x) in enumerate(((0, (u_hi, u_lo)), (1, (xb_hi, xb_lo)), (2, (u_hi, u_lo)))):
                        pe.wait_ge(tile_free[k % 2], t0 // 2 + k // 2 + 1)
                        gemm(n0 + k, k % 2, k % 2, *x, 0, KT, True, True, (x_ready, KT * o), width=HD)
                    pe.wait_ge(tile_free[1], t0 // 2 + 2)
                    gemm(n0 + 3, 1, 1, u_hi, u_lo, 0, KT, True, True, width=HD)
                    pe.wait_ge(urows_copied, 1)
                    for i in range(3):
                        x = (xb_hi, xb_lo) if i % 2 == 0 else (u_hi, u_lo)
                        nb, tb, ab = n0 + 4 + KT * i, t0 + 4 + KT * i, a0 + KT * i
                        with pe.Fori(0, KT // 2) as it:
                            for e in range(2):
                                pe.wait_ge(tile_free[e], tb // 2 + it + 1)
                                gemm(nb + 2 * it + e, e, e, *x, 0, KT, True, True,
                                     (x_ready, KT * (3 + i)) if e == 0 else None)
                                ada_tile(ab + 2 * it + e, ab // 2 + it, e, KT * i + 2 * it + e)
                elif p["kind"] == "gproj":
                    pe.wait_ge(mod_ready, ada_group(p))
                    for k in range(2):
                        pe.wait_ge(tile_free[k], t0 // 2 + 1)
                        gemm(n0 + k, k, k, u_hi, u_lo, 0, KT, True, True,
                             (u_ready, KT * (p["split"] - 1)) if k == 0 else None, width=8)
                    with pe.Fori(0, GT // 2) as it:
                        for e in range(2):
                            pe.wait_ge(tile_free[e], t0 // 2 + 2 + it)
                            gemm(n0 + 2 + 2 * it + e, e, e, u_hi, u_lo, 0, KT, True, True)
                            ada_tile(a0 + 2 * it + e, a0 // 2 + it, e, 2 * it + e)
                elif p["kind"] == "gla":
                    pe.wait_ge(wa2_loaded, 16)
                    for k in range(GH):
                        if k < 2:
                            pe.wait_ge(tile_free[k], t0 // 2 + 1)
                        else:
                            pe.wait_ge(gabs_done, k - 1)
                        for half in range(2):
                            for i in range(2):
                                mm = pe.matmul(tile_ps[k % 2][half][:, 0:HALF], wa2[:, i, k * P:(k + 1) * P],
                                               t_ga[:, i, half * HALF:(half + 1) * HALF], start=(i == 0), stop=(i == 1))
                        mm.then_inc(gz_mm, 1)
                    pe.wait_ge(tile_free[0], t0 // 2 + 1)
                    pe.wait_ge(tile_free[1], t0 // 2 + 1)
                    pe.wait_ge(gkhat_ready, 1)
                    for c in range(NGC):
                        for hd in range(GH):
                            mm = pe.transpose(bank[4 + c][:, hd * P:(hd + 1) * P], g_Kl[:, hd, c * GC:(c + 1) * GC],
                                              ident[:, :])
                        mm.then_inc(gk_turned, 1)
                    for n in range(2 * NGC):
                        pe.wait_ge(*((gk_copied, n + 1) if n < 4 else (gv_copied, n - 3)))
                        for i in range(4):
                            k = 4 * (n % 2) + i
                            mm = pe.transpose(bank[4 + n % 4][:, i * P:(i + 1) * P],
                                              g_v[:, k, (n // 2) * GC:(n // 2 + 1) * GC], ident[:, :])
                        mm.then_inc(gv_turned, 1)
                    for n in range(2):
                        pe.wait_ge(gv_copied, 5 + n)
                        for i in range(4):
                            mm = pe.transpose(bank[4 + n][0:NS, i * P:(i + 1) * P], g_v[:, 4 * n + i, TP:T], ident[:, :])
                        mm.then_inc(gvrow_turned, 1)
                    pe.wait_ge(gq_ready, 1)
                    pe.wait_ge(gabs_done, GH)

                    def level(n, kx, qx):
                        if n:
                            pe.wait_ge(glevel_put, n)
                        for c in range(NGC):
                            for hd in range(GH):
                                mm = pe.matmul(bank[c][:, hd * P:(hd + 1) * P], kx[:, hd, c * GC:(c + 1) * GC],
                                               qx[:, hd, c * GC:(c + 1) * GC], start=True, stop=True)
                            if c == NGC - 1:
                                mm.then_inc(glevel_mm, 1)

                    level(0, g_k, g_q)
                    pe.wait_ge(gvrow_copied, 2)
                    pe.wait_ge(gv_copied, 2 * NGC)
                    for b in range(NS):
                        for half in range(2):
                            if b:
                                pe.wait_ge(gvb_used, b)
                            mm = pe.matmul(bank[4 + half][:, :], ident[0:NS, b:b + 1].to_broadcast([NS, P]),
                                           g_vrow[:, half * 512:(half + 1) * 512], start=True, stop=True)
                        mm.then_inc(gvb_mm, 1)
                    for b in range(NS):
                        pe.wait_ge(gs_ready, b + 1)
                        for hd in range(GH):
                            for i in range(2):
                                c0 = (2 * hd + i) * NS + b
                                mm = pe.matmul(bank[7][:, c0:c0 + 1], g_sS[:, b * GH + hd, i * P:(i + 1) * P],
                                               g_q[:, hd, TP + b:TP + b + 1], start=True, stop=True)
                    mm.then_inc(gs_o_mm, 1)
                    for lvl in range(len(G_LEVELS)):
                        pe.wait_ge(glevel_ready, lvl + 1)
                        level(lvl + 1, g_Kl, g_Ql)
                    pe.wait_ge(glevel_put, len(G_LEVELS) + 1)
                    pe.wait_ge(gq_ready, 2)
                    for c in range(NGC):
                        if c:
                            pe.wait_ge(gS_ready, GH * c + 1)
                        else:
                            pe.wait_ge(gS_ready, 1)
                        for g in range(2):
                            if c >= 2:
                                pe.wait_ge(go_copied, 2 * (c - 2) + g + 1)
                            for i in range(4):
                                hd, half = 2 * g + i // 2, i % 2
                                o = bank[g + 2 * (c % 2)][:, i * P:(i + 1) * P]
                                vs = slice(hd * GDV + half * P, hd * GDV + (half + 1) * P)
                                pe.matmul(o, g_S[:, hd, half * P:(half + 1) * P], g_e[:, hd, c * GC:(c + 1) * GC],
                                          start=True, stop=False)
                                mm = pe.matmul(o, g_Vt[:, c, vs], g_AT[:, c * GH + hd, :], start=False, stop=True)
                            mm.then_inc(go_mm, 1)
                        for g in range(2):
                            for i in range(2):
                                hd = 2 * g + i
                                mm = pe.matmul(bank[4 + g][:, i * GDV:(i + 1) * GDV], g_Kt[:, c, hd, :],
                                               g_Vt[:, c, hd * GDV:(hd + 1) * GDV], start=True, stop=True)
                        mm.then_inc(gsu_mm, 1)
                    pe.wait_ge(gS_ready, NGC * GH + 1)
                    for hd in range(GH):
                        for i in range(2):
                            k = 2 * hd + i
                            pe.wait_ge(gsq_done, k + 1)
                            if k and i == 0:
                                pe.wait_ge(gon_std, hd)
                            for half in range(2):
                                mm = pe.matmul(ss_ps[half][:, 0:HALF], ones[:, :],
                                               g_sq[:, k % 2, half * HALF:(half + 1) * HALF], start=(i == 0),
                                               stop=(i == 1))
                        mm.then_inc(gss_mm, 1)
                elif p["kind"] == "rwkv":
                    pe.wait_ge(lora_loaded, 32)
                    for k in range(KT):
                        for slot, done, sig in ((0, zw_done, sig_w), (1, za_done, sig_a)):
                            pe.wait_ge(tile_free[slot], t0 // 2 + 1)
                            if k:
                                pe.wait_ge(sig, k)
                            for half in range(2):
                                mm = pe.matmul(tile_ps[slot][half][:, 0:HALF], lora2[:, slot, k * P:(k + 1) * P],
                                               t_lora[:, slot, half * HALF:(half + 1) * HALF], start=True, stop=True)
                            mm.then_inc(done, 1)
                    for k in range(KT):
                        pe.wait_ge(ksq_done, k + 1)
                        if k:
                            pe.wait_ge(knorm_done, k)
                        for half in range(2):
                            mm = pe.matmul(ss_ps[half][:, 0:HALF], pair_ones[:, :],
                                           tmp8[:, k % 2, half * HALF:(half + 1) * HALF], start=True, stop=True)
                        mm.then_inc(ksum_done, 1)
                    pe.wait_ge(sig_a, KT)
                    pe.wait_ge(kk_ready, KT)
                    pe.wait_ge(decay_done, 1)
                    for i, src in enumerate((rw_r, rw_k, rw_v, rw_kk, rw_b, decay_s)):
                        if i >= 2:
                            pe.wait_ge(srow_copied, i - 1)
                        for k in range(KT):
                            cols = src[:, k, TP:T] if i < 5 else src[:, k, :]
                            mm = pe.transpose(bank[2 * (i % 2) + k // 4][0:NS, (k % 4) * P:(k % 4 + 1) * P], cols,
                                              ident[:, :])
                        mm.then_inc(srow_turned, 1)
                    pe.wait_ge(syrow_loaded, 16)
                    pe.wait_ge(srow_copied, 6)
                    for k in range(KT):
                        mm = pe.transpose(bank[0][:, k * NS:(k + 1) * NS], s_rows[:, 0, k * P:(k + 1) * P],
                                          ident[0:NS, 0:NS])
                    mm.then_inc(sy_turned, 1)
                    pe.wait_ge(sy_placed, 1)
                    with pe.Fori(0, NCH) as c:
                        for q in range(2):
                            w, b = 2 * c + q, bd[q]
                            pe.wait_ge(bd_ready, w + 1)
                            for i in range(4):
                                o = bank[i]
                                pe.matmul(o[:, 0:P], b["Z"][:, i, :], b["B"][:, i, :], start=True, stop=True)
                                pe.matmul(o[:, P:2 * P], b["B"][:, i, :], b["Z"][:, i, :], start=True, stop=True)
                                pe.matmul(o[:, 2 * P:2 * P + HD], b["B"][:, i, :], b["R"][:, i, :], start=True, stop=True)
                                pe.matmul(o[:, 2 * P + HD:3 * P + HD], b["K"][:, i, :], b["Z"][:, i, :], start=True,
                                          stop=True)
                                pe.matmul(o[:, 3 * P + HD:4 * P], b["K"][:, i, :], b["R"][:, i, :], start=True,
                                          stop=True).then_inc(sc_done, 1)
                            pe.wait_ge(hat_ready, w + 1)
                            pe.wait_ge(vf_ready, w + 1)
                            pe.wait_ge(y_ready, w + 1)
                            pe.wait_ge(st_updated, w + 2)
                            for i in range(4):
                                for n, nm in enumerate(("Bh", "Kh", "Vf")):
                                    mm = pe.transpose(bank[4 + i][:, n * P:(n + 1) * P], b[nm][:, i, :], ident[:, :])
                                mm.then_inc(tok_done, 1)
                            pe.wait_ge(tok_ready, 4 * w + 4)
                            for g in range(2):
                                pe.wait_ge(mmt_ready, 12 * w + g + 1)
                            for i in range(4):
                                o = bank[4][:, i * P:(i + 1) * P]
                                pe.matmul(o, b["Z"][:, i, :], rw_ST[:, 4 * q + i, :], start=True, stop=False)
                                mm = pe.matmul(o, sc[:, i, 2 * P + HD:3 * P + HD], tok[:, i, 2 * P:3 * P], start=False,
                                               stop=True)
                            mm.then_inc(rhs_mm, 1)
                            for lvl in range(len(LEVELS)):
                                for g in range(2):
                                    pe.wait_ge(ct_ready, 10 * w + 2 * lvl + g + 1)
                                    pe.wait_ge(mmt_ready, 12 * w + 2 * lvl + g + 1)
                                    for i in range(2):
                                        mm = pe.matmul(bank[2 * g][:, i * P:(i + 1) * P], ct[:, 2 * g + i, :],
                                                       mmt[:, 2 * g + i, 0:P], start=True, stop=True)
                                    mm.then_inc(t1_mm, 1)
                                for g in range(2):
                                    pe.wait_ge(t1_ready, 10 * w + 2 * lvl + g + 1)
                                    for i in range(2):
                                        z = 2 * g + i
                                        if lvl < len(LEVELS) - 1:
                                            pe.matmul(bank[2 * g + 1][:, 2 * i * P:(2 * i + 1) * P],
                                                      mmt[:, z, P:2 * P], t1[:, z, :], start=True, stop=True)
                                        mm = pe.matmul(bank[2 * g + 1][:, (2 * i + 1) * P:(2 * i + 2) * P], t1[:, z, :],
                                                       mmt[:, z, P:2 * P], start=True, stop=True)
                                    mm.then_inc(d_mm, 1)
                            pe.wait_ge(rhs_ready, w + 1)
                            for i in range(4):
                                if i % 2 == 0:
                                    pe.wait_ge(mmt_ready, 12 * w + 11 + i // 2)
                                mm = pe.matmul(bank[5][:, i * P:(i + 1) * P], mmt[:, i, P:2 * P], rhs_sb[:, i, :],
                                               start=True, stop=True)
                            mm.then_inc(u_mm, 1)
                            pe.wait_ge(uu_ready, w + 1)
                            for i in range(4):
                                o = bank[6][:, i * HD:(i + 1) * HD]
                                pe.matmul(o, rw_ST[:, 4 * q + i, :], b["R"][:, i, :], start=True, stop=False)
                                pe.matmul(o, tok[:, i, 2 * P:3 * P], sc[:, i, 3 * P + HD:4 * P], start=False, stop=False)
                                mm = pe.matmul(o, uu[:, i, :], sc[:, i, 2 * P:2 * P + HD], start=False, stop=True)
                            mm.then_inc(y_mm, 1)
                            for i in range(4):
                                o = bank[7][:, i * P:(i + 1) * P]
                                pe.matmul(o, tok[:, i, 0:P], uu[:, i, :], start=True, stop=False)
                                mm = pe.matmul(o, tok[:, i, P:2 * P], tok[:, i, 2 * P:3 * P], start=False, stop=True)
                            mm.then_inc(st_mm, 1)
                    pe.wait_ge(st_updated, 2 * NCH + 2)
                    for k in range(KT):
                        mm = pe.transpose(bank[k // 4][:, (k % 4) * P:(k % 4 + 1) * P], rw_ST[:, k, :], ident[:, :])
                    mm.then_inc(wkv_turned, 1)
                    pe.wait_ge(wkv_copied, 1)
                    pe.wait_ge(y_ready, 2 * NCH + 1)
                    pe.wait_ge(g2_loaded, 16)
                    for k in range(KT + 1):
                        if k < KT:
                            if k:
                                pe.wait_ge(centred, k)
                            for half in range(2):
                                mm = pe.matmul(tile_ps[0][half][:, 0:HALF], pair_ones[:, :],
                                               rw_y[:, k, half * HALF:(half + 1) * HALF], start=True, stop=True)
                            mm.then_inc(mean_mm, 1)
                            pe.wait_ge(csq_done, k + 1)
                            if k:
                                pe.wait_ge(gstd_done, k)
                            for half in range(2):
                                mm = pe.matmul(tile_ps[1][half][:, 0:HALF], pair_ones[:, :],
                                               gn_tmp[:, k % 2, half * HALF:(half + 1) * HALF], start=True, stop=True)
                            mm.then_inc(var_mm, 1)
                        if k < KT:
                            pe.wait_ge(rk_ready, k + 1)
                            if k:
                                pe.wait_ge(gated, k)
                            for half in range(2):
                                mm = pe.matmul(ss_ps[half][:, 0:HALF], pair_ones[:, :],
                                               rw_r[:, k, half * HALF:(half + 1) * HALF], start=True, stop=True)
                            mm.then_inc(bonus_mm, 1)
                            for half in range(2):
                                for i in range(2):
                                    mm = pe.matmul(bank[6 + half][:, 0:HALF], g2[:, i, k * P:(k + 1) * P],
                                                   t_g[:, i, half * HALF:(half + 1) * HALF], start=(i == 0),
                                                   stop=(i == 1))
                            mm.then_inc(g_mm, 1)
                elif p["kind"] == "out":
                    xh, xl, ready, r0 = p["x"]
                    with pe.Fori(0, p["iters"]) as it:
                        for e in range(2):
                            pe.wait_ge(tile_free[e], t0 // 2 + it + 1)
                            gemm(n0 + 2 * it + e, e, e, xh, xl, 0, KT, True, True, (ready, r0) if e == 0 else None)
                elif p["kind"] == "up":
                    pe.wait_ge(std_done, p["norm"])
                    with pe.Fori(0, p["iters"]) as it:
                        for e in range(2):
                            q = q0 + 2 * it + e
                            turn_state(q, q0 // 2 + it, e)
                            for part in range(2):
                                pe.wait_ge(tile_free[part], t0 // 2 + 2 * it + e + 1)
                                gemm(n0 + 4 * it + 2 * e + part, part, part, u_hi, u_lo, 0, KT, True, True,
                                     (u_ready, KT * (p["split"] - 1)) if e == part == 0 else None)
                            turn_tail(q, e)
                elif p["kind"] == "down":
                    if l + 1 < depth:
                        pe.wait_ge(mod_ready, ada_group(p))
                    with pe.Fori(0, p["iters"]) as it:
                        for e in range(2):
                            pe.wait_ge(tile_free[e], t0 // 2 + it + 1)
                            for i, (k0, nk) in enumerate(DOWN_K):
                                k = 3 * e + i
                                gemm(n0 + 6 * it + k, k % 2, e, hid_hi, hid_lo, k0, nk, i == 0, i == 2,
                                     (hid_ready, p["unit"] - FT + k0) if e == 0 else None)
                                if l + 1 < depth:
                                    ada_tile(a0 + 6 * it + k, a0 // 2 + 3 * it + k // 2, k % 2, 6 * it + k)
            pe.wait_ge(h_ready, KT * (2 * depth + 1))
            for t in range(5):
                n = P if t < 4 else NS
                for g in range(2):
                    b = bank[(2 * t + g) % 8]
                    if t == 4:
                        pe.wait_ge((y_left, y_right)[g], 1)
                    for k in range(4):
                        mm = pe.transpose(b[0:n, k * P:(k + 1) * P], h[:, 4 * g + k, t * P:t * P + n], ident[:, :])
                    mm.then_inc(y_turned, 1)

        @block.vector
        def _(dve):
            step = [0]
            base = [0]

            def link(ins):
                step[0] += 1
                ins.then_inc(dve_step, 1)
                dve.wait_ge(dve_step, base[0] + step[0])

            def loop_steps(per, it):
                base[0] = base[0] + step[0] + per * it
                step[0] = 0

            def after_loop(b, s, per, iters):
                base[0], step[0] = b + s + per * iters, 0

            dve.memset(gate[:, :, :], 0.0).then_inc(conv_done, 2)
            dve.wait_ge(pro_turned, KT + 1)
            dve.tensor_copy(h[:, :, TP:T], bank[0][:, 0:KT * NS].rearrange("p (k s) -> p k s", k=KT))\
               .then_inc(small_copied, 1)
            dve.wait_ge(pro_turned, KT + 2)
            dve.tensor_copy(cT[:, :, :], bank[1][:, 0:KT * NSEQ].rearrange("p (k s) -> p k s", k=KT))\
               .then_inc(small_copied, 1)
            dve.wait_ge(pro_turned, KT + 3)
            dve.tensor_copy(vecs[:, 0:512], bank[2][:, :])
            link(dve.tensor_copy(vecs[:, 512:nrow], bank[3][:, 0:nrow - 512]))
            for s in (small_copied, tile_free[0], tile_free[1]):
                dve.sem_inc(s, 1)
            dve.wait_ge(x_copied, KT)
            for k in range(KT):
                dve.sem_inc(h_ready, 1)

            def modulation(l, half, mod):
                g = 2 * l + half
                dve.wait_ge(ada_used, GT * (g + 1) + 2)
                if True:
                    bias = vecs[:, col["ada_b"] + l * MODT + half * GT:col["ada_b"] + l * MODT + (half + 1) * GT]
                    dst = mod[:, :, :]
                    link(dve.tensor_tensor(dst, ada_ps[:, 0:GT * NSEQ].rearrange("p (t s) -> p t s", s=NSEQ),
                                           bias.unsqueeze(2).to_broadcast([P, GT, NSEQ]), ALU.add))
                    link(dve.tensor_scalar(mod[:, KT:2 * KT, :], mod[:, KT:2 * KT, :], 1.0, None, ALU.add))
                    for i in range(2):
                        c0 = col["norm_g"] + (l * 4 + 2 * half + i) * KT
                        gain = vecs[:, c0:c0 + KT].unsqueeze(2).to_broadcast([P, KT, NSEQ])
                        part = mod[:, (i + 1) * KT:(i + 2) * KT, :]
                        ins = dve.tensor_tensor(part, part, gain, ALU.mult)
                        if i == 1:
                            ins.then_inc(mod_ready, 1)
                        else:
                            link(ins)
                dve.wait_ge(mod_ready, g + 1)

            modulation(0, 0, mod_m)

            def conv3(q, e, name, row0, m, ft):
                w = [vec(name, row0 + j * ft + m) for j in range(3)]
                link(dve.tensor_scalar(conv[:, e, 0:CWD], gate[:, e, 0:CWD], w[0], None, ALU.mult))
                link(dve.scalar_tensor_tensor(conv[:, e, 0:CWD], gate[:, e, 1:1 + CWD], w[1], conv[:, e, 0:CWD],
                                              ALU.mult, ALU.add))
                dve.scalar_tensor_tensor(conv[:, e, 0:CWD], gate[:, e, 2:2 + CWD], w[2], conv[:, e, 0:CWD],
                                         ALU.mult, ALU.add).then_inc(conv_done, 1)
                dve.wait_ge(conv_done, q + 3)

            def times_tile(e, slot, t_after):
                dve.tensor_tensor(prod[:, e, 0:HALF], conv[:, e, 0:HALF], tile_ps[slot][0][:, 0:HALF], ALU.mult)
                dve.tensor_tensor(prod[:, e, HALF:TP], conv[:, e, HALF:TP], tile_ps[slot][1][:, 0:TP - HALF], ALU.mult)
                dve.tensor_tensor(prod[:, e, TP:T], conv[:, e, TP + 2:CWD:3], tile_ps[slot][1][:, TP - HALF:HALF],
                                  ALU.mult).then_inc(tile_free[slot], 1)
                dve.wait_ge(tile_free[slot], t_after)

            def split_hidden(e, m):
                hi = hid_hi[:, ds(m, 1), :].rearrange("p a t -> p (a t)")
                lo = hid_lo[:, ds(m, 1), :].rearrange("p a t -> p (a t)")
                link(dve.tensor_copy(hi, prod[:, e, :]))
                dve.tensor_tensor(lo, prod[:, e, :], hi.bitcast(F32), ALU.subtract).then_inc(hid_ready, 1)

            for p in plan:
                l, n0, q0, a0, t0 = p["l"], p["blk"], p["unit"], p["ada"], p["tile"]
                if p["kind"] == "pre":
                    i, mod = p["pre"], p["mod"]
                    dve.wait_ge(std_done, p["norm"] + 1)
                    link(dve.reciprocal(rstd[:, :], std[:, :]))
                    rs = rstd[:, TP:T].unsqueeze(1).to_broadcast([P, KT, NS])
                    link(dve.tensor_tensor(s8[:, 0], h[:, :, TP:T], rs, ALU.mult))
                    link(dve.tensor_tensor(s8[:, 0], s8[:, 0], mod[:, KT:2 * KT, 1:NSEQ], ALU.mult))
                    link(dve.tensor_tensor(s8[:, 0], s8[:, 0], mod[:, 0:KT, 1:NSEQ], ALU.add))
                    if i:
                        dve.wait_ge(block_done, n0 + 2)
                    if p["full"]:
                        dve.tensor_copy(rw_u[:, :, TP:T], s8[:, 0]).then_inc(us_ready, 1)
                        for k in range(KT):
                            if KT * i + k >= 2:
                                dve.wait_ge(usb_done, KT * i + k - 1)
                            dve.tensor_tensor(normed[:, k % 2, 0:TP], h[:, k, 0:TP], rstd[:, 0:TP], ALU.mult)\
                               .then_inc(norm_done, 1)
                        continue
                    for k in range(KT + 1):
                        if k < KT:
                            if KT * i + k >= 2:
                                dve.wait_ge(usb_done, KT * i + k - 1)
                            dve.tensor_tensor(normed[:, k % 2, 0:TP], h[:, k, 0:TP], rstd[:, 0:TP], ALU.mult)\
                               .then_inc(norm_done, 1)
                        if k:
                            dve.wait_ge(usb_done, KT * i + k)
                            link(dve.tensor_copy(usb[:, (k - 1) % 2, TP:T], s8[:, 0, k - 1, :]))
                            dve.tensor_copy(u_hi[:, k - 1, :], usb[:, (k - 1) % 2, 0:T]).then_inc(uhi_done, 1)
                elif p["kind"] == "post":
                    mod, proj_x = p["mod"], p["proj"]
                    dve.wait_ge(std_done, p["norm"] + 1)
                    link(dve.reciprocal(rstd[:, :], std[:, :]))
                    rs = rstd[:, TP:T].unsqueeze(1).to_broadcast([P, KT, NS])
                    link(dve.tensor_tensor(s8[:, 0], proj_x[:, :, TP:T], rs, ALU.mult))
                    link(dve.tensor_tensor(s8[:, 0], s8[:, 0], mod[:, 2 * KT:3 * KT, 1:NSEQ], ALU.mult))
                    link(dve.tensor_tensor(h[:, :, TP:T], h[:, :, TP:T], s8[:, 0], ALU.add))
                    for k in range(KT):
                        link(dve.tensor_tensor(proj_x[:, k, 0:TP], proj_x[:, k, 0:TP], rstd[:, 0:TP], ALU.mult))
                        dve.scalar_tensor_tensor(h[:, k, 0:TP], proj_x[:, k, 0:TP], mod[:, 2 * KT + k, 0:1],
                                                 h[:, k, 0:TP], ALU.mult, ALU.add).then_inc(h_ready, 1)
                elif p["kind"] == "sconv":
                    j = l // 3
                    b, s, PER = base[0], step[0], 2 * 3
                    with dve.Fori(0, p["iters"]) as it:
                        loop_steps(PER, it)
                        for e in range(2):
                            q, m, n, k = q0 + 2 * it + e, 2 * it + e, n0 + 6 * it + 3 * e, 3 * e
                            dve.wait_ge(tile_free[k % 2], t0 // 2 + 3 * it + k // 2 + 2)
                            dve.wait_ge(block_done, n + 4)
                            sl = (k + 1) % 2
                            dve.tensor_tensor(gate[:, e, 2:2 + HALF], csb[:, e, 0:HALF], tile_ps[sl][0][:, 0:HALF],
                                              ALU.mult)
                            dve.tensor_tensor(gate[:, e, 2 + HALF:2 + TP], csb[:, e, HALF:TP],
                                              tile_ps[sl][1][:, 0:TP - HALF], ALU.mult)
                            dve.tensor_tensor(gate[:, e, TP + 4:GW:3], csb[:, e, TP:T],
                                              tile_ps[sl][1][:, TP - HALF:HALF], ALU.mult).then_inc(gate_ready, 1)
                            dve.wait_ge(gate_ready, q + 1)
                            dve.sem_inc(tile_free[sl], 1)
                            conv3(q, e, "sconv_conv_w", j * 3 * KT, m, KT)
                            dve.wait_ge(block_done, n + 5)
                            times_tile(e, k % 2, t0 // 2 + 3 * it + (k + 2) // 2 + 2)
                            split_hidden(e, m)
                        assert step[0] == PER
                    after_loop(b, s, PER, p["iters"])
                    modulation(l, 1, mod_f)
                elif p["kind"] == "rproj":
                    dve.wait_ge(shift_turned, 1)
                    link(dve.tensor_copy(prev_s[:, :, :], bank[5][:, 0:KT * NS].rearrange("p (k s) -> p k s", k=KT)))
                    dve.wait_ge(usb_done, KT * p["pre"])
                    dve.tensor_scalar(rw_d[:, :, 0:1], rw_u[:, :, 0:1], -1.0, None, ALU.mult)
                    for k in range(KT):
                        dve.tensor_tensor(rw_d[:, k, 1:TP], rw_u[:, k, 0:TP - 1], rw_u[:, k, 1:TP], ALU.subtract)
                    link(dve.tensor_tensor(rw_d[:, :, TP:T], prev_s[:, :, :], rw_u[:, :, TP:T], ALU.subtract))
                    for o, i in enumerate((1, 4, 5, 0, 2, 3)):
                        for k in range(KT):
                            if KT * o + k >= 2:
                                dve.wait_ge(x_ready, KT * o + k - 1)
                            dve.scalar_tensor_tensor(xf[:, k % 2, :], rw_d[:, k, :], vec("rwkv_mu", i * KT + k),
                                                     rw_u[:, k, :], ALU.mult, ALU.add).then_inc(mixed, 1)
                    modulation(l, 1, mod_f)
                elif p["kind"] == "gproj":
                    modulation(l, 1, mod_f)
                elif p["kind"] == "gla":
                    dve.wait_ge(gz_done, GH)
                    link(dve.tensor_scalar(g_z[:, :, :], g_z[:, :, :], 0.0, None, ALU.min))
                    dve.wait_ge(gsoft_done, 1)
                    zf, ef = (x[:, :, :].rearrange("p h t -> p (h t)") for x in (g_z, g_e))
                    link(dve.scalar_tensor_tensor(zf, ef, -1.0, zf, ALU.mult, ALU.add))
                    dve.tensor_scalar(g_z[:, :, :], g_z[:, :, :], 1.0 / 16.0, None, ALU.mult).then_inc(glg_done, 1)
                    dve.wait_ge(glg_done, 1)
                    dve.tensor_scalar(g_q, g_q, float(P) ** -0.5, None, ALU.mult).then_inc(gq_ready, 1)
                    link(dve.memset(g_Ql[:, 0, :], 1.0))
                    link(dve.memset(g_Ql[:, 0, 0:TP:GC], 0.0))
                    for hd in range(GH):
                        ins = dve.tensor_tensor_scan(g_G[:, hd, :], g_Ql[:, 0, :], g_z[:, hd, 0:TP], 0.0, ALU.mult,
                                                     ALU.add)
                    ins.then_inc(gG_done, 1)
                    dve.wait_ge(gG_done, 1)
                    dve.wait_ge(gdec_done, 1)
                    chunks = "p h (c t) -> p (h c) t"
                    Gc = g_G[:, :, :].rearrange(chunks, t=GC)
                    zc = g_z[:, :, 0:TP]
                    for hd in range(GH):
                        Gh = g_G[:, hd, :].rearrange("p (c t) -> p c t", t=GC)
                        ins = dve.tensor_tensor(g_z[:, hd, 0:TP].rearrange("p (c t) -> p c t", t=GC),
                                                Gh[:, :, GC - 1:GC].to_broadcast([P, NGC, GC]), Gh, ALU.subtract)
                    ins.then_inc(gtail_ready, 1)
                    dve.wait_ge(gexp_done, 2)
                    dve.wait_ge(gq_ready, 1)
                    dve.tensor_tensor(g_e[:, :, 0:TP], g_q[:, :, 0:TP], g_e[:, :, 0:TP], ALU.mult).then_inc(gq_ready, 1)
                    dve.wait_ge(gexp_done, 3)
                    dve.tensor_tensor(g_Kl[:, :, :], g_k[:, :, 0:TP], g_z[:, :, 0:TP], ALU.mult).then_inc(gkhat_ready, 1)
                    link(dve.memset(g_Ql[:, :, :], 0.0))
                    link(dve.memset(g_AT[:, :, :], 0.0))
                    link(dve.memset(g_S[:, :, :], 0.0))
                    dve.sem_inc(gS_ready, 1)
                    dve.wait_ge(gk_turned, NGC)

                    def put(n, mask):
                        dve.wait_ge(glevel_mm, n + 1)
                        for c in range(NGC):
                            if mask is None:
                                ins = dve.tensor_copy(
                                    g_AT[0:64, c * GH:(c + 1) * GH, 64:P],
                                    bank[c][0:64, :].rearrange("p (h t) -> p h t", h=GH)[:, :, 64:P])
                            else:
                                ins = dve.copy_predicated(
                                    g_AT[:, c * GH:(c + 1) * GH, :],
                                    mask.unsqueeze(1).to_broadcast([P, GH, P]).bitcast(mybir.dt.uint32),
                                    bank[c][:, :].rearrange("p (h t) -> p h t", h=GH))
                        ins.then_inc(glevel_put, 1)
                        dve.wait_ge(glevel_put, n + 1)

                    def sample(b):
                        dve.wait_ge(gvb_mm, b + 1)
                        for hd in range(GH):
                            x = b * GH + hd
                            ins = dve.tensor_scalar(g_sS[:, x, :], g_sS[:, x, :], g_dec[:, hd, b:b + 1], None, ALU.mult)
                        link(ins)
                        for hd in range(GH):
                            x = b * GH + hd
                            vb = bank[4 + hd // 2][:, (hd % 2) * GDV:(hd % 2 + 1) * GDV]
                            ins = dve.scalar_tensor_tensor(g_sS[:, x, :], vb, g_k[:, hd, TP + b:TP + b + 1],
                                                           g_sS[:, x, :], ALU.mult, ALU.add)
                        ins.then_inc(gs_ready, 1)
                        dve.wait_ge(gs_ready, b + 1)
                        dve.sem_inc(gvb_used, 1)

                    put(0, ident[:, :])
                    dve.wait_ge(gS_loaded, 32)
                    for b in range(NS):
                        sample(b)
                    for lvl, z in enumerate(G_LEVELS):
                        if lvl:
                            dve.wait_ge(glevel_ready, lvl)
                        for hd in range(GH):
                            Gb = g_G[:, hd, :].rearrange("p (b t) -> p b t", t=2 * z)
                            eb = g_z[:, hd, 0:TP].rearrange("p (b t) -> p b t", t=2 * z)
                            ref = Gb[:, :, z - 1:z].to_broadcast([P, TP // (2 * z), z])
                            dve.tensor_tensor(eb[:, :, z:2 * z], Gb[:, :, z:2 * z], ref, ALU.subtract)
                            ins = dve.tensor_tensor(eb[:, :, 0:z], ref, Gb[:, :, 0:z], ALU.subtract)
                        ins.then_inc(gdiff_ready, 1)
                        dve.wait_ge(gexp_done, 4 + lvl)
                        if lvl:
                            dve.wait_ge(glevel_mm, lvl + 1)
                        for hd in range(GH):
                            bl = lambda x: x.rearrange("p (b t) -> p b t", t=2 * z)
                            dve.tensor_tensor(bl(g_Ql[:, hd, :])[:, :, z:2 * z], bl(g_q[:, hd, 0:TP])[:, :, z:2 * z],
                                              bl(g_z[:, hd, 0:TP])[:, :, z:2 * z], ALU.mult)
                            ins = dve.tensor_tensor(bl(g_Kl[:, hd, :])[:, :, 0:z], bl(g_k[:, hd, 0:TP])[:, :, 0:z],
                                                    bl(g_z[:, hd, 0:TP])[:, :, 0:z], ALU.mult)
                        ins.then_inc(glevel_ready, 1)
                        put(lvl + 1, None if z == 64 else up_masks[:, z.bit_length() - 1, :])
                    dve.wait_ge(gexp_done, 1)
                    for c in range(NGC):
                        dve.wait_ge(gsu_mm, c + 1)
                        dve.wait_ge(gS_ready, GH * c + 1)
                        for hd in range(GH):
                            dve.scalar_tensor_tensor(
                                g_S[:, hd, :], g_S[:, hd, :], g_end[:, hd, c:c + 1],
                                bank[4 + hd // 2][:, (hd % 2) * GDV:(hd % 2 + 1) * GDV], ALU.mult, ALU.add)\
                               .then_inc(gS_ready, 1)
                    dve.wait_ge(gsilu_done, 1)
                    for hd in range(GH):
                        dve.wait_ge(gon_std, hd + 1)
                        dve.reciprocal(rstd[:, :], std[:, :]).then_inc(gon_done, 1)
                        dve.wait_ge(gon_done, hd + 1)
                        for i in range(2):
                            k = 2 * hd + i
                            link(dve.tensor_tensor(g_o[:, k, :], g_o[:, k, :], rstd[:, :], ALU.mult))
                            if k >= 2:
                                dve.wait_ge(gy_ready, k - 1)
                            link(dve.scalar_tensor_tensor(prod[:, k % 2, :], g_o[:, k, :], vec("gla_onorm_g", i),
                                                          g_og[:, k, :], ALU.mult, ALU.mult))
                            dve.tensor_copy(u_hi[:, k, :], prod[:, k % 2, :]).then_inc(gyhi_done, 1)
                    dve.wait_ge(gyhi_done, KT)
                    dve.wait_ge(gss_mm, GH)
                    link(dve.memset(gate[:, :, 0:2], 0.0))
                elif p["kind"] == "rwkv":
                    link(dve.tensor_scalar(one_less_ka[:, :], vecs[:, col["rwkv_k_a"]:col["rwkv_k_a"] + KT], -1.0, 1.0,
                                           ALU.mult, ALU.add))
                    link(dve.memset(tmp8[:, 5, 0:TP], 1.0))
                    link(dve.memset(tmp8[:, 5, 0:TP:HD], 0.0))
                    for k in range(KT):
                        dve.wait_ge(sig_w, k + 1)
                        link(dve.tensor_scalar(rw_G[:, k, :], rw_G[:, k, :], DECAY, None, ALU.mult))
                        link(dve.tensor_tensor_scan(tmp8[:, 6 + k % 2, 0:TP], tmp8[:, 5, 0:TP], rw_G[:, k, 0:TP], 0.0,
                                                    ALU.mult, ALU.add))
                        link(dve.tensor_copy(rw_G[:, k, 0:TP], tmp8[:, 6 + k % 2, 0:TP]))
                    dve.sem_inc(prep_done, 1)
                    for k in range(KT):
                        dve.wait_ge(sig_a, KT)
                        dve.wait_ge(knorm_done, k + 1)
                        nr = tmp8[:, 2 + k % 2, :]
                        link(dve.tensor_scalar(nr, nr, 1e-12, None, ALU.max))
                        link(dve.reciprocal(nr, nr))
                        link(dve.scalar_tensor_tensor(rw_kk[:, k, :], rw_k[:, k, :], vec("rwkv_k_k", k), nr, ALU.mult,
                                                      ALU.mult))
                        link(dve.tensor_scalar(tmp8[:, 4, :], rw_b[:, k, :], vec("rwkv_k_a", k), one_less_ka[:, k:k + 1],
                                               ALU.mult, ALU.add))
                        link(dve.tensor_tensor(rw_k[:, k, :], rw_k[:, k, :], tmp8[:, 4, :], ALU.mult))
                        dve.scalar_tensor_tensor(rw_b[:, k, :], rw_kk[:, k, :], -1.0, rw_b[:, k, :], ALU.mult,
                                                 ALU.mult).then_inc(kk_ready, 1)
                    dve.wait_ge(kk_ready, KT)
                    dve.wait_ge(svec_loaded, 96)
                    dve.wait_ge(sstate_loaded, 16)
                    rows_of = lambda i: s_vec[:, i, :].unsqueeze(1).to_broadcast([P, HD, HD])
                    cols_of = lambda i: s_vec[:, i, :].unsqueeze(2).to_broadcast([P, HD, HD])
                    S, W = s_state[:, :, :], s_tmp[:, :, :]
                    link(dve.tensor_tensor(W, S, rows_of(3), ALU.mult))
                    link(dve.tensor_reduce(s_vec[:, 6, :], W, AX.X, ALU.add))
                    link(dve.tensor_tensor(S, S, rows_of(5), ALU.mult))
                    link(dve.tensor_tensor(W, cols_of(6), rows_of(4), ALU.mult))
                    link(dve.tensor_tensor(S, S, W, ALU.add))
                    link(dve.tensor_tensor(W, cols_of(2), rows_of(1), ALU.mult))
                    link(dve.tensor_tensor(S, S, W, ALU.add))
                    link(dve.tensor_tensor(W, S, rows_of(0), ALU.mult))
                    dve.tensor_reduce(s_vec[:, 7, :], W, AX.X, ALU.add).then_inc(s_y_done, 1)
                    dve.wait_ge(s_state_out, 16)
                    dve.wait_ge(s_y_done, 1)
                    for q in range(2):
                        for nm in ("Z", "B", "K", "Bh", "Kh", "Vf"):
                            ins = dve.memset(bd[q][nm][:, :, :], 0.0)
                        ins.then_inc(bd_zeroed, 1)
                        link(dve.memset(bd[q]["Ep"][:, :, 0:1], 1.0))
                    dve.wait_ge(bd_zeroed, 2)
                    dve.wait_ge(sy_turned, 1)
                    link(dve.memset(rw_ST[:, :, :], 0.0))
                    dve.sem_inc(st_updated, 2)
                    dve.wait_ge(masks_ready, 1)
                    b0, s0, PER = base[0], step[0], 2 * 4
                    with dve.Fori(0, NCH) as c:
                        loop_steps(PER, c)
                        for q in range(2):
                            w, b, qs = 2 * c + q, bd[q], slice(4 * q, 4 * q + 4)
                            now = ds(HD * c, HD)
                            dve.wait_ge(exp_done, w + 1)
                            Ep, Em = b["Ep"], b["Em"]
                            dve.tensor_tensor(b["R"][:, :, :], rw_r[:, qs, now], Ep[:, :, 1:HD + 1], ALU.mult)
                            for hh in range(2):
                                rs = slice(hh * HD, (hh + 1) * HD)
                                dve.tensor_tensor(b["Z"][rs, :, rs], rw_kk[rs, qs, now], Ep[rs, :, 0:HD], ALU.mult)
                                dve.tensor_tensor(b["K"][rs, :, rs], rw_k[rs, qs, now], Em[rs, :, :], ALU.mult)
                                ins = dve.tensor_tensor(b["B"][rs, :, rs], rw_b[rs, qs, now], Em[rs, :, :], ALU.mult)
                            ins.then_inc(bd_ready, 1)
                            dve.wait_ge(bd_ready, w + 1)
                            dve.wait_ge(st_updated, w + 1)
                            end = Ep[:, :, HD:HD + 1].to_broadcast([P, 4, P])
                            dve.tensor_tensor(b["Bh"][:, :, :], b["B"][:, :, :], end, ALU.mult)
                            dve.tensor_tensor(b["Kh"][:, :, :], b["K"][:, :, :], end, ALU.mult).then_inc(hat_ready, 1)
                            for g in range(2):
                                for i in (2 * g, 2 * g + 1):
                                    dve.wait_ge(sc_done, 4 * w + i + 1)
                                    ins = dve.tensor_tensor(sc[:, i, :], bank[i][:, :], sc_mask[:, :], ALU.mult)
                                link(ins)
                                gs = slice(2 * g, 2 * g + 2)
                                lm = low_mask[:, :].unsqueeze(1).to_broadcast([P, 2, P])
                                um = up_masks[:, 0, :].unsqueeze(1).to_broadcast([P, 2, P])
                                dve.tensor_tensor(mmt[:, gs, 0:P], sc[:, gs, 0:P], lm, ALU.mult)
                                link(dve.tensor_tensor(mmt[:, gs, P:2 * P], sc[:, gs, P:2 * P], um, ALU.mult))
                                idb = ident[:, :].unsqueeze(1).to_broadcast([P, 4, P])
                                mv = mmt[:, gs, :].rearrange("p i (two t) -> p (i two) t", two=2)
                                dve.tensor_tensor(mv, mv, idb, ALU.add).then_inc(mmt_ready, 1)
                            for lvl in range(len(LEVELS)):
                                for g in range(2):
                                    gs = slice(2 * g, 2 * g + 2)
                                    dve.wait_ge(d_mm, 10 * w + 2 * lvl + g + 1)
                                    dve.wait_ge(mmt_ready, 12 * w + 2 * lvl + g + 1)
                                    dv = bank[2 * g + 1][:, :].rearrange("p (i t) -> p i t", i=2)
                                    lo = 0 if lvl < len(LEVELS) - 1 else P
                                    dve.tensor_tensor(mmt[:, gs, lo:2 * P], mmt[:, gs, lo:2 * P], dv[:, :, lo:2 * P],
                                                      ALU.add).then_inc(mmt_ready, 1)
                            dve.wait_ge(st_mm, w + 1)
                            for i in range(4):
                                ins = dve.scalar_tensor_tensor(rw_ST[:, 4 * q + i, :], rw_ST[:, 4 * q + i, :],
                                                               Ep[:, i, HD:HD + 1], bank[7][:, i * P:(i + 1) * P],
                                                               ALU.mult, ALU.add)
                            ins.then_inc(st_updated, 1)
                        assert step[0] == PER, step[0]
                    after_loop(b0, s0, PER, NCH)
                    for k in range(KT + 1):
                        if k < KT:
                            dve.wait_ge(mean_mm, k + 1)
                            for half in range(2):
                                hs = slice(half * HALF, (half + 1) * HALF)
                                ins = dve.scalar_tensor_tensor(rw_y[:, k, hs], tile_ps[0][half][:, 0:HALF], -1.0 / HD,
                                                               rw_y[:, k, hs], ALU.mult, ALU.add)
                            ins.then_inc(centred, 1)
                            dve.scalar_tensor_tensor(rw_r[:, k, :], rw_r[:, k, :], vec("rwkv_r_k", k), rw_k[:, k, :],
                                                     ALU.mult, ALU.mult).then_inc(rk_ready, 1)
                        if k:
                            j = k - 1
                            dve.wait_ge(bonus_mm, j + 1)
                            for half in range(2):
                                hs = slice(half * HALF, (half + 1) * HALF)
                                ins = dve.tensor_tensor(rw_v[:, j, hs], rw_v[:, j, hs], ss_ps[half][:, 0:HALF], ALU.mult)
                            link(ins)
                            dve.wait_ge(gstd_done, j + 1)
                            nr = gn_tmp[:, 2 + j % 2, :]
                            link(dve.reciprocal(nr, nr))
                            dve.tensor_tensor(rw_y[:, j, :], rw_y[:, j, :], nr, ALU.mult).then_inc(ynorm_done, 1)
                            dve.wait_ge(yaff_done, j + 1)
                            link(dve.tensor_tensor(rw_y[:, j, :], rw_y[:, j, :], rw_v[:, j, :], ALU.add))
                            dve.wait_ge(g_mm, j + 1)
                            if j >= 2:
                                dve.wait_ge(xy_ready, j - 1)
                            for half in range(2):
                                hs = slice(half * HALF, (half + 1) * HALF)
                                ins = dve.tensor_tensor(gated_sb[:, j % 2, hs], rw_y[:, j, hs],
                                                        bank[6 + half][:, 0:HALF], ALU.mult)
                            ins.then_inc(gated, 1)
                            dve.wait_ge(gated, j + 1)
                            dve.tensor_copy(u_hi[:, j, :], gated_sb[:, j % 2, :]).then_inc(yhi_done, 1)
                    link(dve.memset(gate[:, :, 0:2], 0.0))
                elif p["kind"] == "up":
                    b, s, PER = base[0], step[0], 2 * 3
                    with dve.Fori(0, p["iters"]) as it:
                        loop_steps(PER, it)
                        for e in range(2):
                            q, m, n = q0 + 2 * it + e, 2 * it + e, n0 + 4 * it + 2 * e
                            dve.wait_ge(gate_ready, q + 1)
                            conv3(q, e, "ffn_conv_w", l * 3 * FT, m, FT)
                            dve.wait_ge(block_done, n + 4)
                            dve.wait_ge(silu_done, p["up_unit"] + m + 1)
                            times_tile(e, 1, t0 // 2 + 2 * it + e + 2)
                            split_hidden(e, m)
                        assert step[0] == PER
                    after_loop(b, s, PER, p["iters"])
                elif p["kind"] in ("out", "down"):
                    per = 1 if p["kind"] == "out" else 3
                    b, s, PER = base[0], step[0], 2
                    link(dve.memset(csb[:, 0, :], 0.0))
                    b, s = base[0], step[0]
                    with dve.Fori(0, p["iters"]) as it:
                        loop_steps(4, it)
                        for e in range(2):
                            dve.wait_ge(tile_free[e], t0 // 2 + it + 2)
                            o = p["proj"][:, ds(2 * it + e, 1), :].rearrange("p a t -> p (a t)")
                            link(dve.tensor_tensor(csb[:, 1, :], o, o, ALU.mult))
                            link(dve.tensor_tensor(csb[:, 0, :], csb[:, 0, :], csb[:, 1, :], ALU.add))
                    after_loop(b, s, 4, p["iters"])
                    dve.sem_inc(sum_ready, 1)
                    if p["kind"] == "down" and l + 1 < depth:
                        modulation(l + 1, 0, mod_m)
            for k in range(5):
                dve.wait_ge(y_turned, 2 * k + 2)
                n = P if k < 4 else NS
                dve.tensor_copy(y_rows[0:n, k, 512:1024], bank[(2 * k + 1) % 8][0:n, :]).then_inc(y_right, 1)


_INS = ['x_prompt', 'x_sample', 'state_conv_a', 'state_shift_b', 'state_wkv_b', 'state_gla_c', 'state_conv_ffn',
        'c_prompt', 'c_sample', 'ada_w', 'ada_b', 'norm_g', 'sconv_w_in', 'sconv_conv_w', 'sconv_w_out',
        'rwkv_mu', 'rwkv_w_rkv', 'rwkv_w0', 'rwkv_w1', 'rwkv_w2', 'rwkv_a0', 'rwkv_a1', 'rwkv_a2', 'rwkv_g1',
        'rwkv_g2', 'rwkv_k_k', 'rwkv_k_a', 'rwkv_r_k', 'rwkv_lnx_w', 'rwkv_lnx_b', 'rwkv_w_o',
        'gla_w_in', 'gla_wa1', 'gla_wa2', 'gla_ba', 'gla_onorm_g', 'gla_w_o',
        'ffn_w_up', 'ffn_conv_w', 'ffn_conv_b', 'ffn_w_down']
_OUTS = [('y_prompt', (1, 512, 1024)), ('y_sample', (8, 1, 1024)),
         ('conv_a_prompt', (2, 1, 2, 1024)), ('conv_a_sample', (2, 8, 2, 1024)),
         ('shift_b_prompt', (1, 1, 1024)), ('shift_b_sample', (1, 8, 1024)),
         ('wkv_b_prompt', (1, 1, 16, 64, 64)), ('wkv_b_sample', (1, 8, 16, 64, 64)),
         ('gla_c_prompt', (1, 1, 4, 128, 256)), ('gla_c_sample', (1, 8, 4, 128, 256)),
         ('conv_ffn_prompt', (4, 1, 2, 2816)), ('conv_ffn_sample', (4, 8, 2, 2816))]


def kernel(**inputs):
    import numpy as _np
    import concourse.bacc as _bacc
    from concourse.bass_utils import run_bass_kernel_spmd as _run

    nc = _bacc.Bacc("TRN2", target_bir_lowering=False, num_devices=1)
    arrays, ins, outs = {}, {}, {}
    for name in _INS:
        a = _np.ascontiguousarray(inputs[name])
        arrays[f"in_{name}_dram"] = a
        ins[name] = nc.dram_tensor(f"in_{name}_dram", a.shape, F32, kind="ExternalInput").ap()
    for name, shape in _OUTS:
        outs[name] = nc.dram_tensor(f"out_{name}_dram", shape, F32, kind="ExternalOutput").ap()
    trunk_kernel(nc, ins, outs, 4)
    r = _run(nc, [arrays], core_ids=[0])
    return tuple(r.results[0][f"out_{name}_dram"] for name, _ in _OUTS)
```

```python
import math
from contextlib import ExitStack

import concourse.bass as bass
from concourse import mybir

F32 = mybir.dt.float32
F32R = mybir.dt.float32r
ALU = mybir.AluOpType
ACT = mybir.ActivationFunctionType
AX = mybir.AxisListType

P = 128
D = 1024
TP = 512
NS = 8
T = TP + NS
HALF = T // 2
KT = D // P
DFF = 2816
FT = DFF // P
NSEQ = 1 + NS
MODT = 6 * KT
GT = 3 * KT
GW = 2 + TP + 3 * NS
CWD = GW - 2
EPS = 1e-6
HD = 64
NCH = TP // HD
RWKV_GN_EPS = 64e-5
DECAY = -math.exp(-0.5)
LEVELS = (2, 4, 8, 16, 32)
GH = 4
GDV = 256
GC = P
NGC = TP // GC
G_LEVELS = (64, 32, 16, 8, 4, 2, 1)
SCW = 512
POOL_TILES = (1, 2, 4, 5, 7)
PRO_T = 4
DOWN_K = ((0, 8), (8, 7), (15, 7))


def ds(i, n):
    return bass.ds(i, n)


def trunk_kernel(nc, A, O, depth):
    ctx = ExitStack()
    with ctx:
        cursor = [(nc.sbuf_base + 63) // 64 * 64]

        def at(name, shape, dt, offset):
            return nc.alloc_sbuf_tensor_at(name, shape, dt, offset=offset)

        def sb(name, shape, dt=F32):
            n = 4
            for s in shape[1:]:
                n *= s
            off = cursor[0]
            cursor[0] = (off + n + 31) // 32 * 32
            return at(name, shape, dt, off)

        h = sb("h", [P, KT, T])
        u_off = cursor[0]
        u_hi = sb("u_hi", [P, KT, T], F32R)
        u_lo = sb("u_lo", [P, KT, T], F32R)
        proj = at("proj", [P, KT, T], F32, u_off)
        big_off = cursor[0]
        hid_hi = sb("hid_hi", [P, FT, T], F32R)
        hid_lo = sb("hid_lo", [P, FT, T], F32R)
        w_raw_at = cursor[0]
        w_raw = sb("w_raw", [P, 2, KT, P])
        w_hi_at = cursor[0]
        w_hi = sb("w_hi", [P, 2, KT, P], F32R)
        w_lo = sb("w_lo", [P, 2, KT, P], F32R)
        ada_raw = sb("ada_raw", [P, 2, KT, P])
        vecs = sb("vecs", [P, 7 * P])
        mod_m = sb("mod_m", [P, GT, NSEQ])
        mod_f = sb("mod_f", [P, GT, NSEQ])
        cT = sb("cT", [P, KT, NSEQ])
        ident = sb("ident", [P, P])
        ones = sb("ones", [P, P])
        eps_col = sb("eps_col", [P, 1])
        std_at = cursor[0]
        std = sb("std", [P, T])
        rstd = sb("rstd", [P, T])
        gate_at = cursor[0]
        gate = sb("gate", [P, 2, GW])
        conv = sb("conv", [P, 2, GW])
        csb = sb("csb", [P, 2, T])
        prod = sb("prod", [P, 2, T])
        st_in = sb("st_in", [P, 2, P])
        tail = sb("tail", [P, 2, 2 + NS])
        rows = sb("rows", [2 + NS, 2, P])
        s8 = sb("s8", [P, 2, KT, NS])
        pair_ones = sb("pair_ones", [P, P])
        sc_mask = sb("sc_mask", [P, SCW])
        low_mask = sb("low_mask", [P, P])
        up_masks = sb("up_masks", [P, 1 + len(LEVELS), P])
        eps_gn = sb("eps_gn", [P, 1])
        warm = sb("warm", [P, 1])
        prev_s = sb("prev_s", [P, KT, NS])
        one_less_ka = sb("one_less_ka", [P, KT])
        decay_s = sb("decay_s", [P, KT, NS])
        end_decay = sb("end_decay", [P, 2, 4])
        assert cursor[0] <= nc.sbuf_usable_end, cursor[0]
        slab_bytes = KT * T * 4

        def slab(name, i, dt=F32):
            return at(name, [P, KT, T], dt, big_off + i * slab_bytes)

        xb_hi, xb_lo = slab("xb_hi", 0, F32R), slab("xb_lo", 1, F32R)
        rw_G, rw_kk, rw_b = slab("rw_G", 0), slab("rw_kk", 1), slab("rw_b", 2)
        rw_u, rw_r, rw_k = slab("rw_u", 2), slab("rw_r", 3), slab("rw_k", 4)
        rw_y, proj_b = rw_kk, rw_G
        gate_off = gate_at
        rw_v = at("rw_v", [P, KT, T], F32, gate_off)
        rw_d = at("rw_d", [P, KT, T], F32, gate_off)
        half_off = big_off + 5 * slab_bytes
        t_lora = at("t_lora", [HD, 2, T], F32, half_off)
        rw_ST = at("rw_ST", [P, KT, P], F32, half_off)
        t_g = at("t_g", [HD, 2, T], F32, half_off + 2 * T * 4)
        xf = at("xf", [P, 2, T], F32, std_at)
        xf2 = at("xf2", [P, 2, T], F32, big_off + 4 * slab_bytes)

        def mix_tile(m):
            return xf[:, m % 2, :] if m >= 5 * KT or m % 4 < 2 else xf2[:, m % 2, :]

        lora2 = at("lora2", [HD, 2, D], F32, u_off + slab_bytes)
        gn_tmp = slab("gn_tmp", 0)
        gated_sb = at("gated_sb", [P, 2, T], F32, big_off + 4 * T * 4)
        g2 = at("g2", [HD, 2, D], F32, big_off + 2 * slab_bytes)
        tmp8 = at("tmp8", [P, KT, T], F32, u_off)
        s_state = at("s_state", [P, HD, HD], F32, u_off)
        s_tmp = at("s_tmp", [P, HD, HD], F32, u_off + slab_bytes)
        SAMPLE_ROWS = ((0, rw_r), (2, rw_v), (5, decay_s), (3, rw_kk), (4, rw_b), (1, rw_k))
        s_rows = at("s_rows", [NS, 6, D], F32, w_hi_at)
        s_vec = at("s_vec", [P, 8, HD], F32, std_at)
        bd = []
        for q in range(2):
            o = u_off + q * slab_bytes
            names = ("Z", "B", "K", "Bh", "Kh", "Vf")
            d = {nm: at(f"bd_{nm}{q}", [P, 4, P], F32, o + i * 2048) for i, nm in enumerate(names)}
            d["R"] = at(f"bd_R{q}", [P, 4, HD], F32, o + 6 * 2048)
            d["Em"] = at(f"bd_Em{q}", [P, 4, HD], F32, o + 6 * 2048 + 1024)
            d["Ep"] = at(f"bd_Ep{q}", [P, 4, HD + 1], F32, o + 6 * 2048 + 2048)
            bd.append(d)
        sc = [at("sc0", [P, 4, SCW], F32, w_hi_at), at("sc1", [P, 4, SCW], F32, w_raw_at)]
        mmt = at("mmt", [P, 4, 2 * P], F32, w_hi_at + 8192)
        ct = at("ct", [P, 4, P], F32, w_hi_at + 8192 + 4096)
        t1 = at("t1", [P, 4, P], F32, w_hi_at + 8192 + 6144)
        tok = at("tok", [P, 4, 3 * P], F32, w_hi_at + 16384)
        rhs_sb = at("rhs_sb", [P, 4, P], F32, w_hi_at + 16384 + 6144)
        uu = at("uu", [P, 4, P], F32, std_at)
        wkv_out = at("wkv_out", [P, KT, HD], F32, w_hi_at)
        g_in = at("g_in", [P, 3 * KT, T], F32, big_off)
        g_q, g_k, g_v, g_og = (g_in[:, 0:GH, :], g_in[:, GH:2 * GH, :], g_in[:, KT:2 * KT, :],
                               g_in[:, 2 * KT:3 * KT, :])
        g_o = at("g_o", [P, KT, T], F32, big_off + slab_bytes)
        g_z2 = at("g_z2", [P, GH, T], F32, big_off + slab_bytes)
        g_sS = at("g_sS", [P, NS * GH, GDV], F32, big_off + 3 * slab_bytes)
        g_Kt = at("g_Kt", [P, NGC, GH, P], F32, half_off)
        g_AT = at("g_AT", [P, GH * NGC, P], F32, u_off)
        g_Vt = at("g_Vt", [P, NGC, D], F32, u_off + 8192)
        g_G = at("g_G", [P, GH, TP], F32, u_off + 8192 + 16384)
        g_Ql = at("g_Ql", [P, GH, TP], F32, gate_off)
        g_Kl = at("g_Kl", [P, GH, TP], F32, gate_off + 8192)
        g_z = at("g_z", [P, GH, T], F32, w_hi_at)
        g_e = at("g_e", [P, GH, T], F32, w_hi_at + GH * T * 4)
        g_S = at("g_S", [P, GH, GDV], F32, w_hi_at + 2 * GH * T * 4)
        g_end = at("g_end", [P, GH, NGC], F32, w_hi_at + 2 * GH * T * 4 + 4096)
        g_dec = at("g_dec", [P, GH, NS], F32, w_hi_at + 2 * GH * T * 4 + 4096 + 64)
        t_ga = at("t_ga", [8, 2, T], F32, half_off)
        wa2 = at("wa2", [8, 2, GH * P], F32, half_off + 2 * T * 4)
        g_sq = at("g_sq", [P, 2, T], F32, gate_off)
        g_vrow = at("g_vrow", [NS, D], F32, std_at)
        shift_rows = at("shift_rows", [NSEQ, D], F32, big_off + 3 * slab_bytes)
        shift_in = at("shift_in", [NS, D], F32, big_off + 3 * slab_bytes + 4096)
        normed = prod
        usb = conv
        sq = csb
        vec_rows = at("vec_rows", [P, 7, P], F32, big_off)
        x_rows = at("x_rows", [P, 4, D], F32, big_off + 4096)
        xs_rows = at("xs_rows", [NS, D], F32, big_off + 4096 + 16384)
        c_rows = at("c_rows", [NSEQ, D], F32, big_off + 8192 + 16384)
        mod_rows = at("mod_rows", [NSEQ, 2, PRO_T * P], F32, big_off + 28672)
        ada_pro = [at(f"ada_pro{i}", [P, KT, PRO_T * P], F32,
                      (big_off + 32768 + i * 16384) if i < 3 else u_off + (i - 3) * 16384) for i in range(5)]
        y_rows = at("y_rows", [P, 5, D], F32, big_off)

        bank = [ctx.enter_context(nc.psum_tensor(f"bank{i}", [P, 512], F32)) for i in range(8)]
        tile_ps = [(bank[0], bank[1]), (bank[2], bank[3])]
        ss_ps = (bank[4], bank[5])
        st_ps, ada_ps, tail_ps = bank[4], bank[6], bank[7]

        def sem(name):
            return ctx.enter_context(nc.semaphore(name))

        consts_ready = sem("consts_ready")
        rows_loaded = sem("rows_loaded")
        c_silu = sem("c_silu")
        pro_turned = sem("pro_turned")
        x_copied = sem("x_copied")
        small_copied = sem("small_copied")
        w_loaded = [sem(f"w_loaded{i}") for i in range(2)]
        hi_done = sem("hi_done")
        lo_done = sem("lo_done")
        block_done = sem("block_done")
        tile_free = [sem(f"tile_free{i}") for i in range(2)]
        ada_loaded = [sem(f"ada_loaded{i}") for i in range(2)]
        pro_mod_mm, pro_mod_copied = sem("pro_mod_mm"), sem("pro_mod_copied")
        ada_pro_loaded = [sem(f"ada_pro_loaded{i}") for i in range(GT // PRO_T)]
        ada_used = sem("ada_used")
        mod_ready = sem("mod_ready")
        st_loaded = [sem(f"st_loaded{i}") for i in range(2)]
        st_turned = sem("st_turned")
        st_zeroed = sem("st_zeroed")
        st_placed = sem("st_placed")
        gate_ready = sem("gate_ready")
        conv_done = sem("conv_done")
        silu_done = sem("silu_done")
        hid_ready = sem("hid_ready")
        tail_copied = sem("tail_copied")
        tail_turned = sem("tail_turned")
        rows_copied = sem("rows_copied")
        rows_out = [sem(f"rows_out{i}") for i in range(2)]
        sq_done = sem("sq_done")
        sq_used = sem("sq_used")
        ss_done = sem("ss_done")
        std_done = sem("std_done")
        norm_done = sem("norm_done")
        rstd_ready, tile_scaled = sem("rstd_ready"), sem("tile_scaled")
        usb_done = sem("usb_done")
        uhi_done = sem("uhi_done")
        u_ready = sem("u_ready")
        h_ready = sem("h_ready")
        sum_ready = sem("sum_ready")
        y_turned = sem("y_turned")
        y_left = sem("y_left")
        y_right = sem("y_right")
        outs_done = sem("outs_done")
        dve_step = sem("dve_step")
        pool_step = sem("pool_step")
        masks_ready = sem("masks_ready")
        wa2_loaded, gz_mm, gz_done, ggate_done = sem("wa2_loaded"), sem("gz_mm"), sem("gz_done"), sem("ggate_done")
        gS_loaded, gargs_ready, gexp_done, gq_ready = (sem("gS_loaded"), sem("gargs_ready"), sem("gexp_done"),
                                                       sem("gq_ready"))
        gkhat_ready, g_turned, g_copied = sem("gkhat_ready"), sem("g_turned"), sem("g_copied")
        g_pool_done, gs_decayed = sem("g_pool_done"), sem("gs_decayed")
        glevel_ready, glevel_mm, glevel_put = sem("glevel_ready"), sem("glevel_mm"), sem("glevel_put")
        gvb_mm, gvb_used, gs_ready, gs_o_mm, gs_out = (sem("gvb_mm"), sem("gvb_used"), sem("gs_ready"),
                                                       sem("gs_o_mm"), sem("gs_out"))
        G_ABS, G_SOFT, G_DEC = GH, GH + 2, GH + 3
        G_GATED = len(G_LEVELS)
        G_LOG, G_SUM, G_TAIL = 1, 2, 3
        G_K, G_V, G_VROW = NGC, 3 * NGC, 3 * NGC + 2
        go_mm, go_copied, gsu_mm, gS_ready, gS_out, gsilu_done = (
            sem("go_mm"), sem("go_copied"), sem("gsu_mm"), sem("gS_ready"), sem("gS_out"), sem("gsilu_done"))
        gsq_done, gss_mm, gon_std, gon_done, gyhi_done, gy_ready = (
            sem("gsq_done"), sem("gss_mm"), sem("gon_std"), sem("gon_done"), sem("gyhi_done"), sem("gy_ready"))
        shift_loaded, shift_turned = sem("shift_loaded"), sem("shift_turned")
        us_ready = sem("us_ready")
        urows_copied, shift_out = sem("urows_copied"), sem("shift_out")
        mixed, xhi_done = sem("mixed"), sem("xhi_done")
        x_ready = [sem(f"x_ready{i}") for i in range(2)]
        lora_loaded, zw_done, za_done = sem("lora_loaded"), sem("zw_done"), sem("za_done")
        sig_w, sig_a = sem("sig_w"), sem("sig_a")
        ksq_done, ksum_done, knorm_done, kk_ready = (sem("ksq_done"), sem("ksum_done"), sem("knorm_done"),
                                                     sem("kk_ready"))
        prep_done, keys_ready = sem("prep_done"), sem("keys_ready")
        decay_done, srow_turned, srow_copied = sem("decay_done"), sem("srow_turned"), sem("srow_copied")
        svec_loaded, sstate_loaded, s_y_done = sem("svec_loaded"), sem("sstate_loaded"), sem("s_y_done")
        s_state_out, syrow_loaded = sem("s_state_out"), sem("syrow_loaded")
        bd_zeroed, scores_masked = sem("bd_zeroed"), sem("scores_masked")
        exp_done, bd_ready, hat_ready, vf_ready = sem("exp_done"), sem("bd_ready"), sem("hat_ready"), sem("vf_ready")
        sc_done, tok_done, tok_ready = sem("sc_done"), sem("tok_done"), sem("tok_ready")
        ct_ready, t1_mm, t1_ready, d_mm, mmt_ready = (sem("ct_ready"), sem("t1_mm"), sem("t1_ready"), sem("d_mm"),
                                                      sem("mmt_ready"))
        rhs_mm, rhs_ready, u_mm, uu_ready = sem("rhs_mm"), sem("rhs_ready"), sem("u_mm"), sem("uu_ready")
        y_mm, y_ready, st_mm, st_updated = sem("y_mm"), sem("y_ready"), sem("st_mm"), sem("st_updated")
        wkv_copied, wkv_out_done = sem("wkv_copied"), sem("wkv_out_done")
        g2_loaded, mean_mm, centred, csq_done, var_mm, gstd_done, ynorm_done, yaff_done = (
            sem("g2_loaded"), sem("mean_mm"), sem("centred"), sem("csq_done"), sem("var_mm"), sem("gstd_done"),
            sem("ynorm_done"), sem("yaff_done"))
        rk_ready, bonus_mm, g_mm, gated, yhi_done, xy_ready = (sem("rk_ready"), sem("bonus_mm"), sem("g_mm"),
                                                               sem("gated"), sem("yhi_done"), sem("xy_ready"))

        col = {}
        pieces = []
        nrow = 0
        for name, ap in (
            ("norm_g", A["norm_g"].rearrange("l s (t p) -> (l s t) p", p=P)),
            ("ada_b", A["ada_b"].rearrange("l (t p) -> (l t) p", p=P)),
            ("ffn_conv_w", A["ffn_conv_w"].rearrange("l j (t p) -> (l j t) p", p=P)),
            ("ffn_conv_b", A["ffn_conv_b"].rearrange("l (t p) -> (l t) p", p=P)),
            ("sconv_conv_w", A["sconv_conv_w"].rearrange("l j (t p) -> (l j t) p", p=P)),
            ("rwkv_mu", A["rwkv_mu"].rearrange("l i (t p) -> (l i t) p", p=P)),
            ("rwkv_w0", A["rwkv_w0"].rearrange("l (t p) -> (l t) p", p=P)),
            ("rwkv_a0", A["rwkv_a0"].rearrange("l (t p) -> (l t) p", p=P)),
            ("rwkv_k_k", A["rwkv_k_k"].rearrange("l (t p) -> (l t) p", p=P)),
            ("rwkv_k_a", A["rwkv_k_a"].rearrange("l (t p) -> (l t) p", p=P)),
            ("rwkv_r_k", A["rwkv_r_k"].rearrange("l (t a) n -> (l t) (a n)", a=2)),
            ("rwkv_lnx_w", A["rwkv_lnx_w"].rearrange("l (t p) -> (l t) p", p=P)),
            ("rwkv_lnx_b", A["rwkv_lnx_b"].rearrange("l (t p) -> (l t) p", p=P)),
            ("gla_ba", A["gla_ba"].rearrange("l (t p) -> (l t) p", p=P)),
            ("gla_onorm_g", A["gla_onorm_g"].rearrange("l (t p) -> (l t) p", p=P)),
        ):
            col[name] = nrow
            done, n = 0, ap.shape[0]
            while done < n:
                k = min(n - done, P - nrow % P)
                pieces.append((nrow // P, nrow % P, k, ap[done:done + k, :]))
                done += k
                nrow += k
        NVG = (nrow + P - 1) // P
        NLOADS = len(pieces) + 4 + 1 + 2

        def vec(name, i):
            c = col[name] + i
            return vecs[:, ds(c, 1)]

        plan = []
        count = dict(blk=0, tile=0, unit=0, ada=GT, norm=0, split=0)

        def phase(kind, layer, iters, blk, tile, unit, ada, **more):
            plan.append(dict(kind=kind, l=layer, iters=iters, **{k: v for k, v in count.items()}, **more))
            count["blk"] += iters * blk
            count["tile"] += iters * tile
            count["unit"] += iters * unit
            count["ada"] += iters * ada

        def norm(kind, layer, **more):
            phase(kind, layer, 0, 0, 0, 0, 0, **more)
            count["norm"] += 1

        post = 0
        pre = 0
        for l in range(depth):
            mixer = l % 3
            norm("pre", l, mod=mod_m, group=2 * l, pre=pre, post=post, full=mixer == 1)
            count["split"] += mixer != 1
            pre += 1
            if mixer == 0:
                phase("sconv", l, KT // 2, 6, 6, 2, 6, pre=pre)
            elif mixer == 1:
                phase("rproj", l, 1, 28, 28, 0, GT, pre=pre)
                phase("rwkv", l, 0, 0, 0, 0, 0)
            else:
                phase("gproj", l, 1, 26, 26, 0, GT, pre=pre)
                phase("gla", l, 0, 0, 0, 0, 0)
            hid_x = mixer == 0
            phase("out", l, KT // 2, 2, 2, 0, 0, pre=pre,
                  x=(hid_hi, hid_lo, hid_ready, count["unit"] - KT) if hid_x else (u_hi, u_lo, (xy_ready, gy_ready)[mixer - 1], 0),
                  proj=proj if hid_x else proj_b)
            norm("post", l, mod=mod_m, sub=1, post=post, proj=proj if hid_x else proj_b)
            post += 1
            norm("pre", l, mod=mod_f, group=2 * l + 1, pre=pre, post=post, full=False)
            count["split"] += 1
            pre += 1
            phase("up", l, FT // 2, 4, 4, 2, 0, pre=pre, up_unit=l * FT)
            phase("down", l, KT // 2, 6, 2, 0, 6 if l + 1 < depth else 0, proj=proj)
            norm("post", l, mod=mod_f, sub=3, post=post, proj=proj)
            post += 1
        NBLK, NUNIT = count["blk"], count["unit"]
        for p in plan:
            p["last"] = p["kind"] == "down" and p["l"] == depth - 1

        def ada_group(p):
            return p["ada"] // GT

        block = ctx.enter_context(nc.Block())

        @block.sync
        def _(sp):
            for g, r, k, ap in pieces:
                sp.dma_start(vec_rows[r:r + k, g, :], ap).then_inc(rows_loaded, 16)
            sp.dma_start(c_rows[0:1, :], A["c_prompt"]).then_inc(rows_loaded, 16)
            sp.dma_start(c_rows[1:NSEQ, :], A["c_sample"]).then_inc(rows_loaded, 16)
            for t in range(4):
                sp.dma_start(x_rows[:, t, :], A["x_prompt"][0, t * P:(t + 1) * P, :]).then_inc(rows_loaded, 16)
            sp.dma_start(xs_rows[:, :], A["x_sample"].rearrange("b o d -> (b o) d")).then_inc(rows_loaded, 16)

            def load_block(n, s, src):
                sp.wait_ge(lo_done, n + 1)
                nk = src.shape[1]
                m = src.shape[2]
                sp.dma_start(w_raw[:, s, 0:nk, 0:m], src).then_inc(w_loaded[s], 16)

            def load_ada(a, s, l, t):
                sp.wait_ge(ada_used, a + 1)
                src = A["ada_w"][l].rearrange("(k p) c -> p k c", p=P)[:, :, ds(t * P, P)]
                sp.dma_start(ada_raw[:, s, :, :], src).then_inc(ada_loaded[s], 16)

            def load_state(q, src):
                sp.wait_ge(st_turned, q + 1)
                sp.dma_start(st_in[0:2 * NS, q_par, :], src).then_inc(st_loaded[q_par], 16)

            w = A["ada_w"][0].rearrange("(k p) c -> p k c", p=P)
            for i in range(GT // PRO_T):
                if i == len(ada_pro):
                    sp.wait_ge(pro_mod_mm, 1)
                sp.dma_start(ada_pro[i % len(ada_pro)][:, :, :], w[:, :, i * PRO_T * P:(i + 1) * PRO_T * P])\
                  .then_inc(ada_pro_loaded[i], 16)
            sp.wait_ge(st_zeroed, 1)
            for p in plan:
                l, n0, q0, a0 = p["l"], p["blk"], p["unit"], p["ada"]
                j = l // 3
                if p["kind"] == "sconv":
                    w = A["sconv_w_in"][j].rearrange("(k p) c -> p k c", p=P)
                    st = A["state_conv_a"][j].rearrange("b r c -> (b r) c")
                    with sp.Fori(0, p["iters"]) as it:
                        for e in range(2):
                            m = 2 * it + e
                            q_par = e
                            load_state(q0 + m, st[:, ds(m * P, P)])
                            for i, part in enumerate((1, 2, 0)):
                                k = 3 * e + i
                                load_block(n0 + 6 * it + k, k % 2, w[:, :, ds((part * KT + m) * P, P)])
                                load_ada(a0 + 6 * it + k, k % 2, l, GT + 6 * it + k)
                elif p["kind"] == "rproj":
                    for k, src in enumerate((A["rwkv_w1"][j], A["rwkv_a1"][j], A["rwkv_g1"][j][:, 0:HD],
                                             A["rwkv_g1"][j][:, HD:2 * HD])):
                        if k == 2:
                            sp.wait_ge(block_done, n0 + 2)
                            sp.dma_start(shift_in[:, :], A["state_shift_b"][j]).then_inc(shift_loaded, 16)
                        load_block(n0 + k, k % 2, src.rearrange("(k p) c -> p k c", p=P))
                    for i in range(3):
                        w = A["rwkv_w_rkv"][j, i].rearrange("(k p) c -> p k c", p=P)
                        with sp.Fori(0, KT // 2) as it:
                            for e in range(2):
                                load_block(n0 + 4 + KT * i + 2 * it + e, e, w[:, :, ds((2 * it + e) * P, P)])
                                load_ada(a0 + KT * i + 2 * it + e, e, l, GT + KT * i + 2 * it + e)
                    sp.wait_ge(block_done, n0 + 28 + 2)
                    sp.dma_start(lora2[:, 0, :], A["rwkv_w2"][j]).then_inc(lora_loaded, 16)
                    sp.dma_start(lora2[:, 1, :], A["rwkv_a2"][j]).then_inc(lora_loaded, 16)
                elif p["kind"] == "gproj":
                    for k in range(2):
                        load_block(n0 + k, k % 2, A["gla_wa1"][0][:, 8 * k:8 * k + 8].rearrange("(k p) c -> p k c", p=P))
                    w = A["gla_w_in"][0].rearrange("(k p) c -> p k c", p=P)
                    with sp.Fori(0, GT // 2) as it:
                        for e in range(2):
                            load_block(n0 + 2 + 2 * it + e, e, w[:, :, ds((2 * it + e) * P, P)])
                            load_ada(a0 + 2 * it + e, e, l, GT + 2 * it + e)
                    sp.dma_start(wa2[:, :, :], A["gla_wa2"][0].rearrange("(i r) c -> r i c", i=2)).then_inc(wa2_loaded, 16)
                    st = A["state_gla_c"][0].rearrange("b h k v -> k (b h) v")
                    for half in range(2):
                        hs = slice(half * NS * GH // 2, (half + 1) * NS * GH // 2)
                        sp.dma_start(g_sS[:, hs, :], st[:, hs, :]).then_inc(gS_loaded, 16)
                elif p["kind"] == "out":
                    if l % 3 == 1:
                        sp.wait_ge(srow_turned, 8)
                    w = {0: A["sconv_w_out"][j], 1: A["rwkv_w_o"][j % 1], 2: A["gla_w_o"][j % 1]}[l % 3]
                    w = w.rearrange("(k p) c -> p k c", p=P)
                    with sp.Fori(0, p["iters"]) as it:
                        for e in range(2):
                            load_block(n0 + 2 * it + e, e, w[:, :, ds((2 * it + e) * P, P)])
                elif p["kind"] == "up":
                    w = A["ffn_w_up"][l].rearrange("(k p) c -> p k c", p=P)
                    st = A["state_conv_ffn"][l].rearrange("b r c -> (b r) c")
                    with sp.Fori(0, p["iters"]) as it:
                        for e in range(2):
                            m = 2 * it + e
                            q_par = e
                            load_state(q0 + m, st[:, ds(m * P, P)])
                            for part in range(2):
                                load_block(n0 + 4 * it + 2 * e + part, part, w[:, :, ds((part * FT + m) * P, P)])
                elif p["kind"] == "down":
                    w = A["ffn_w_down"][l].rearrange("(k p) c -> p k c", p=P)
                    with sp.Fori(0, p["iters"]) as it:
                        for e in range(2):
                            for i, (k0, nk) in enumerate(DOWN_K):
                                k = 3 * e + i
                                load_block(n0 + 6 * it + k, k % 2, w[:, k0:k0 + nk, ds((2 * it + e) * P, P)])
                                if l + 1 < depth:
                                    load_ada(a0 + 6 * it + k, k % 2, l + 1, 6 * it + k)
            for l in range(depth):
                sp.dma_start(O["conv_ffn_sample"][l, :, 0, :], A["state_conv_ffn"][l, :, 1, :]).then_inc(outs_done, 16)
            n_copies = depth
            if depth > 2:
                sp.wait_ge(gs_out, 32)
                sp.wait_ge(gS_out, 16)
            if depth > 1:
                sp.wait_ge(s_state_out, 16)
                sp.wait_ge(shift_out, 32)
                sp.wait_ge(wkv_out_done, 32)
            for j in range((depth + 2) // 3):
                sp.dma_start(O["conv_a_sample"][j, :, 0, :], A["state_conv_a"][j, :, 1, :]).then_inc(outs_done, 16)
                n_copies += 1
            sp.wait_ge(y_left, 5)
            sp.wait_ge(y_right, 5)
            for t in range(4):
                sp.dma_start(O["y_prompt"][0, t * P:(t + 1) * P, :], y_rows[:, t, :]).then_inc(outs_done, 16)
            sp.dma_start(O["y_sample"].rearrange("b o d -> (b o) d"), y_rows[0:NS, 4, :]).then_inc(outs_done, 16)
            sp.wait_ge(outs_done, 16 * (n_copies + 5))

        @block.gpsimd
        def _(pool):
            pool.memset(w_raw[:, :, :, :], 0.0).then_inc(lo_done, 2)
            pool.memset(ident[:, :], 0.0).then_inc(pool_step, 1)
            pool.memset(ones[:, :], 1.0).then_inc(consts_ready, 1)
            pool.wait_ge(pool_step, 1)
            pool.affine_select(out=ident[:, :], in_=ident[:, :], compare_op=ALU.not_equal, fill=1.0, base=0,
                               pattern=[[-1, P]], channel_multiplier=1).then_inc(consts_ready, 1)
            pool.memset(eps_col[:, :], EPS)
            pool.memset(tail[:, :, :], 0.0).then_inc(tail_copied, 2)
            pool.memset(st_in[:, :, :], 0.0).then_inc(st_zeroed, 1)

            pool.memset(pair_ones[:, :], 0.0).then_inc(pool_step, 1)
            pool.memset(sc_mask[:, :], 1.0).then_inc(pool_step, 1)
            pool.memset(up_masks[:, :, :], 0.0).then_inc(pool_step, 1)
            pool.memset(eps_gn[:, :], RWKV_GN_EPS).then_inc(pool_step, 1)
            pool.wait_ge(pool_step, 5)
            n_step = [5]

            def pstep(ins):
                n_step[0] += 1
                ins.then_inc(pool_step, 1)
                pool.wait_ge(pool_step, n_step[0])

            def select(view, pattern, base, mult, op=ALU.is_ge):
                pstep(pool.affine_select(out=view, in_=view, compare_op=op, fill=0.0, base=base,
                                         pattern=pattern, channel_multiplier=mult))

            for hh in range(2):
                pstep(pool.memset(pair_ones[hh * HD:(hh + 1) * HD, hh * HD:(hh + 1) * HD], 1.0))
            two = "p (a t) -> p a t"
            for c0, strict_low in ((0, True), (P, False), (2 * P + HD, False)):
                v = sc_mask[:, c0:c0 + P].rearrange(two, a=2)
                if strict_low:
                    select(v, [[-HD, 2], [-1, HD]], 0, 1, ALU.is_gt)
                    select(v, [[HD, 2], [0, HD]], HD - 1, -1)
                else:
                    select(v, [[HD, 2], [1, HD]], 0, -1, ALU.is_gt)
                    select(v, [[-HD, 2], [0, HD]], 0, 1)
            for c0 in (2 * P, 3 * P + HD):
                for hh in range(2):
                    select(sc_mask[hh * HD:(hh + 1) * HD, c0:c0 + HD], [[1, HD]], 0, -1)
            for i, z in enumerate((1,) + LEVELS):
                v = up_masks[:, i, :].rearrange("p (a two z) -> p a two z", two=2, z=z)[:, :, 1, :]
                pstep(pool.memset(v, 1.0))
                select(v, [[-2 * z, P // (2 * z)], [0, z]], 0, 1)
                select(v, [[2 * z, P // (2 * z)], [0, z]], z - 1, -1)
            pstep(pool.memset(low_mask[:, :], 0.0))
            v = low_mask[:, :].rearrange("p (a two) -> p a two", two=2)[:, :, 0]
            pstep(pool.memset(v, 1.0))
            select(v, [[-2, HD]], 0, 1, ALU.is_gt)
            select(v, [[2, HD]], 1, -1)
            pool.sem_inc(masks_ready, 1)

            def low(n, s):
                pool.wait_ge(hi_done, n + 1)
                pool.tensor_tensor(w_lo[:, s, :, :], w_raw[:, s, :, :], w_hi[:, s, :, :].bitcast(F32),
                                   ALU.subtract).then_inc(lo_done, 1)

            def tails(q, e, ready):
                pool.wait_ge(ready, q + 1)
                pool.wait_ge(tail_turned, q + 1)
                pool.tensor_tensor(tail[:, e, 0:2], gate[:, e, TP:TP + 2], ones[:, 0:2], ALU.mult).then_inc(pool_step, 1)
                pool.tensor_tensor(tail[:, e, 2:2 + NS], gate[:, e, TP + 4:GW:3], ones[:, 0:NS], ALU.mult).then_inc(tail_copied, 1)

            low(0, 0)
            for p in plan:
                n0, q0 = p["blk"], p["unit"]
                last = p["last"]
                if p["kind"] == "pre":
                    low(n0 + 1, 1)
                    for k in range(0 if p["full"] else KT):
                        pool.wait_ge(uhi_done, p["split"] * KT + k + 1)
                        pool.tensor_tensor(u_lo[:, k, 0:TP], usb[:, k % 2, 0:TP], u_hi[:, k, 0:TP].bitcast(F32),
                                           ALU.subtract).then_inc(u_ready, 1)
                elif p["kind"] == "post":
                    pool.wait_ge(rstd_ready, p["post"] + 1)
                    for k in POOL_TILES:
                        pool.tensor_tensor(p["proj"][:, k, 0:TP], p["proj"][:, k, 0:TP], rstd[:, 0:TP],
                                           ALU.mult).then_inc(tile_scaled, 1)
                elif p["kind"] == "sconv":
                    def conv_tile(it, e, ahead):
                        n, k = n0 + 6 * it + 3 * e, 3 * e
                        low(n + 2, k % 2)
                        low(n + 3, (k + 1) % 2)
                        tails(q0 + 2 * it + e, e, gate_ready)
                        if ahead:
                            low(n + 4, k % 2)

                    with pool.Fori(0, p["iters"] - 1) as it:
                        conv_tile(it, 0, True)
                        conv_tile(it, 1, True)
                    conv_tile(p["iters"] - 1, 0, True)
                    conv_tile(p["iters"] - 1, 1, False)
                elif p["kind"] == "rproj":
                    def mix_low(o):
                        lo, hi = (u_lo, u_hi) if o % 2 == 0 else (xb_lo, xb_hi)
                        for k in range(0, KT, 2):
                            pool.wait_ge(xhi_done, KT * o + k + 1)
                            pool.tensor_tensor(lo[:, k, :], mix_tile(KT * o + k), hi[:, k, :].bitcast(F32),
                                               ALU.subtract).then_inc(x_ready[0], 1)

                    mix_low(0)
                    mix_low(1)
                    mix_low(2)
                    low(n0 + 2, 0)
                    mix_low(3)
                    low(n0 + 3, 1)
                    low(n0 + 4, 0)
                    for i in range(3):
                        if i < 2:
                            mix_low(4 + i)
                        iters = KT // 2 - (i == 2)
                        nb = n0 + 4 + KT * i
                        with pool.Fori(0, iters) as it:
                            for e in range(2):
                                low(nb + 2 * it + e + 1, (e + 1) % 2)
                    low(n0 + 27, 1)
                elif p["kind"] == "gproj":
                    low(n0 + 2, 0)
                    with pool.Fori(0, GT // 2 - 1) as it:
                        for e in range(2):
                            low(n0 + 3 + 2 * it + e, 1 - e)
                    low(n0 + 25, 1)
                elif p["kind"] == "gla":
                    pool.wait_ge(gargs_ready, G_SUM)
                    pool.wait_ge(g_turned, G_VROW)
                    for lvl, z in enumerate(G_LEVELS):
                        if lvl == 1:
                            pool.wait_ge(gkhat_ready, 1)
                        elif lvl >= 2:
                            pool.wait_ge(glevel_ready, 2 * (lvl - 1))
                        Gb = g_G[:, :, :].rearrange("p h (b t) -> p h b t", t=2 * z)
                        eb = (g_z2, g_z)[lvl % 2][:, :, 0:TP].rearrange("p h (b t) -> p h b t", t=2 * z)
                        ref = Gb[:, :, :, z - 1:z].to_broadcast([P, GH, TP // (2 * z), z])
                        pool.tensor_tensor(eb[:, :, :, z:2 * z], Gb[:, :, :, z:2 * z], ref, ALU.subtract)
                        pool.tensor_tensor(eb[:, :, :, 0:z], ref, Gb[:, :, :, 0:z], ALU.subtract)\
                            .then_inc(g_pool_done, 1)
                    pool.wait_ge(go_copied, 2 * NGC)
                    pool.wait_ge(gsilu_done, 1)
                    for k in range(KT):
                        pool.tensor_tensor(g_og[:, k, :], g_og[:, k, :], g_o[:, k, :], ALU.mult).then_inc(g_pool_done, 1)
                    for k in range(KT):
                        if k == 6:
                            low(n0, n0 % 2)
                        pool.wait_ge(gyhi_done, k + 1)
                        pool.tensor_tensor(u_lo[:, k, :], prod[:, k % 2, :], u_hi[:, k, :].bitcast(F32),
                                           ALU.subtract).then_inc(gy_ready, 1)
                elif p["kind"] == "rwkv":
                    def masked(w, q, g, lvl):
                        if lvl:
                            pool.wait_ge(t1_mm, 10 * w + 2 * lvl + g - 1)
                        else:
                            pool.wait_ge(mmt_ready, 12 * w + g + 1)
                        m = up_masks[:, lvl + 1, :].unsqueeze(1).to_broadcast([P, 2, P])
                        pool.tensor_tensor(ct[:, 2 * g:2 * g + 2, :], sc[q][:, 2 * g:2 * g + 2, P:2 * P], m,
                                           ALU.mult).then_inc(ct_ready, 1)

                    for k in range(KT):
                        pool.wait_ge(knorm_done, k + 1)
                        pool.wait_ge(kk_ready, k + 1)
                        pool.tensor_tensor(rw_k[:, k, :], rw_k[:, k, :], tmp8[:, 4 + k % 2, :], ALU.mult)\
                            .then_inc(keys_ready, 1)
                    with pool.Fori(0, NCH) as c:
                        for q in range(2):
                            for lvl in range(len(LEVELS)):
                                for g in range(2):
                                    masked(2 * c + q, q, g, lvl)
                    for k in range(KT):
                        if k == 7:
                            low(n0, n0 % 2)
                        pool.wait_ge(yhi_done, k + 1)
                        pool.tensor_tensor(u_lo[:, k, :], gated_sb[:, k % 2, :], u_hi[:, k, :].bitcast(F32),
                                           ALU.subtract).then_inc(xy_ready, 1)
                elif p["kind"] == "out":
                    with pool.Fori(0, p["iters"]) as it:
                        for e in range(2):
                            low(n0 + 2 * it + e + 1, (e + 1) % 2)
                elif p["kind"] == "up":
                    def hidden_tile(it, e, ahead):
                        tails(q0 + 2 * it + e, e, gate_ready)
                        low(n0 + 4 * it + 2 * e + 2, 0)
                        if ahead:
                            low(n0 + 4 * it + 2 * e + 3, 1)

                    with pool.Fori(0, p["iters"] - 1) as it:
                        hidden_tile(it, 0, True)
                        hidden_tile(it, 1, True)
                    hidden_tile(p["iters"] - 1, 0, True)
                    hidden_tile(p["iters"] - 1, 1, False)
                elif p["kind"] == "down":
                    iters = p["iters"] - last
                    if iters:
                        with pool.Fori(0, iters) as it:
                            for k in range(6):
                                low(n0 + 6 * it + k + 1, (k + 1) % 2)
                    if last:
                        for k in range(5):
                            low(n0 + 6 * iters + k + 1, (k + 1) % 2)

        @block.scalar
        def _(act):
            act.wait_ge(rows_loaded, 16 * NLOADS)
            act.activation(c_rows[:, :], c_rows[:, :], ACT.Silu).then_inc(c_silu, 1)
            act.wait_ge(consts_ready, 2)
            act.activation(rows[:, 0, :], ones[0:2 + NS, :], ACT.Copy).then_inc(rows_out[0], 32)
            act.activation(rows[:, 1, :], ones[0:2 + NS, :], ACT.Copy).then_inc(rows_out[1], 32)
            for k in range(KT):
                act.wait_ge(pro_turned, k + 1)
                act.activation(h[:, k, 0:TP], bank[k][:, :], ACT.Copy).then_inc(x_copied, 1)

            def high(n, s):
                act.wait_ge(w_loaded[s], 16 * half_of(n) + 16)
                act.wait_ge(block_done, n + 1)
                act.activation(w_hi[:, s, :, :], w_raw[:, s, :, :], ACT.Copy).then_inc(hi_done, 1)

            def place_state(q, e):
                act.wait_ge(st_turned, q + 3)
                act.activation(gate[:, e, TP + 2:GW].rearrange("p (b r) -> p b r", r=3)[:, :, 0:2],
                               st_ps[:, 0:2 * NS].rearrange("p (b r) -> p b r", r=2), ACT.Copy)\
                   .then_inc(st_placed, 1)

            def rows_to_dram(q, qh, e, prompt, sample):
                act.wait_ge(tail_turned, q + 3)
                act.wait_ge(rows_out[e], 32 * qh + 32)
                act.activation(rows[:, e, :], tail_ps[0:2 + NS, 0:P], ACT.Copy).then_inc(rows_copied, 1)
                act.wait_ge(rows_copied, q + 2)
                act.dma_start(prompt, rows[0:2, e, :]).then_inc(rows_out[e], 16)
                act.dma_start(sample, rows[2:2 + NS, e, :]).then_inc(rows_out[e], 16)

            act.wait_ge(x_copied, KT)
            act.sem_inc(rows_copied, 1)
            act.sem_inc(st_placed, 1)
            half_of = lambda n: 0
            high(0, 0)

            def evacuate(s, n, dst):
                act.wait_ge(block_done, n + 3)
                act.activation(dst[:, 0:HALF], tile_ps[s][0][:, 0:HALF], ACT.Copy)
                return act.activation(dst[:, HALF:T], tile_ps[s][1][:, 0:HALF], ACT.Copy)

            for p in plan:
                l, n0, q0, t0 = p["l"], p["blk"], p["unit"], p["tile"]
                last = p["last"]
                if p["kind"] == "pre":
                    i, hs = p["pre"], KT * p["post"]
                    for k in range(KT):
                        act.wait_ge(h_ready, hs + k + 1)
                        if KT * i + k >= 2:
                            act.wait_ge(sq_used, KT * i + k - 1)
                        act.activation(sq[:, k % 2, :], h[:, k, :], ACT.Square).then_inc(sq_done, 1)
                    act.wait_ge(sq_used, KT * (i + 1))
                    act.activation(std[:, 0:HALF], ss_ps[0][:, 0:HALF], ACT.Sqrt, bias=eps_col[:, 0:1], scale=1.0 / D)
                    act.activation(std[:, HALF:T], ss_ps[1][:, 0:HALF], ACT.Sqrt, bias=eps_col[:, 0:1],
                                   scale=1.0 / D).then_inc(std_done, 1)
                    half_of = lambda _n: n0 // 2
                    high(n0 + 1, 1)
                    for k in range(KT):
                        act.wait_ge(norm_done, KT * i + k + 1)
                        dst = usb[:, k % 2, 0:TP]
                        if p["full"]:
                            dst = rw_u[:, k, 0:TP]
                        elif KT * p["split"] + k >= 2:
                            act.wait_ge(u_ready, KT * p["split"] + k - 1)
                        act.activation(dst, normed[:, k % 2, 0:TP], ACT.Identity,
                                       bias=p["mod"][:, k, 0:1], scale=p["mod"][:, KT + k, 0:1]).then_inc(usb_done, 1)
                elif p["kind"] == "post":
                    act.activation(warm[:, :], eps_col[:, :], ACT.Sqrt)
                    act.wait_ge(ss_done, p["post"] + 1)
                    act.activation(std[:, 0:HALF], ss_ps[0][:, 0:HALF], ACT.Sqrt, bias=eps_col[:, 0:1], scale=1.0 / D)
                    act.activation(std[:, HALF:T], ss_ps[1][:, 0:HALF], ACT.Sqrt, bias=eps_col[:, 0:1],
                                   scale=1.0 / D).then_inc(std_done, 1)
                elif p["kind"] == "sconv":
                    j = l // 3

                    def conv_tile(it, e, ahead):
                        nonlocal half_of
                        n, q, m = n0 + 6 * it + 3 * e, q0 + 2 * it + e, 2 * it + e
                        k = 3 * e
                        act.wait_ge(conv_done, q + 1)
                        act.wait_ge(tail_copied, q + 1)
                        place_state(q, e)
                        evacuate(k % 2, n, csb[:, e, :]).then_inc(tile_free[k % 2], 1)
                        for i in range(2, 4 + ahead):
                            half_of = lambda _n, i=i: n0 // 2 + 3 * it + (k + i) // 2
                            high(n + i, (k + i) % 2)
                        rows_to_dram(q, q0 // 2 + it, e,
                                     O["conv_a_prompt"][j, 0, :, ds(m * P, P)],
                                     O["conv_a_sample"][j, :, 1, ds(m * P, P)])

                    with act.Fori(0, p["iters"] - 1) as it:
                        conv_tile(it, 0, True)
                        conv_tile(it, 1, True)
                    conv_tile(p["iters"] - 1, 0, True)
                    conv_tile(p["iters"] - 1, 1, False)
                elif p["kind"] == "rproj":
                    act.wait_ge(shift_turned, 2)
                    act.activation(shift_rows[:, 0:512], bank[6][0:NSEQ, :], ACT.Copy)
                    act.activation(shift_rows[:, 512:D], bank[7][0:NSEQ, :], ACT.Copy).then_inc(urows_copied, 1)
                    act.wait_ge(urows_copied, 1)
                    act.dma_start(O["shift_b_prompt"][0], shift_rows[0:1, :]).then_inc(shift_out, 16)
                    act.dma_start(O["shift_b_sample"][0], shift_rows[1:NSEQ, :]).then_inc(shift_out, 16)

                    def mix_high(o):
                        hi = u_hi if o % 2 == 0 else xb_hi
                        if o == 2:
                            act.wait_ge(block_done, n0 + 1 + 2)
                        elif o == 3:
                            act.wait_ge(block_done, n0 + 2 + 2)
                        elif o >= 4:
                            act.wait_ge(block_done, n0 + 4 + KT * (o - 4) + 2)
                        for k in range(KT):
                            act.wait_ge(mixed, KT * o + k + 1)
                            act.activation(hi[:, k, :], mix_tile(KT * o + k), ACT.Copy).then_inc(xhi_done, 1)

                    def lora_tile(n, s, dst, func):
                        act.wait_ge(block_done, n + 3)
                        act.activation(dst[:, 0:HALF], tile_ps[s][0][0:HD, 0:HALF], func)
                        act.activation(dst[:, HALF:T], tile_ps[s][1][0:HD, 0:HALF], func).then_inc(tile_free[s], 1)

                    half_of = lambda _n: n0 // 2
                    mix_high(0)
                    mix_high(1)
                    lora_tile(n0, 0, t_lora[:, 0, :], ACT.Tanh)
                    mix_high(2)
                    half_of = lambda _n: n0 // 2 + 1
                    high(n0 + 2, 0)
                    lora_tile(n0 + 1, 1, t_lora[:, 1, :], ACT.Copy)
                    mix_high(3)
                    high(n0 + 3, 1)
                    lora_tile(n0 + 2, 0, t_g[:, 0, :], ACT.Sigmoid)
                    half_of = lambda _n: n0 // 2 + 2
                    high(n0 + 4, 0)
                    lora_tile(n0 + 3, 1, t_g[:, 1, :], ACT.Sigmoid)
                    act.wait_ge(shift_out, 32)
                    for i, dst_slab in enumerate((rw_r, rw_k, rw_v)):
                        if i < 2:
                            mix_high(4 + i)
                        else:
                            act.wait_ge(mixed, KT * 6)
                        nb = n0 + 4 + KT * i

                        def proj_tile(it, e, ahead):
                            nonlocal half_of
                            n = nb + 2 * it + e
                            if ahead:
                                half_of = lambda _n: nb // 2 + it + (e + 1) // 2
                                high(n + 1, (e + 1) % 2)
                            dst = dst_slab[:, ds(2 * it + e, 1), :].rearrange("p a t -> p (a t)")
                            evacuate(e, n, dst).then_inc(tile_free[e], 1)

                        with act.Fori(0, KT // 2 - (i == 2)) as it:
                            proj_tile(it, 0, True)
                            proj_tile(it, 1, True)
                        if i == 2:
                            proj_tile(KT // 2 - 1, 0, True)
                            proj_tile(KT // 2 - 1, 1, False)
                elif p["kind"] == "gproj":
                    def gate_rank(n, s):
                        act.wait_ge(block_done, n + 3)
                        act.activation(t_ga[:, s, 0:HALF], tile_ps[s][0][0:8, 0:HALF], ACT.Copy)
                        act.activation(t_ga[:, s, HALF:T], tile_ps[s][1][0:8, 0:HALF], ACT.Copy)\
                           .then_inc(tile_free[s], 1)

                    half_of = lambda _n: n0 // 2
                    gate_rank(n0, 0)
                    half_of = lambda _n: n0 // 2 + 1
                    high(n0 + 2, 0)
                    gate_rank(n0 + 1, 1)

                    def in_tile(it, e, ahead):
                        nonlocal half_of
                        n = n0 + 2 + 2 * it + e
                        if ahead:
                            half_of = lambda _n: n0 // 2 + 1 + it + (e + 1) // 2
                            high(n + 1, 1 - e)
                        dst = g_in[:, ds(2 * it + e, 1), :].rearrange("p a t -> p (a t)")
                        evacuate(e, n, dst).then_inc(tile_free[e], 1)

                    with act.Fori(0, GT // 2 - 1) as it:
                        in_tile(it, 0, True)
                        in_tile(it, 1, True)
                    in_tile(GT // 2 - 1, 0, True)
                    in_tile(GT // 2 - 1, 1, False)
                elif p["kind"] == "gla":
                    act.wait_ge(block_done, n0 + 2)
                    for k in range(GH):
                        act.wait_ge(gz_mm, k + 1)
                        for func, dst, done in ((ACT.Identity, g_z, gz_done), (ACT.Abs, g_e, ggate_done)):
                            for half in range(2):
                                ins = act.activation(dst[:, k, half * HALF:(half + 1) * HALF],
                                                     tile_ps[k % 2][half][:, 0:HALF], func, bias=vec("gla_ba", k))
                            ins.then_inc(done, 1)
                    act.wait_ge(ggate_done, G_ABS)
                    act.activation(g_e[:, :, :], g_e[:, :, :], ACT.Exp, scale=-1.0).then_inc(ggate_done, 1)
                    act.wait_ge(ggate_done, G_ABS + 1)
                    act.activation(g_e[:, :, :], g_e[:, :, :], ACT.Ln, bias=1.0).then_inc(ggate_done, 1)
                    act.wait_ge(gargs_ready, G_LOG)
                    act.activation(g_dec[:, :, :], g_z[:, :, TP:T], ACT.Exp).then_inc(ggate_done, 1)
                    act.wait_ge(gargs_ready, G_SUM)
                    act.activation(g_end[:, :, :], g_G[:, :, GC - 1:TP:GC], ACT.Exp).then_inc(gexp_done, 1)
                    act.activation(g_e[:, :, 0:TP], g_G[:, :, :], ACT.Exp).then_inc(gexp_done, 1)
                    act.wait_ge(gargs_ready, G_TAIL)
                    act.activation(g_z[:, :, 0:TP], g_z[:, :, 0:TP], ACT.Exp).then_inc(gexp_done, 1)
                    act.activation(g_og[:, :, :], g_og[:, :, :], ACT.Silu).then_inc(gsilu_done, 1)
                    for c in range(NGC):
                        act.wait_ge(g_turned, c + 1)
                        act.activation(g_Kt[:, c, :, :], bank[4 + c][:, :].rearrange("p (h k) -> p h k", h=GH), ACT.Copy)\
                           .then_inc(g_copied, 1)
                    for n in range(2 * NGC):
                        act.wait_ge(g_turned, G_K + n + 1)
                        act.activation(g_Vt[:, n // 2, (n % 2) * 512:(n % 2 + 1) * 512], bank[4 + n % 4][:, :],
                                       ACT.Copy).then_inc(g_copied, 1)
                    for n in range(2):
                        act.wait_ge(g_turned, G_V + n + 1)
                        act.activation(g_vrow[:, n * 512:(n + 1) * 512], bank[4 + n][0:NS, :], ACT.Copy)\
                           .then_inc(g_copied, 1)
                    act.wait_ge(gS_loaded, 32)
                    act.wait_ge(ggate_done, G_DEC)
                    for b in range(NS):
                        for hd in range(GH):
                            x = b * GH + hd
                            ins = act.activation(g_sS[:, x, :], g_sS[:, x, :], ACT.Copy, scale=g_dec[:, hd, b:b + 1])
                        ins.then_inc(gs_decayed, 1)
                    for lvl in range(len(G_LEVELS)):
                        act.wait_ge(g_pool_done, lvl + 1)
                        z = (g_z2, g_z)[lvl % 2][:, :, 0:TP]
                        act.activation(z, z, ACT.Exp).then_inc(gexp_done, 1)
                    act.wait_ge(gs_ready, NS)
                    for half in range(2):
                        hs = slice(half * NS * GH // 2, (half + 1) * NS * GH // 2)
                        act.dma_start(O["gla_c_sample"][0].rearrange("b h k v -> k (b h) v")[:, hs, :],
                                      g_sS[:, hs, :]).then_inc(gs_out, 16)
                    act.wait_ge(gs_o_mm, 1)
                    act.activation(g_o[:, :, TP:T], bank[7][:, 0:KT * NS].rearrange("p (k s) -> p k s", k=KT), ACT.Copy)
                    for c in range(NGC):
                        for g in range(2):
                            act.wait_ge(go_mm, 2 * c + g + 1)
                            ins = act.activation(g_o[:, 4 * g:4 * g + 4, c * GC:(c + 1) * GC],
                                                 bank[g + 2 * (c % 2)][:, :].rearrange("p (k t) -> p k t", k=4), ACT.Copy)
                            ins.then_inc(go_copied, 1)
                    act.wait_ge(gS_ready, NGC * GH + 1)
                    act.dma_start(O["gla_c_prompt"][0, 0].rearrange("h k v -> k h v"), g_S[:, :, :]).then_inc(gS_out, 16)
                    act.wait_ge(go_copied, 2 * NGC)
                    for hd in range(GH):
                        for i in range(2):
                            k = 2 * hd + i
                            if k >= 2:
                                act.wait_ge(gss_mm, hd)
                            act.activation(g_sq[:, k % 2, :], g_o[:, k, :], ACT.Square).then_inc(gsq_done, 1)
                        act.wait_ge(gss_mm, hd + 1)
                        if hd:
                            act.wait_ge(gon_done, hd)
                        for half in range(2):
                            ins = act.activation(std[:, half * HALF:(half + 1) * HALF], ss_ps[half][:, 0:HALF], ACT.Sqrt,
                                                 bias=eps_col[:, 0:1], scale=1.0 / GDV)
                        ins.then_inc(gon_std, 1)
                    act.wait_ge(gS_out, 16)
                    half_of = lambda _n: n0 // 2
                    high(n0, n0 % 2)
                elif p["kind"] == "rwkv":
                    for k in range(KT):
                        for slot, done, dst, bias, sig in ((0, zw_done, rw_G, "rwkv_w0", sig_w),
                                                           (1, za_done, rw_b, "rwkv_a0", sig_a)):
                            act.wait_ge(done, k + 1)
                            for half in range(2):
                                ins = act.activation(dst[:, k, half * HALF:(half + 1) * HALF],
                                                     tile_ps[slot][half][:, 0:HALF], ACT.Sigmoid, bias=vec(bias, k))
                            ins.then_inc(sig, 1)
                    for k in range(KT):
                        if k >= 2:
                            act.wait_ge(ksum_done, k - 1)
                        act.activation(tmp8[:, k % 2, :], rw_k[:, k, :], ACT.Square, scale=vec("rwkv_k_k", k))\
                           .then_inc(ksq_done, 1)
                        if k == 0:
                            act.wait_ge(prep_done, 1)
                        if k >= 2:
                            act.wait_ge(kk_ready, k - 1)
                            act.wait_ge(keys_ready, k - 1)
                        act.activation(tmp8[:, 4 + k % 2, :], rw_b[:, k, :], ACT.Identity,
                                       bias=one_less_ka[:, k:k + 1], scale=vec("rwkv_k_a", k))
                        act.wait_ge(ksum_done, k + 1)
                        for half in range(2):
                            ins = act.activation(tmp8[:, 2 + k % 2, half * HALF:(half + 1) * HALF],
                                                 ss_ps[half][:, 0:HALF], ACT.Sqrt)
                        ins.then_inc(knorm_done, 1)
                    act.activation(decay_s[:, :, :], rw_G[:, :, TP:T], ACT.Exp).then_inc(decay_done, 1)
                    act.wait_ge(kk_ready, KT)
                    act.wait_ge(keys_ready, KT)
                    act.dma_start(s_state[:, :, :], A["state_wkv_b"][0].rearrange("b h v k -> (b h) v k"))\
                       .then_inc(sstate_loaded, 16)
                    for j, (i, _) in enumerate(SAMPLE_ROWS):
                        act.wait_ge(srow_turned, j + 1)
                        act.activation(s_rows[:, i, 0:512], bank[2 * (j % 2)][0:NS, :], ACT.Copy)
                        act.activation(s_rows[:, i, 512:D], bank[2 * (j % 2) + 1][0:NS, :], ACT.Copy)\
                           .then_inc(srow_copied, 1)
                        act.wait_ge(srow_copied, j + 1)
                        act.dma_start(s_vec[:, i, :], s_rows[:, i, :]).then_inc(svec_loaded, 16)
                    act.wait_ge(s_y_done, 1)
                    act.dma_start(O["wkv_b_sample"][0].rearrange("b h v k -> (b h) v k"), s_state[:, :, :])\
                       .then_inc(s_state_out, 16)
                    act.dma_start(s_rows[:, 0, :], s_vec[:, 7, :]).then_inc(syrow_loaded, 16)
                    act.wait_ge(srow_turned, 7)
                    act.activation(rw_y[:, :, TP:T], bank[0][:, 0:KT * NS].rearrange("p (k s) -> p k s", k=KT),
                                   ACT.Copy).then_inc(srow_copied, 1)
                    act.wait_ge(bd_zeroed, 2)
                    act.sem_inc(y_ready, 1)

                    def exponents(c, q):
                        src, b = rw_G[:, 4 * q:4 * q + 4, ds(HD * c, HD)], bd[q]
                        act.activation(b["Ep"][:, :, 1:HD + 1], src, ACT.Exp)
                        act.activation(b["Em"][:, :, :], src, ACT.Exp, scale=-1.0).then_inc(exp_done, 1)

                    def values(c, q):
                        for hh in range(2):
                            rs = slice(hh * HD, (hh + 1) * HD)
                            ins = act.activation(bd[q]["Vf"][rs, :, rs], rw_v[rs, 4 * q:4 * q + 4, ds(HD * c, HD)],
                                                 ACT.Copy)
                        ins.then_inc(vf_ready, 1)

                    def tokens_out(w):
                        for i, (n, bk) in enumerate(((2, 4), (0, 1), (1, 3))):
                            act.wait_ge(tok_done, 3 * w + i + 1)
                            act.activation(tok[:, :, n * P:(n + 1) * P], bank[bk][:, :].rearrange("p (i t) -> p i t", i=4),
                                           ACT.Copy).then_inc(tok_ready, 1)

                    def scan_step(c, q, one_more, two_more):
                        w = 2 * c + q
                        for lvl in range(len(LEVELS)):
                            for g in range(2):
                                act.wait_ge(t1_mm, 10 * w + 2 * lvl + g + 1)
                                act.activation(t1[:, 2 * g:2 * g + 2, :],
                                               bank[2 * g][:, 0:2 * P].rearrange("p (i t) -> p i t", i=2),
                                               ACT.Copy).then_inc(t1_ready, 1)
                            if lvl == 0:
                                act.wait_ge(rhs_mm, w + 1)
                                act.activation(rhs_sb[:, :, :], bank[4][:, :].rearrange("p (i t) -> p i t", i=4),
                                               ACT.Copy).then_inc(rhs_ready, 1)
                            if lvl == 1 and two_more:
                                act.wait_ge(bd_ready, w + 1)
                                exponents(c + 1, q)
                            if lvl == 2 and two_more:
                                act.wait_ge(tok_done, 3 * w + 1)
                                values(c + 1, q)
                        act.wait_ge(u_mm, w + 1)
                        act.activation(uu[:, :, :], bank[5][:, :].rearrange("p (i t) -> p i t", i=4), ACT.Copy)\
                           .then_inc(uu_ready, 1)
                        act.wait_ge(y_mm, w + 1)
                        act.activation(rw_y[:, 4 * q:4 * q + 4, ds(HD * c, HD)],
                                       bank[6][:, 0:4 * HD].rearrange("p (i t) -> p i t", i=4), ACT.Copy)\
                           .then_inc(y_ready, 1)
                        if one_more:
                            act.wait_ge(st_mm, w + 1)
                            tokens_out(w + 1)

                    for q in range(2):
                        exponents(0, q)
                        values(0, q)
                    tokens_out(0)
                    with act.Fori(0, NCH - 1) as c:
                        for q in range(2):
                            scan_step(c, q, True, True)
                    for q in range(2):
                        scan_step(NCH - 1, q, q == 0, False)
                    act.dma_start(g2[:, :, :], A["rwkv_g2"][0].rearrange("(i r) c -> r i c", i=2)).then_inc(g2_loaded, 16)
                    act.wait_ge(srow_turned, 8)
                    for hh in range(2):
                        rs = slice(hh * HD, (hh + 1) * HD)
                        for i in range(2):
                            ins = act.activation(wkv_out[rs, 4 * i:4 * i + 4, :],
                                                 bank[i][rs, :].rearrange("p (i t) -> p i t", i=4)[:, :, rs], ACT.Copy)
                    ins.then_inc(wkv_copied, 1)
                    act.wait_ge(wkv_copied, 1)
                    for hh in range(2):
                        rs = slice(hh * HD, (hh + 1) * HD)
                        act.dma_start(O["wkv_b_prompt"][0, 0].rearrange("(j a) v k -> a v j k", a=2)[hh],
                                      wkv_out[rs, :, :]).then_inc(wkv_out_done, 16)
                    for k in range(KT + 2):
                        if k < KT:
                            act.wait_ge(centred, k + 1)
                            if k >= 2:
                                act.wait_ge(var_mm, k - 1)
                            act.activation(gn_tmp[:, k % 2, :], rw_y[:, k, :], ACT.Square).then_inc(csq_done, 1)
                        if 1 <= k <= KT:
                            j = k - 1
                            act.wait_ge(var_mm, j + 1)
                            if j >= 2:
                                act.wait_ge(ynorm_done, j - 1)
                            for half in range(2):
                                ins = act.activation(gn_tmp[:, 2 + j % 2, half * HALF:(half + 1) * HALF],
                                                     tile_ps[1][half][:, 0:HALF], ACT.Sqrt, bias=eps_gn[:, 0:1],
                                                     scale=1.0 / HD)
                            ins.then_inc(gstd_done, 1)
                        if k >= 2:
                            j = k - 2
                            act.wait_ge(ynorm_done, j + 1)
                            act.activation(rw_y[:, j, :], rw_y[:, j, :], ACT.Identity, bias=vec("rwkv_lnx_b", j),
                                           scale=vec("rwkv_lnx_w", j)).then_inc(yaff_done, 1)
                    act.wait_ge(wkv_out_done, 32)
                    half_of = lambda _n: n0 // 2
                    high(n0, n0 % 2)
                elif p["kind"] == "out":
                    with act.Fori(0, p["iters"]) as it:
                        for e in range(2):
                            n = n0 + 2 * it + e
                            half_of = lambda _n, e=e: n0 // 2 + it + (e + 1) // 2
                            high(n + 1, (e + 1) % 2)
                            dst = p["proj"][:, ds(2 * it + e, 1), :].rearrange("p a t -> p (a t)")
                            evacuate(e, n, dst).then_inc(tile_free[e], 1)
                elif p["kind"] == "up":
                    act.activation(warm[:, :], eps_col[:, :], ACT.Silu)

                    def hidden_tile(it, e, ahead):
                        nonlocal half_of
                        n, q, m = n0 + 4 * it + 2 * e, q0 + 2 * it + e, 2 * it + e
                        act.wait_ge(conv_done, q + 1)
                        act.wait_ge(tail_copied, q + 1)
                        place_state(q, e)
                        act.wait_ge(block_done, n + 3)
                        act.activation(gate[:, e, 2:2 + HALF], tile_ps[0][0][:, 0:HALF], ACT.Copy)
                        act.activation(gate[:, e, 2 + HALF:2 + TP], tile_ps[0][1][:, 0:TP - HALF], ACT.Copy)
                        act.activation(gate[:, e, TP + 4:GW:3], tile_ps[0][1][:, TP - HALF:HALF], ACT.Copy)\
                           .then_inc(gate_ready, 1)
                        act.wait_ge(gate_ready, q + 1)
                        act.sem_inc(tile_free[0], 1)
                        half_of = lambda _n: n0 // 2 + 2 * it + e + 1
                        high(n + 2, 0)
                        act.wait_ge(conv_done, q + 3)
                        act.activation(conv[:, e, 0:CWD], conv[:, e, 0:CWD], ACT.Silu,
                                       bias=vec("ffn_conv_b", l * FT + m)).then_inc(silu_done, 1)
                        if ahead:
                            high(n + 3, 1)
                        rows_to_dram(q, q0 // 2 + it, e,
                                     O["conv_ffn_prompt"][l, 0, :, ds(m * P, P)],
                                     O["conv_ffn_sample"][l, :, 1, ds(m * P, P)])

                    with act.Fori(0, p["iters"] - 1) as it:
                        hidden_tile(it, 0, True)
                        hidden_tile(it, 1, True)
                    hidden_tile(p["iters"] - 1, 0, True)
                    hidden_tile(p["iters"] - 1, 1, False)
                elif p["kind"] == "down":
                    def down(it, final):
                        for e in range(2):
                            for i in range(3):
                                k = 3 * e + i
                                nonlocal half_of
                                half_of = lambda _n, k=k: n0 // 2 + 3 * it + (k + 1) // 2
                                if not (final and k == 5):
                                    high(n0 + 6 * it + k + 1, (k + 1) % 2)
                            dst = p["proj"][:, ds(2 * it + e, 1), :].rearrange("p a t -> p (a t)")
                            evacuate(e, n0 + 6 * it + 3 * e + 2, dst).then_inc(tile_free[e], 1)
                    iters = p["iters"] - last
                    if iters:
                        with act.Fori(0, iters) as it:
                            down(it, False)
                    if last:
                        down(iters, True)
            for k in range(5):
                act.wait_ge(y_turned, 2 * k + 1)
                n = P if k < 4 else NS
                act.activation(y_rows[0:n, k, 0:512], bank[(2 * k) % 8][0:n, :], ACT.Copy).then_inc(y_left, 1)
            for e in range(2):
                act.wait_ge(rows_out[e], 32 * (NUNIT // 2) + 32)

        @block.tensor
        def _(pe):
            pe.wait_ge(consts_ready, 2)
            pe.wait_ge(rows_loaded, 16 * NLOADS)
            for k in range(KT):
                for t in range(4):
                    mm = pe.transpose(bank[k][:, t * P:(t + 1) * P], x_rows[:, t, k * P:(k + 1) * P], ident[:, :])
                mm.then_inc(pro_turned, 1)
            pe.wait_ge(x_copied, 1)
            for k in range(KT):
                mm = pe.transpose(bank[0][:, k * NS:(k + 1) * NS], xs_rows[:, k * P:(k + 1) * P], ident[0:NS, 0:NS])
            mm.then_inc(pro_turned, 1)
            pe.wait_ge(x_copied, 2)
            pe.wait_ge(c_silu, 1)
            for k in range(KT):
                mm = pe.transpose(bank[1][:, k * NSEQ:(k + 1) * NSEQ], c_rows[:, k * P:(k + 1) * P],
                                  ident[0:NSEQ, 0:NSEQ])
            mm.then_inc(pro_turned, 1)
            pe.wait_ge(x_copied, 4)
            for g in range(NVG):
                rws = min(P, nrow - g * P)
                mm = pe.transpose(bank[2 + g // 4][:, (g % 4) * P:(g % 4) * P + rws], vec_rows[0:rws, g, :],
                                  ident[0:rws, 0:rws])
            mm.then_inc(pro_turned, 1)
            pe.wait_ge(x_copied, KT)
            for s in (block_done, ada_used, st_turned, tail_turned):
                pe.sem_inc(s, 2)

            def ada_tile(a, ah, s, t):
                pe.wait_ge(ada_loaded[s], 16 * (ah - GT // 2) + 16)
                for k in range(KT):
                    mm = pe.matmul(ada_ps[:, ds(t * NSEQ, NSEQ)], ada_raw[:, s, k, :], cT[:, k, :],
                                   start=(k == 0), stop=(k == KT - 1))
                mm.then_inc(ada_used, 1)

            def gemm(n, s, slot, xh, xl, k0, nk, start, stop, ready=None, width=P, mix=0):
                pe.wait_ge(hi_done, n + 1)
                pe.wait_ge(lo_done, n + 3)
                for k in range(nk):
                    if ready is x_ready:
                        pe.wait_ge(x_ready[k % 2], (mix * KT + k) // 2 + 1)
                    elif ready is not None:
                        pe.wait_ge(ready[0], ready[1] + k + 1)
                    first, final = start and k == 0, stop and k == nk - 1
                    for i, (w, x) in enumerate(((w_hi, xh), (w_hi, xl), (w_lo, xh))):
                        for half in range(2):
                            mm = pe.matmul(tile_ps[slot][half][0:width, 0:HALF], w[:, s, k, 0:width],
                                           x[:, k0 + k, half * HALF:(half + 1) * HALF],
                                           start=first and i == 0, stop=final and i == 2)
                return mm.then_inc(block_done, 1)

            def gemm_pair(n, xh, xl, ready):
                pe.wait_ge(hi_done, n + 2)
                pe.wait_ge(lo_done, n + 4)
                for k in range(KT):
                    pe.wait_ge(ready[0], ready[1] + k + 1)
                    for s in range(2):
                        for i, (w, x) in enumerate(((w_hi, xh), (w_hi, xl), (w_lo, xh))):
                            for half in range(2):
                                mm = pe.matmul(tile_ps[s][half][:, 0:HALF], w[:, s, k, :],
                                               x[:, k, half * HALF:(half + 1) * HALF],
                                               start=(k == 0 and i == 0), stop=(k == KT - 1 and i == 2))
                        if k == KT - 1:
                            mm.then_inc(block_done, 1)

            def turn_state(q, qh, e):
                pe.wait_ge(st_loaded[e], 16 * qh + 16)
                pe.wait_ge(st_placed, q + 1)
                pe.transpose(st_ps[:, 0:P], st_in[:, e, :], ident[:, :]).then_inc(st_turned, 1)

            def turn_tail(q, e):
                pe.wait_ge(tail_copied, q + 3)
                pe.wait_ge(rows_copied, q + 1)
                pe.transpose(tail_ps[0:2 + NS, 0:P], tail[:, e, :], ident[:, :]).then_inc(tail_turned, 1)

            pe.wait_ge(small_copied, 3)
            for i in range(GT // PRO_T + 1):
                if i < GT // PRO_T:
                    pe.wait_ge(ada_pro_loaded[i], 16)
                    if i >= 2:
                        pe.wait_ge(pro_mod_copied, i - 1)
                    for k in range(KT):
                        mm = pe.matmul(bank[i % 2][0:NSEQ, :], cT[:, k, :], ada_pro[i % len(ada_pro)][:, k, :],
                                       start=(k == 0), stop=(k == KT - 1))
                    mm.then_inc(pro_mod_mm, 1)
                if i:
                    pe.wait_ge(pro_mod_copied, i)
                    for j in range(PRO_T):
                        t = (i - 1) * PRO_T + j
                        pe.transpose(ada_ps[:, t * NSEQ:(t + 1) * NSEQ], mod_rows[:, (i - 1) % 2, j * P:(j + 1) * P],
                                     ident[0:NSEQ, 0:NSEQ]).then_inc(ada_used, 1)
            for p in plan:
                l, n0, q0, a0, t0 = p["l"], p["blk"], p["unit"], p["ada"], p["tile"]
                if p["kind"] == "pre":
                    i = p["pre"]
                    for k in range(KT):
                        pe.wait_ge(sq_done, KT * i + k + 1)
                        if k == 0 and q0:
                            pe.wait_ge(st_placed, q0 + 1)
                        for half in range(2):
                            mm = pe.matmul(ss_ps[half][:, 0:HALF], ones[:, :], sq[:, k % 2, half * HALF:(half + 1) * HALF],
                                           start=(k == 0), stop=(k == KT - 1))
                        mm.then_inc(sq_used, 1)
                elif p["kind"] == "post":
                    pe.wait_ge(sum_ready, p["post"] + 1)
                    for half in range(2):
                        mm = pe.matmul(ss_ps[half][:, 0:HALF], ones[:, :], csb[:, 0, half * HALF:(half + 1) * HALF],
                                       start=True, stop=True)
                    mm.then_inc(ss_done, 1)
                elif p["kind"] == "sconv":
                    pe.wait_ge(mod_ready, ada_group(p))
                    pe.wait_ge(std_done, p["norm"])

                    def conv_tile(it, e, first=False):
                        q = q0 + 2 * it + e
                        turn_state(q, q0 // 2 + it, e)
                        for i in range(3):
                            k = 3 * e + i
                            if first and i == 0:
                                pe.wait_ge(tile_free[0], t0 // 2 + 1)
                                pe.wait_ge(tile_free[1], t0 // 2 + 1)
                                gemm_pair(n0, u_hi, u_lo, (u_ready, KT * (p["split"] - 1)))
                            elif not (first and i == 1):
                                pe.wait_ge(tile_free[k % 2], t0 // 2 + 3 * it + k // 2 + 1)
                                gemm(n0 + 6 * it + k, k % 2, k % 2, u_hi, u_lo, 0, KT, True, True)
                            ada_tile(a0 + 6 * it + k, a0 // 2 + 3 * it + k // 2, k % 2, 6 * it + k)
                        turn_tail(q, e)

                    conv_tile(0, 0, True)
                    conv_tile(0, 1)
                    with pe.Fori(1, p["iters"]) as it:
                        for e in range(2):
                            conv_tile(it, e)
                elif p["kind"] == "rproj":
                    pe.wait_ge(mod_ready, ada_group(p))
                    pe.wait_ge(shift_loaded, 16)
                    pe.wait_ge(std_done, p["norm"])
                    for k in range(KT):
                        mm = pe.transpose(bank[5][:, k * NS:(k + 1) * NS], shift_in[:, k * P:(k + 1) * P],
                                          ident[0:NS, 0:NS])
                    mm.then_inc(shift_turned, 1)
                    pe.wait_ge(usb_done, KT * p["pre"])
                    pe.wait_ge(us_ready, 1)
                    for k in range(KT):
                        mm = pe.transpose(bank[6 + k // 4][0:NSEQ, (k % 4) * P:(k % 4 + 1) * P],
                                          rw_u[:, k, TP - 1:T], ident[:, :])
                    mm.then_inc(shift_turned, 1)
                    for o, (k, x) in enumerate(((0, (u_hi, u_lo)), (1, (xb_hi, xb_lo)), (2, (u_hi, u_lo)))):
                        pe.wait_ge(tile_free[k % 2], t0 // 2 + k // 2 + 1)
                        gemm(n0 + k, k % 2, k % 2, *x, 0, KT, True, True, x_ready, width=HD, mix=o)
                    pe.wait_ge(tile_free[1], t0 // 2 + 2)
                    gemm(n0 + 3, 1, 1, u_hi, u_lo, 0, KT, True, True, width=HD)
                    pe.wait_ge(urows_copied, 1)
                    for i in range(3):
                        x = (xb_hi, xb_lo) if i % 2 == 0 else (u_hi, u_lo)
                        nb, tb, ab = n0 + 4 + KT * i, t0 + 4 + KT * i, a0 + KT * i
                        with pe.Fori(0, KT // 2) as it:
                            for e in range(2):
                                pe.wait_ge(tile_free[e], tb // 2 + it + 1)
                                gemm(nb + 2 * it + e, e, e, *x, 0, KT, True, True,
                                     x_ready if e == 0 else None, mix=3 + i)
                                ada_tile(ab + 2 * it + e, ab // 2 + it, e, KT * i + 2 * it + e)
                elif p["kind"] == "gproj":
                    pe.wait_ge(mod_ready, ada_group(p))
                    for k in range(2):
                        pe.wait_ge(tile_free[k], t0 // 2 + 1)
                        gemm(n0 + k, k, k, u_hi, u_lo, 0, KT, True, True,
                             (u_ready, KT * (p["split"] - 1)) if k == 0 else None, width=8)
                    with pe.Fori(0, GT // 2) as it:
                        for e in range(2):
                            pe.wait_ge(tile_free[e], t0 // 2 + 2 + it)
                            gemm(n0 + 2 + 2 * it + e, e, e, u_hi, u_lo, 0, KT, True, True)
                            ada_tile(a0 + 2 * it + e, a0 // 2 + it, e, 2 * it + e)
                elif p["kind"] == "gla":
                    pe.wait_ge(wa2_loaded, 16)
                    for k in range(GH):
                        if k < 2:
                            pe.wait_ge(tile_free[k], t0 // 2 + 1)
                        else:
                            pe.wait_ge(ggate_done, k - 1)
                        for half in range(2):
                            for i in range(2):
                                mm = pe.matmul(tile_ps[k % 2][half][:, 0:HALF], wa2[:, i, k * P:(k + 1) * P],
                                               t_ga[:, i, half * HALF:(half + 1) * HALF], start=(i == 0), stop=(i == 1))
                        mm.then_inc(gz_mm, 1)
                    pe.wait_ge(tile_free[0], t0 // 2 + 1)
                    pe.wait_ge(tile_free[1], t0 // 2 + 1)
                    pe.wait_ge(gkhat_ready, 1)
                    for c in range(NGC):
                        for hd in range(GH):
                            mm = pe.transpose(bank[4 + c][:, hd * P:(hd + 1) * P], g_Kl[:, hd, c * GC:(c + 1) * GC],
                                              ident[:, :])
                        mm.then_inc(g_turned, 1)
                    for n in range(2 * NGC):
                        pe.wait_ge(g_copied, n + 1)
                        for i in range(4):
                            k = 4 * (n % 2) + i
                            mm = pe.transpose(bank[4 + n % 4][:, i * P:(i + 1) * P],
                                              g_v[:, k, (n // 2) * GC:(n // 2 + 1) * GC], ident[:, :])
                        mm.then_inc(g_turned, 1)
                    for n in range(2):
                        pe.wait_ge(g_copied, G_K + 5 + n)
                        for i in range(4):
                            mm = pe.transpose(bank[4 + n][0:NS, i * P:(i + 1) * P], g_v[:, 4 * n + i, TP:T], ident[:, :])
                        mm.then_inc(g_turned, 1)
                    pe.wait_ge(gq_ready, 1)
                    pe.wait_ge(ggate_done, G_ABS)

                    def level(n, kx, qx):
                        for c in range(NGC):
                            if c % 2 == 0:
                                s = c // 2
                                if n:
                                    pe.wait_ge(glevel_ready, 2 * (n - 1) + s + 1)
                                    pe.wait_ge(glevel_put, 2 * (n - 1) + s + 1)
                            for hd in range(GH):
                                mm = pe.matmul(bank[c][:, hd * P:(hd + 1) * P], kx[:, hd, c * GC:(c + 1) * GC],
                                               qx[:, hd, c * GC:(c + 1) * GC], start=True, stop=True)
                            if c % 2:
                                mm.then_inc(glevel_mm, 1)

                    level(0, g_k, g_q)
                    pe.wait_ge(g_copied, G_VROW)
                    for b in range(NS):
                        for half in range(2):
                            if b:
                                pe.wait_ge(gvb_used, b)
                            mm = pe.matmul(bank[4 + half][:, :], ident[0:NS, b:b + 1].to_broadcast([NS, P]),
                                           g_vrow[:, half * 512:(half + 1) * 512], start=True, stop=True)
                        mm.then_inc(gvb_mm, 1)
                    for b in range(NS):
                        pe.wait_ge(gs_ready, b + 1)
                        for hd in range(GH):
                            for i in range(2):
                                c0 = (2 * hd + i) * NS + b
                                mm = pe.matmul(bank[7][:, c0:c0 + 1], g_sS[:, b * GH + hd, i * P:(i + 1) * P],
                                               g_q[:, hd, TP + b:TP + b + 1], start=True, stop=True)
                    mm.then_inc(gs_o_mm, 1)
                    for lvl in range(len(G_LEVELS)):
                        level(lvl + 1, g_Kl, g_Ql)
                    pe.wait_ge(glevel_put, 2 * (len(G_LEVELS) + 1))
                    pe.wait_ge(gq_ready, 2)
                    for c in range(NGC):
                        if c:
                            pe.wait_ge(gS_ready, GH * c + 1)
                        else:
                            pe.wait_ge(gS_ready, 1)
                        for g in range(2):
                            if c >= 2:
                                pe.wait_ge(go_copied, 2 * (c - 2) + g + 1)
                            for i in range(4):
                                hd, half = 2 * g + i // 2, i % 2
                                o = bank[g + 2 * (c % 2)][:, i * P:(i + 1) * P]
                                vs = slice(hd * GDV + half * P, hd * GDV + (half + 1) * P)
                                pe.matmul(o, g_S[:, hd, half * P:(half + 1) * P], g_e[:, hd, c * GC:(c + 1) * GC],
                                          start=True, stop=False)
                                mm = pe.matmul(o, g_Vt[:, c, vs], g_AT[:, c * GH + hd, :], start=False, stop=True)
                            mm.then_inc(go_mm, 1)
                        for g in range(2):
                            for i in range(2):
                                hd = 2 * g + i
                                mm = pe.matmul(bank[4 + g][:, i * GDV:(i + 1) * GDV], g_Kt[:, c, hd, :],
                                               g_Vt[:, c, hd * GDV:(hd + 1) * GDV], start=True, stop=True)
                        mm.then_inc(gsu_mm, 1)
                    pe.wait_ge(gS_ready, NGC * GH + 1)
                    for hd in range(GH):
                        for i in range(2):
                            k = 2 * hd + i
                            pe.wait_ge(gsq_done, k + 1)
                            if k and i == 0:
                                pe.wait_ge(gon_std, hd)
                            for half in range(2):
                                mm = pe.matmul(ss_ps[half][:, 0:HALF], ones[:, :],
                                               g_sq[:, k % 2, half * HALF:(half + 1) * HALF], start=(i == 0),
                                               stop=(i == 1))
                        mm.then_inc(gss_mm, 1)
                elif p["kind"] == "rwkv":
                    pe.wait_ge(lora_loaded, 32)
                    for k in range(KT):
                        for slot, done, sig in ((0, zw_done, sig_w), (1, za_done, sig_a)):
                            pe.wait_ge(tile_free[slot], t0 // 2 + 1)
                            if k:
                                pe.wait_ge(sig, k)
                            for half in range(2):
                                mm = pe.matmul(tile_ps[slot][half][:, 0:HALF], lora2[:, slot, k * P:(k + 1) * P],
                                               t_lora[:, slot, half * HALF:(half + 1) * HALF], start=True, stop=True)
                            mm.then_inc(done, 1)
                    for k in range(KT):
                        pe.wait_ge(ksq_done, k + 1)
                        if k:
                            pe.wait_ge(knorm_done, k)
                        for half in range(2):
                            mm = pe.matmul(ss_ps[half][:, 0:HALF], pair_ones[:, :],
                                           tmp8[:, k % 2, half * HALF:(half + 1) * HALF], start=True, stop=True)
                        mm.then_inc(ksum_done, 1)
                    pe.wait_ge(sig_a, KT)
                    pe.wait_ge(kk_ready, KT)
                    pe.wait_ge(decay_done, 1)
                    for j, (i, src) in enumerate(SAMPLE_ROWS):
                        if j >= 2:
                            pe.wait_ge(srow_copied, j - 1)
                        if src is rw_k:
                            pe.wait_ge(keys_ready, KT)
                        for k in range(KT):
                            cols = src[:, k, :] if src is decay_s else src[:, k, TP:T]
                            mm = pe.transpose(bank[2 * (j % 2) + k // 4][0:NS, (k % 4) * P:(k % 4 + 1) * P], cols,
                                              ident[:, :])
                        mm.then_inc(srow_turned, 1)
                    pe.wait_ge(syrow_loaded, 16)
                    pe.wait_ge(srow_copied, 6)
                    for k in range(KT):
                        mm = pe.transpose(bank[0][:, k * NS:(k + 1) * NS], s_rows[:, 0, k * P:(k + 1) * P],
                                          ident[0:NS, 0:NS])
                    mm.then_inc(srow_turned, 1)
                    pe.wait_ge(srow_copied, 7)

                    def scores_among(w, q, i):
                        b, o = bd[q], bank[4 + (i + 1) % 4]
                        if i == 0:
                            pe.wait_ge(bd_ready, w + 1)
                        pe.matmul(o[:, 0:P], b["Z"][:, i, :], b["B"][:, i, :], start=True, stop=True)
                        pe.matmul(o[:, P:2 * P], b["B"][:, i, :], b["Z"][:, i, :], start=True, stop=True)
                        pe.matmul(o[:, 2 * P:2 * P + HD], b["B"][:, i, :], b["R"][:, i, :], start=True, stop=True)

                    def scores_of_keys(w, q, i):
                        b, o = bd[q], bank[4 + (i + 1) % 4]
                        pe.matmul(o[:, 2 * P + HD:3 * P + HD], b["K"][:, i, :], b["Z"][:, i, :], start=True, stop=True)
                        pe.matmul(o[:, 3 * P + HD:4 * P], b["K"][:, i, :], b["R"][:, i, :], start=True,
                                  stop=True).then_inc(sc_done, 1)

                    def turn(q, nm, bk):
                        for i in range(4):
                            mm = pe.transpose(bank[bk][:, i * P:(i + 1) * P], bd[q][nm][:, i, :], ident[:, :])
                        mm.then_inc(tok_done, 1)

                    def scan_step(c, q, one_more):
                        w, b = 2 * c + q, bd[q]
                        for lvl in range(len(LEVELS)):
                            for g in range(2):
                                pe.wait_ge(ct_ready, 10 * w + 2 * lvl + g + 1)
                                pe.wait_ge(mmt_ready, 12 * w + 2 * lvl + g + 1)
                                for i in range(2):
                                    mm = pe.matmul(bank[2 * g][:, i * P:(i + 1) * P], ct[:, 2 * g + i, :],
                                                   mmt[:, 2 * g + i, 0:P], start=True, stop=True)
                                mm.then_inc(t1_mm, 1)
                            if lvl == 0:
                                pe.wait_ge(st_updated, w + 1)
                                pe.wait_ge(tok_ready, 3 * w + 1)
                                for i in range(4):
                                    o = bank[4][:, i * P:(i + 1) * P]
                                    pe.matmul(o, b["Z"][:, i, :], rw_ST[:, 4 * q + i, :], start=True, stop=False)
                                    mm = pe.matmul(o, sc[q][:, i, 2 * P + HD:3 * P + HD], tok[:, i, 2 * P:3 * P],
                                                   start=False, stop=True)
                                mm.then_inc(rhs_mm, 1)
                                pe.wait_ge(tok_ready, 3 * w + 3)
                            if one_more and lvl < 4:
                                if lvl == 1:
                                    pe.wait_ge(y_ready, w + 1)
                                elif lvl == 2:
                                    pe.wait_ge(st_updated, w + 2)
                                elif lvl == 3:
                                    pe.wait_ge(rhs_ready, w + 1)
                                scores_among(w + 1, 1 - q, lvl)
                            for g in range(2):
                                pe.wait_ge(t1_ready, 10 * w + 2 * lvl + g + 1)
                                for i in range(2):
                                    z = 2 * g + i
                                    if lvl < len(LEVELS) - 1:
                                        pe.matmul(bank[2 * g + 1][:, 2 * i * P:(2 * i + 1) * P],
                                                  mmt[:, z, P:2 * P], t1[:, z, :], start=True, stop=True)
                                    mm = pe.matmul(bank[2 * g + 1][:, (2 * i + 1) * P:(2 * i + 2) * P], t1[:, z, :],
                                                   mmt[:, z, P:2 * P], start=True, stop=True)
                                mm.then_inc(d_mm, 1)
                            if one_more and lvl < 4:
                                scores_of_keys(w + 1, 1 - q, lvl)
                        if one_more:
                            pe.wait_ge(scores_masked, 4 * w + 8)
                            pe.wait_ge(vf_ready, w + 2)
                            turn(1 - q, "Vf", 4)
                        pe.wait_ge(rhs_ready, w + 1)
                        for i in range(4):
                            if i % 2 == 0:
                                pe.wait_ge(mmt_ready, 12 * w + 11 + i // 2)
                            mm = pe.matmul(bank[5][:, i * P:(i + 1) * P], mmt[:, i, P:2 * P], rhs_sb[:, i, :],
                                           start=True, stop=True)
                        mm.then_inc(u_mm, 1)
                        if one_more:
                            pe.wait_ge(hat_ready, w + 2)
                            turn(1 - q, "Bh", 1)
                            turn(1 - q, "Kh", 3)
                        pe.wait_ge(uu_ready, w + 1)
                        pe.wait_ge(y_ready, w + 1)
                        for i in range(4):
                            o = bank[6][:, i * HD:(i + 1) * HD]
                            pe.matmul(o, rw_ST[:, 4 * q + i, :], b["R"][:, i, :], start=True, stop=False)
                            pe.matmul(o, tok[:, i, 2 * P:3 * P], sc[q][:, i, 3 * P + HD:4 * P], start=False, stop=False)
                            mm = pe.matmul(o, uu[:, i, :], sc[q][:, i, 2 * P:2 * P + HD], start=False, stop=True)
                        mm.then_inc(y_mm, 1)
                        pe.wait_ge(st_updated, w + 2)
                        for i in range(4):
                            o = bank[7][:, i * P:(i + 1) * P]
                            pe.matmul(o, tok[:, i, 0:P], uu[:, i, :], start=True, stop=False)
                            mm = pe.matmul(o, tok[:, i, P:2 * P], tok[:, i, 2 * P:3 * P], start=False, stop=True)
                        mm.then_inc(st_mm, 1)

                    for i in range(4):
                        scores_among(0, 0, i)
                        scores_of_keys(0, 0, i)
                    pe.wait_ge(vf_ready, 1)
                    pe.wait_ge(scores_masked, 4)
                    turn(0, "Vf", 4)
                    pe.wait_ge(hat_ready, 1)
                    turn(0, "Bh", 1)
                    turn(0, "Kh", 3)
                    with pe.Fori(0, NCH - 1) as c:
                        for q in range(2):
                            scan_step(c, q, True)
                    for q in range(2):
                        scan_step(NCH - 1, q, q == 0)
                    pe.wait_ge(st_updated, 2 * NCH + 2)
                    for k in range(KT):
                        mm = pe.transpose(bank[k // 4][:, (k % 4) * P:(k % 4 + 1) * P], rw_ST[:, k, :], ident[:, :])
                    mm.then_inc(srow_turned, 1)
                    pe.wait_ge(wkv_copied, 1)
                    pe.wait_ge(y_ready, 2 * NCH + 1)
                    pe.wait_ge(g2_loaded, 16)
                    for k in range(KT + 2):
                        if k < KT:
                            if k:
                                pe.wait_ge(centred, k)
                            for half in range(2):
                                mm = pe.matmul(tile_ps[0][half][:, 0:HALF], pair_ones[:, :],
                                               rw_y[:, k, half * HALF:(half + 1) * HALF], start=True, stop=True)
                            mm.then_inc(mean_mm, 1)
                        if 1 <= k <= KT:
                            j = k - 1
                            pe.wait_ge(csq_done, j + 1)
                            if j:
                                pe.wait_ge(gstd_done, j)
                            for half in range(2):
                                mm = pe.matmul(tile_ps[1][half][:, 0:HALF], pair_ones[:, :],
                                               gn_tmp[:, j % 2, half * HALF:(half + 1) * HALF], start=True, stop=True)
                            mm.then_inc(var_mm, 1)
                            pe.wait_ge(rk_ready, j + 1)
                            if j:
                                pe.wait_ge(ynorm_done, j)
                            for half in range(2):
                                mm = pe.matmul(ss_ps[half][:, 0:HALF], pair_ones[:, :],
                                               rw_r[:, j, half * HALF:(half + 1) * HALF], start=True, stop=True)
                            mm.then_inc(bonus_mm, 1)
                        if k >= 2:
                            j = k - 2
                            if j:
                                pe.wait_ge(gated, j)
                            for half in range(2):
                                for i in range(2):
                                    mm = pe.matmul(bank[6 + half][:, 0:HALF], g2[:, i, j * P:(j + 1) * P],
                                                   t_g[:, i, half * HALF:(half + 1) * HALF], start=(i == 0),
                                                   stop=(i == 1))
                            mm.then_inc(g_mm, 1)
                elif p["kind"] == "out":
                    xh, xl, ready, r0 = p["x"]
                    with pe.Fori(0, p["iters"]) as it:
                        for e in range(2):
                            pe.wait_ge(tile_free[e], t0 // 2 + it + 1)
                            gemm(n0 + 2 * it + e, e, e, xh, xl, 0, KT, True, True, (ready, r0) if e == 0 else None)
                elif p["kind"] == "up":
                    pe.wait_ge(std_done, p["norm"])

                    def hidden_tile(it, e, first=False):
                        q = q0 + 2 * it + e
                        turn_state(q, q0 // 2 + it, e)
                        if first:
                            pe.wait_ge(tile_free[0], t0 // 2 + 1)
                            pe.wait_ge(tile_free[1], t0 // 2 + 1)
                            gemm_pair(n0, u_hi, u_lo, (u_ready, KT * (p["split"] - 1)))
                        else:
                            for part in range(2):
                                pe.wait_ge(tile_free[part], t0 // 2 + 2 * it + e + 1)
                                gemm(n0 + 4 * it + 2 * e + part, part, part, u_hi, u_lo, 0, KT, True, True)
                        turn_tail(q, e)

                    hidden_tile(0, 0, True)
                    hidden_tile(0, 1)
                    with pe.Fori(1, p["iters"]) as it:
                        for e in range(2):
                            hidden_tile(it, e)
                elif p["kind"] == "down":
                    if l + 1 < depth:
                        pe.wait_ge(mod_ready, ada_group(p))
                    with pe.Fori(0, p["iters"]) as it:
                        for e in range(2):
                            pe.wait_ge(tile_free[e], t0 // 2 + it + 1)
                            for i, (k0, nk) in enumerate(DOWN_K):
                                k = 3 * e + i
                                gemm(n0 + 6 * it + k, k % 2, e, hid_hi, hid_lo, k0, nk, i == 0, i == 2,
                                     (hid_ready, p["unit"] - FT + k0) if e == 0 else None)
                                if l + 1 < depth:
                                    ada_tile(a0 + 6 * it + k, a0 // 2 + 3 * it + k // 2, k % 2, 6 * it + k)
            pe.wait_ge(h_ready, KT * (2 * depth + 1))
            for t in range(5):
                n = P if t < 4 else NS
                for g in range(2):
                    b = bank[(2 * t + g) % 8]
                    if t == 4:
                        pe.wait_ge((y_left, y_right)[g], 1)
                    for k in range(4):
                        mm = pe.transpose(b[0:n, k * P:(k + 1) * P], h[:, 4 * g + k, t * P:t * P + n], ident[:, :])
                    mm.then_inc(y_turned, 1)

        @block.vector
        def _(dve):
            step = [0]
            base = [0]

            def link(ins):
                step[0] += 1
                ins.then_inc(dve_step, 1)
                dve.wait_ge(dve_step, base[0] + step[0])

            def loop_steps(per, it):
                base[0] = base[0] + step[0] + per * it
                step[0] = 0

            def after_loop(b, s, per, iters):
                base[0], step[0] = b + s + per * iters, 0

            dve.memset(gate[:, :, :], 0.0).then_inc(conv_done, 2)
            dve.wait_ge(pro_turned, KT + 1)
            dve.tensor_copy(h[:, :, TP:T], bank[0][:, 0:KT * NS].rearrange("p (k s) -> p k s", k=KT))\
               .then_inc(small_copied, 1)
            dve.wait_ge(pro_turned, KT + 2)
            dve.tensor_copy(cT[:, :, :], bank[1][:, 0:KT * NSEQ].rearrange("p (k s) -> p k s", k=KT))\
               .then_inc(small_copied, 1)
            dve.wait_ge(pro_turned, KT + 3)
            dve.tensor_copy(vecs[:, 0:512], bank[2][:, :])
            link(dve.tensor_copy(vecs[:, 512:nrow], bank[3][:, 0:nrow - 512]))
            for s in (small_copied, tile_free[0], tile_free[1]):
                dve.sem_inc(s, 1)
            dve.wait_ge(x_copied, KT)
            for k in range(KT):
                dve.sem_inc(h_ready, 1)

            def modulation(l, half, mod):
                g = 2 * l + half
                dve.wait_ge(ada_used, GT * (g + 1) + 2)
                bias = vecs[:, col["ada_b"] + l * MODT + half * GT:col["ada_b"] + l * MODT + (half + 1) * GT]
                dst = mod[:, :, :]
                link(dve.tensor_tensor(dst, ada_ps[:, 0:GT * NSEQ].rearrange("p (t s) -> p t s", s=NSEQ),
                                       bias.unsqueeze(2).to_broadcast([P, GT, NSEQ]), ALU.add))
                link(dve.tensor_scalar(mod[:, KT:2 * KT, :], mod[:, KT:2 * KT, :], 1.0, None, ALU.add))
                for i in range(2):
                    c0 = col["norm_g"] + (l * 4 + 2 * half + i) * KT
                    gain = vecs[:, c0:c0 + KT].unsqueeze(2).to_broadcast([P, KT, NSEQ])
                    part = mod[:, (i + 1) * KT:(i + 2) * KT, :]
                    ins = dve.tensor_tensor(part, part, gain, ALU.mult)
                    if i == 1:
                        ins.then_inc(mod_ready, 1)
                    else:
                        link(ins)
                dve.wait_ge(mod_ready, g + 1)

            for i in range(GT // PRO_T):
                dve.wait_ge(pro_mod_mm, i + 1)
                if i >= 2:
                    dve.wait_ge(ada_used, 2 + (i - 1) * PRO_T)
                dve.tensor_copy(mod_rows[:, i % 2, :], bank[i % 2][0:NSEQ, :]).then_inc(pro_mod_copied, 1)
            modulation(0, 0, mod_m)

            def conv3(q, e, name, row0, m, ft):
                w = [vec(name, row0 + j * ft + m) for j in range(3)]
                link(dve.tensor_scalar(conv[:, e, 0:CWD], gate[:, e, 0:CWD], w[0], None, ALU.mult))
                link(dve.scalar_tensor_tensor(conv[:, e, 0:CWD], gate[:, e, 1:1 + CWD], w[1], conv[:, e, 0:CWD],
                                              ALU.mult, ALU.add))
                dve.scalar_tensor_tensor(conv[:, e, 0:CWD], gate[:, e, 2:2 + CWD], w[2], conv[:, e, 0:CWD],
                                         ALU.mult, ALU.add).then_inc(conv_done, 1)
                dve.wait_ge(conv_done, q + 3)

            def times_tile(e, slot, t_after):
                dve.tensor_tensor(prod[:, e, 0:HALF], conv[:, e, 0:HALF], tile_ps[slot][0][:, 0:HALF], ALU.mult)
                dve.tensor_tensor(prod[:, e, HALF:TP], conv[:, e, HALF:TP], tile_ps[slot][1][:, 0:TP - HALF], ALU.mult)
                dve.tensor_tensor(prod[:, e, TP:T], conv[:, e, TP + 2:CWD:3], tile_ps[slot][1][:, TP - HALF:HALF],
                                  ALU.mult).then_inc(tile_free[slot], 1)
                dve.wait_ge(tile_free[slot], t_after)

            def split_hidden(e, m):
                hi = hid_hi[:, ds(m, 1), :].rearrange("p a t -> p (a t)")
                lo = hid_lo[:, ds(m, 1), :].rearrange("p a t -> p (a t)")
                link(dve.tensor_copy(hi, prod[:, e, :]))
                dve.tensor_tensor(lo, prod[:, e, :], hi.bitcast(F32), ALU.subtract).then_inc(hid_ready, 1)

            for p in plan:
                l, n0, q0, a0, t0 = p["l"], p["blk"], p["unit"], p["ada"], p["tile"]
                if p["kind"] == "pre":
                    i, mod = p["pre"], p["mod"]
                    dve.wait_ge(std_done, p["norm"] + 1)
                    link(dve.reciprocal(rstd[:, :], std[:, :]))
                    rs = rstd[:, TP:T].unsqueeze(1).to_broadcast([P, KT, NS])
                    link(dve.tensor_tensor(s8[:, 0], h[:, :, TP:T], rs, ALU.mult))
                    link(dve.tensor_tensor(s8[:, 0], s8[:, 0], mod[:, KT:2 * KT, 1:NSEQ], ALU.mult))
                    link(dve.tensor_tensor(s8[:, 0], s8[:, 0], mod[:, 0:KT, 1:NSEQ], ALU.add))
                    if i:
                        dve.wait_ge(block_done, n0 + 2)
                    if p["full"]:
                        dve.tensor_copy(rw_u[:, :, TP:T], s8[:, 0]).then_inc(us_ready, 1)
                        for k in range(KT):
                            if KT * i + k >= 2:
                                dve.wait_ge(usb_done, KT * i + k - 1)
                            dve.tensor_tensor(normed[:, k % 2, 0:TP], h[:, k, 0:TP], rstd[:, 0:TP], ALU.mult)\
                               .then_inc(norm_done, 1)
                        continue
                    for k in range(KT + 1):
                        if k < KT:
                            if KT * i + k >= 2:
                                dve.wait_ge(usb_done, KT * i + k - 1)
                            dve.tensor_tensor(normed[:, k % 2, 0:TP], h[:, k, 0:TP], rstd[:, 0:TP], ALU.mult)\
                               .then_inc(norm_done, 1)
                        if k == 0:
                            link(dve.tensor_copy(u_hi[:, :, TP:T], s8[:, 0]))
                            dve.tensor_tensor(u_lo[:, :, TP:T], s8[:, 0], u_hi[:, :, TP:T].bitcast(F32), ALU.subtract)
                        if k:
                            dve.wait_ge(usb_done, KT * i + k)
                            dve.tensor_copy(u_hi[:, k - 1, 0:TP], usb[:, (k - 1) % 2, 0:TP]).then_inc(uhi_done, 1)
                elif p["kind"] == "post":
                    mod, proj_x = p["mod"], p["proj"]
                    dve.wait_ge(std_done, p["norm"] + 1)
                    link(dve.reciprocal(rstd[:, :], std[:, :]))
                    dve.sem_inc(rstd_ready, 1)
                    rs = rstd[:, TP:T].unsqueeze(1).to_broadcast([P, KT, NS])
                    link(dve.tensor_tensor(s8[:, 0], proj_x[:, :, TP:T], rs, ALU.mult))
                    link(dve.tensor_tensor(s8[:, 0], s8[:, 0], mod[:, 2 * KT:3 * KT, 1:NSEQ], ALU.mult))
                    link(dve.tensor_tensor(h[:, :, TP:T], h[:, :, TP:T], s8[:, 0], ALU.add))
                    for k in range(KT):
                        if k in POOL_TILES:
                            dve.wait_ge(tile_scaled, p["post"] * len(POOL_TILES) + POOL_TILES.index(k) + 1)
                        else:
                            link(dve.tensor_tensor(proj_x[:, k, 0:TP], proj_x[:, k, 0:TP], rstd[:, 0:TP], ALU.mult))
                        dve.scalar_tensor_tensor(h[:, k, 0:TP], proj_x[:, k, 0:TP], mod[:, 2 * KT + k, 0:1],
                                                 h[:, k, 0:TP], ALU.mult, ALU.add).then_inc(h_ready, 1)
                elif p["kind"] == "sconv":
                    j = l // 3
                    b, s, PER = base[0], step[0], 2 * 3
                    with dve.Fori(0, p["iters"]) as it:
                        loop_steps(PER, it)
                        for e in range(2):
                            q, m, n, k = q0 + 2 * it + e, 2 * it + e, n0 + 6 * it + 3 * e, 3 * e
                            dve.wait_ge(tile_free[k % 2], t0 // 2 + 3 * it + k // 2 + 2)
                            dve.wait_ge(block_done, n + 4)
                            sl = (k + 1) % 2
                            dve.tensor_tensor(gate[:, e, 2:2 + HALF], csb[:, e, 0:HALF], tile_ps[sl][0][:, 0:HALF],
                                              ALU.mult)
                            dve.tensor_tensor(gate[:, e, 2 + HALF:2 + TP], csb[:, e, HALF:TP],
                                              tile_ps[sl][1][:, 0:TP - HALF], ALU.mult)
                            dve.tensor_tensor(gate[:, e, TP + 4:GW:3], csb[:, e, TP:T],
                                              tile_ps[sl][1][:, TP - HALF:HALF], ALU.mult).then_inc(gate_ready, 1)
                            dve.wait_ge(gate_ready, q + 1)
                            dve.sem_inc(tile_free[sl], 1)
                            conv3(q, e, "sconv_conv_w", j * 3 * KT, m, KT)
                            dve.wait_ge(block_done, n + 5)
                            times_tile(e, k % 2, t0 // 2 + 3 * it + (k + 2) // 2 + 2)
                            split_hidden(e, m)
                        assert step[0] == PER
                    after_loop(b, s, PER, p["iters"])
                    modulation(l, 1, mod_f)
                elif p["kind"] == "rproj":
                    dve.wait_ge(shift_turned, 1)
                    link(dve.tensor_copy(prev_s[:, :, :], bank[5][:, 0:KT * NS].rearrange("p (k s) -> p k s", k=KT)))
                    dve.wait_ge(usb_done, KT * p["pre"])
                    link(dve.tensor_tensor(rw_d[:, :, TP:T], prev_s[:, :, :], rw_u[:, :, TP:T], ALU.subtract))

                    def mix_low(m):
                        hi, lo = ((u_hi, u_lo), (xb_hi, xb_lo))[m // KT % 2]
                        dve.wait_ge(xhi_done, m + 1)
                        dve.tensor_tensor(lo[:, m % KT, :], mix_tile(m), hi[:, m % KT, :].bitcast(F32),
                                          ALU.subtract).then_inc(x_ready[1], 1)

                    for o, i in enumerate((1, 4, 5, 0, 2, 3)):
                        for k in range(KT):
                            m = KT * o + k
                            if o == 0:
                                dve.tensor_scalar(rw_d[:, k, 0:1], rw_u[:, k, 0:1], -1.0, None, ALU.mult)
                                link(dve.tensor_tensor(rw_d[:, k, 1:TP], rw_u[:, k, 0:TP - 1], rw_u[:, k, 1:TP],
                                                       ALU.subtract))
                            if o == 5:
                                dve.wait_ge(x_ready[k % 2], m // 2)
                            elif m >= 4:
                                dve.wait_ge(x_ready[k % 2], m // 2 - 1)
                            dve.scalar_tensor_tensor(mix_tile(m), rw_d[:, k, :], vec("rwkv_mu", i * KT + k),
                                                     rw_u[:, k, :], ALU.mult, ALU.add).then_inc(mixed, 1)
                            if m and k % 2 == 0:
                                mix_low(m - 1)
                    mix_low(KT * 6 - 1)
                    modulation(l, 1, mod_f)
                elif p["kind"] == "gproj":
                    modulation(l, 1, mod_f)
                elif p["kind"] == "gla":
                    dve.wait_ge(gz_done, GH)
                    link(dve.tensor_scalar(g_z[:, :, :], g_z[:, :, :], 0.0, None, ALU.min))
                    dve.wait_ge(ggate_done, G_SOFT)
                    zf, ef = (x[:, :, :].rearrange("p h t -> p (h t)") for x in (g_z, g_e))
                    link(dve.scalar_tensor_tensor(zf, ef, -1.0, zf, ALU.mult, ALU.add))
                    dve.tensor_scalar(g_z[:, :, :], g_z[:, :, :], 1.0 / 16.0, None, ALU.mult).then_inc(gargs_ready, 1)
                    dve.wait_ge(gargs_ready, G_LOG)
                    dve.tensor_scalar(g_q, g_q, float(P) ** -0.5, None, ALU.mult).then_inc(gq_ready, 1)
                    link(dve.memset(g_Ql[:, 0, :], 1.0))
                    link(dve.memset(g_Ql[:, 0, 0:TP:GC], 0.0))
                    for hd in range(GH):
                        ins = dve.tensor_tensor_scan(g_G[:, hd, :], g_Ql[:, 0, :], g_z[:, hd, 0:TP], 0.0, ALU.mult,
                                                     ALU.add)
                    ins.then_inc(gargs_ready, 1)
                    dve.wait_ge(gargs_ready, G_SUM)
                    dve.wait_ge(ggate_done, G_DEC)
                    for hd in range(GH):
                        Gh = g_G[:, hd, :].rearrange("p (c t) -> p c t", t=GC)
                        ins = dve.tensor_tensor(g_z[:, hd, 0:TP].rearrange("p (c t) -> p c t", t=GC),
                                                Gh[:, :, GC - 1:GC].to_broadcast([P, NGC, GC]), Gh, ALU.subtract)
                    ins.then_inc(gargs_ready, 1)
                    dve.wait_ge(gexp_done, 2)
                    dve.wait_ge(gq_ready, 1)
                    dve.tensor_tensor(g_e[:, :, 0:TP], g_q[:, :, 0:TP], g_e[:, :, 0:TP], ALU.mult).then_inc(gq_ready, 1)
                    dve.wait_ge(gexp_done, 3)
                    dve.tensor_tensor(g_Kl[:, :, :], g_k[:, :, 0:TP], g_z[:, :, 0:TP], ALU.mult).then_inc(gkhat_ready, 1)
                    link(dve.memset(g_Ql[:, :, :], 0.0))
                    link(dve.memset(g_AT[:, :, :], 0.0))
                    link(dve.memset(g_S[:, :, :], 0.0))
                    dve.sem_inc(gS_ready, 1)
                    dve.wait_ge(g_turned, G_K)

                    def put(n, s, mask):
                        dve.wait_ge(glevel_mm, 2 * n + s + 1)
                        if n:
                            dve.wait_ge(glevel_put, 2 * (n - 1) + s + 1)
                        for c in (2 * s, 2 * s + 1):
                            if mask is None:
                                ins = dve.tensor_copy(
                                    g_AT[0:64, c * GH:(c + 1) * GH, 64:P],
                                    bank[c][0:64, :].rearrange("p (h t) -> p h t", h=GH)[:, :, 64:P])
                            else:
                                ins = dve.copy_predicated(
                                    g_AT[:, c * GH:(c + 1) * GH, :],
                                    mask.unsqueeze(1).to_broadcast([P, GH, P]).bitcast(mybir.dt.uint32),
                                    bank[c][:, :].rearrange("p (h t) -> p h t", h=GH))
                        ins.then_inc(glevel_put, 1)

                    def decayed(lvl, s):
                        z = G_LEVELS[lvl]
                        half = lambda x: x[:, :, s * 2 * GC:(s + 1) * 2 * GC].rearrange("p h (b t) -> p h b t", t=2 * z)
                        e = half((g_z2, g_z)[lvl % 2])
                        dve.tensor_tensor(half(g_Ql)[:, :, :, z:2 * z], half(g_q)[:, :, :, z:2 * z], e[:, :, :, z:2 * z],
                                          ALU.mult)
                        dve.tensor_tensor(half(g_Kl)[:, :, :, 0:z], half(g_k)[:, :, :, 0:z], e[:, :, :, 0:z],
                                          ALU.mult).then_inc(glevel_ready, 1)

                    def sample(b):
                        dve.wait_ge(gvb_mm, b + 1)
                        dve.wait_ge(gs_decayed, b + 1)
                        for hd in range(GH):
                            x = b * GH + hd
                            vb = bank[4 + hd // 2][:, (hd % 2) * GDV:(hd % 2 + 1) * GDV]
                            ins = dve.scalar_tensor_tensor(g_sS[:, x, :], vb, g_k[:, hd, TP + b:TP + b + 1],
                                                           g_sS[:, x, :], ALU.mult, ALU.add)
                        ins.then_inc(gs_ready, 1)
                        dve.wait_ge(gs_ready, b + 1)
                        dve.sem_inc(gvb_used, 1)

                    for s in range(2):
                        put(0, s, ident[:, :])
                    for b in range(NS):
                        sample(b)
                    for lvl in range(len(G_LEVELS) + 1):
                        for s in range(2):
                            if lvl:
                                z = G_LEVELS[lvl - 1]
                                put(lvl, s, None if z == 64 else up_masks[:, z.bit_length() - 1, :])
                            if lvl < len(G_LEVELS):
                                dve.wait_ge(gexp_done, 4 + lvl)
                                decayed(lvl, s)
                    dve.wait_ge(gexp_done, 1)
                    for c in range(NGC):
                        dve.wait_ge(gsu_mm, c + 1)
                        dve.wait_ge(gS_ready, GH * c + 1)
                        for hd in range(GH):
                            dve.scalar_tensor_tensor(
                                g_S[:, hd, :], g_S[:, hd, :], g_end[:, hd, c:c + 1],
                                bank[4 + hd // 2][:, (hd % 2) * GDV:(hd % 2 + 1) * GDV], ALU.mult, ALU.add)\
                               .then_inc(gS_ready, 1)
                    for hd in range(GH):
                        dve.wait_ge(gon_std, hd + 1)
                        dve.reciprocal(rstd[:, :], std[:, :]).then_inc(gon_done, 1)
                        dve.wait_ge(gon_done, hd + 1)
                        for i in range(2):
                            k = 2 * hd + i
                            dve.wait_ge(g_pool_done, G_GATED + k + 1)
                            if k >= 2:
                                dve.wait_ge(gy_ready, k - 1)
                            link(dve.scalar_tensor_tensor(prod[:, k % 2, :], g_og[:, k, :], vec("gla_onorm_g", i),
                                                          rstd[:, :], ALU.mult, ALU.mult))
                            dve.tensor_copy(u_hi[:, k, :], prod[:, k % 2, :]).then_inc(gyhi_done, 1)
                    dve.wait_ge(gyhi_done, KT)
                    dve.wait_ge(gss_mm, GH)
                    link(dve.memset(gate[:, :, 0:2], 0.0))
                elif p["kind"] == "rwkv":
                    link(dve.tensor_scalar(one_less_ka[:, :], vecs[:, col["rwkv_k_a"]:col["rwkv_k_a"] + KT], -1.0, 1.0,
                                           ALU.mult, ALU.add))
                    link(dve.memset(tmp8[:, 5, 0:TP], 1.0))
                    link(dve.memset(tmp8[:, 5, 0:TP:HD], 0.0))
                    for k in range(KT):
                        dve.wait_ge(sig_w, k + 1)
                        link(dve.tensor_scalar(rw_G[:, k, :], rw_G[:, k, :], DECAY, None, ALU.mult))
                        link(dve.tensor_tensor_scan(tmp8[:, 6 + k % 2, 0:TP], tmp8[:, 5, 0:TP], rw_G[:, k, 0:TP], 0.0,
                                                    ALU.mult, ALU.add))
                        link(dve.tensor_copy(rw_G[:, k, 0:TP], tmp8[:, 6 + k % 2, 0:TP]))
                    dve.sem_inc(prep_done, 1)
                    for k in range(KT):
                        dve.wait_ge(sig_a, KT)
                        dve.wait_ge(knorm_done, k + 1)
                        nr = tmp8[:, 2 + k % 2, :]
                        link(dve.tensor_scalar(nr, nr, 1e-12, None, ALU.max))
                        link(dve.reciprocal(nr, nr))
                        link(dve.scalar_tensor_tensor(rw_kk[:, k, :], rw_k[:, k, :], vec("rwkv_k_k", k), nr, ALU.mult,
                                                      ALU.mult))
                        dve.scalar_tensor_tensor(rw_b[:, k, :], rw_kk[:, k, :], -1.0, rw_b[:, k, :], ALU.mult,
                                                 ALU.mult).then_inc(kk_ready, 1)
                    dve.wait_ge(keys_ready, KT)
                    dve.wait_ge(kk_ready, KT)
                    dve.wait_ge(svec_loaded, 96)
                    dve.wait_ge(sstate_loaded, 16)
                    rows_of = lambda i: s_vec[:, i, :].unsqueeze(1).to_broadcast([P, HD, HD])
                    cols_of = lambda i: s_vec[:, i, :].unsqueeze(2).to_broadcast([P, HD, HD])
                    S, W = s_state[:, :, :], s_tmp[:, :, :]
                    link(dve.tensor_tensor(W, S, rows_of(3), ALU.mult))
                    link(dve.tensor_reduce(s_vec[:, 6, :], W, AX.X, ALU.add))
                    link(dve.tensor_tensor(S, S, rows_of(5), ALU.mult))
                    link(dve.tensor_tensor(W, cols_of(6), rows_of(4), ALU.mult))
                    link(dve.tensor_tensor(S, S, W, ALU.add))
                    link(dve.tensor_tensor(W, cols_of(2), rows_of(1), ALU.mult))
                    link(dve.tensor_tensor(S, S, W, ALU.add))
                    link(dve.tensor_tensor(W, S, rows_of(0), ALU.mult))
                    dve.tensor_reduce(s_vec[:, 7, :], W, AX.X, ALU.add).then_inc(s_y_done, 1)
                    dve.wait_ge(s_state_out, 16)
                    dve.wait_ge(s_y_done, 1)
                    for q in range(2):
                        for nm in ("Z", "B", "K", "Bh", "Kh", "Vf"):
                            ins = dve.memset(bd[q][nm][:, :, :], 0.0)
                        ins.then_inc(bd_zeroed, 1)
                        link(dve.memset(bd[q]["Ep"][:, :, 0:1], 1.0))
                    dve.wait_ge(bd_zeroed, 2)
                    dve.wait_ge(srow_turned, 7)
                    link(dve.memset(rw_ST[:, :, :], 0.0))
                    dve.sem_inc(st_updated, 2)
                    dve.wait_ge(masks_ready, 1)

                    def build(c, q, hh):
                        b, qs, now = bd[q], slice(4 * q, 4 * q + 4), ds(HD * c, HD)
                        rs = slice(hh * HD, (hh + 1) * HD)
                        dve.tensor_tensor(b["Z"][rs, :, rs], rw_kk[rs, qs, now], b["Ep"][rs, :, 0:HD], ALU.mult)
                        dve.tensor_tensor(b["K"][rs, :, rs], rw_k[rs, qs, now], b["Em"][rs, :, :], ALU.mult)
                        return dve.tensor_tensor(b["B"][rs, :, rs], rw_b[rs, qs, now], b["Em"][rs, :, :], ALU.mult)

                    def hat(q, nm, src):
                        end = bd[q]["Ep"][:, :, HD:HD + 1].to_broadcast([P, 4, P])
                        return dve.tensor_tensor(bd[q][nm][:, :, :], bd[q][src][:, :, :], end, ALU.mult)

                    def receptances(c, q):
                        b = bd[q]
                        dve.tensor_tensor(b["R"][:, :, :], rw_r[:, 4 * q:4 * q + 4, ds(HD * c, HD)],
                                          b["Ep"][:, :, 1:HD + 1], ALU.mult)
                        dve.tensor_copy(end_decay[:, q, :], b["Ep"][:, :, HD:HD + 1].rearrange("p i a -> p (i a)"))\
                           .then_inc(bd_ready, 1)

                    def mask_scores(w, q, i):
                        dve.wait_ge(sc_done, 4 * w + i + 1)
                        dve.tensor_tensor(sc[q][:, i, :], bank[4 + (i + 1) % 4][:, :], sc_mask[:, :], ALU.mult)\
                           .then_inc(scores_masked, 1)

                    def first_inverse(w, q):
                        lm = low_mask[:, :].unsqueeze(1).to_broadcast([P, 2, P])
                        um = up_masks[:, 0, :].unsqueeze(1).to_broadcast([P, 2, P])
                        idb = ident[:, :].unsqueeze(1).to_broadcast([P, 4, P])
                        dve.wait_ge(scores_masked, 4 * w + 4)
                        for g in range(2):
                            gs = slice(2 * g, 2 * g + 2)
                            dve.tensor_tensor(mmt[:, gs, 0:P], sc[q][:, gs, 0:P], lm, ALU.mult)
                            link(dve.tensor_tensor(mmt[:, gs, P:2 * P], sc[q][:, gs, P:2 * P], um, ALU.mult))
                            mv = mmt[:, gs, :].rearrange("p i (two t) -> p (i two) t", two=2)
                            dve.tensor_tensor(mv, mv, idb, ALU.add).then_inc(mmt_ready, 1)

                    def scan_step(c, q, one_more, two_more):
                        w = 2 * c + q
                        for lvl in range(len(LEVELS)):
                            for g in range(2):
                                gs = slice(2 * g, 2 * g + 2)
                                dve.wait_ge(d_mm, 10 * w + 2 * lvl + g + 1)
                                dve.wait_ge(mmt_ready, 12 * w + 2 * lvl + g + 1)
                                dv = bank[2 * g + 1][:, :].rearrange("p (i t) -> p i t", i=2)
                                lo = 0 if lvl < len(LEVELS) - 1 else P
                                dve.tensor_tensor(mmt[:, gs, lo:2 * P], mmt[:, gs, lo:2 * P], dv[:, :, lo:2 * P],
                                                  ALU.add).then_inc(mmt_ready, 1)
                            if one_more and lvl < 4:
                                mask_scores(w + 1, 1 - q, lvl)
                            if two_more:
                                if lvl == 1:
                                    dve.wait_ge(exp_done, w + 3)
                                    dve.wait_ge(tok_done, 3 * w + 3)
                                    build(c + 1, q, 0)
                                elif lvl == 2:
                                    link(build(c + 1, q, 1))
                                elif lvl == 3:
                                    hat(q, "Bh", "B")
                                    hat(q, "Kh", "K").then_inc(hat_ready, 1)
                        if one_more:
                            dve.wait_ge(u_mm, w + 1)
                            first_inverse(w + 1, 1 - q)
                        dve.wait_ge(st_mm, w + 1)
                        for i in range(4):
                            ins = dve.scalar_tensor_tensor(rw_ST[:, 4 * q + i, :], rw_ST[:, 4 * q + i, :],
                                                           end_decay[:, q, i:i + 1], bank[7][:, i * P:(i + 1) * P],
                                                           ALU.mult, ALU.add)
                        ins.then_inc(st_updated, 1)
                        if two_more:
                            dve.wait_ge(st_updated, w + 3)
                            receptances(c + 1, q)

                    for q in range(2):
                        dve.wait_ge(exp_done, q + 1)
                        build(0, q, 0)
                        link(build(0, q, 1))
                        hat(q, "Bh", "B")
                        hat(q, "Kh", "K").then_inc(hat_ready, 1)
                        receptances(0, q)
                    dve.wait_ge(block_done, n0 + 2)
                    for i in range(4):
                        mask_scores(0, 0, i)
                    first_inverse(0, 0)
                    b0, s0, PER = base[0], step[0], 2 * 3
                    with dve.Fori(0, NCH - 1) as c:
                        loop_steps(PER, c)
                        for q in range(2):
                            scan_step(c, q, True, True)
                        assert step[0] == PER, step[0]
                    after_loop(b0, s0, PER, NCH - 1)
                    for q in range(2):
                        scan_step(NCH - 1, q, q == 0, False)
                    for k in range(KT + 2):
                        if k < KT:
                            dve.wait_ge(mean_mm, k + 1)
                            for half in range(2):
                                hs = slice(half * HALF, (half + 1) * HALF)
                                ins = dve.scalar_tensor_tensor(rw_y[:, k, hs], tile_ps[0][half][:, 0:HALF], -1.0 / HD,
                                                               rw_y[:, k, hs], ALU.mult, ALU.add)
                            ins.then_inc(centred, 1)
                            dve.scalar_tensor_tensor(rw_r[:, k, :], rw_r[:, k, :], vec("rwkv_r_k", k), rw_k[:, k, :],
                                                     ALU.mult, ALU.mult).then_inc(rk_ready, 1)
                        if 1 <= k <= KT:
                            j = k - 1
                            dve.wait_ge(gstd_done, j + 1)
                            nr = gn_tmp[:, 2 + j % 2, :]
                            link(dve.reciprocal(nr, nr))
                            dve.wait_ge(bonus_mm, j + 1)
                            for half in range(2):
                                hs = slice(half * HALF, (half + 1) * HALF)
                                dve.tensor_tensor(rw_v[:, j, hs], rw_v[:, j, hs], ss_ps[half][:, 0:HALF], ALU.mult)
                            dve.tensor_tensor(rw_y[:, j, :], rw_y[:, j, :], nr, ALU.mult).then_inc(ynorm_done, 1)
                        if k >= 2:
                            j = k - 2
                            dve.wait_ge(yaff_done, j + 1)
                            link(dve.tensor_tensor(rw_y[:, j, :], rw_y[:, j, :], rw_v[:, j, :], ALU.add))
                            dve.wait_ge(g_mm, j + 1)
                            if j >= 2:
                                dve.wait_ge(xy_ready, j - 1)
                            for half in range(2):
                                hs = slice(half * HALF, (half + 1) * HALF)
                                ins = dve.tensor_tensor(gated_sb[:, j % 2, hs], rw_y[:, j, hs],
                                                        bank[6 + half][:, 0:HALF], ALU.mult)
                            ins.then_inc(gated, 1)
                            dve.wait_ge(gated, j + 1)
                            dve.tensor_copy(u_hi[:, j, :], gated_sb[:, j % 2, :]).then_inc(yhi_done, 1)
                    link(dve.memset(gate[:, :, 0:2], 0.0))
                elif p["kind"] == "up":
                    b, s, PER = base[0], step[0], 2 * 3
                    with dve.Fori(0, p["iters"]) as it:
                        loop_steps(PER, it)
                        for e in range(2):
                            q, m, n = q0 + 2 * it + e, 2 * it + e, n0 + 4 * it + 2 * e
                            dve.wait_ge(gate_ready, q + 1)
                            conv3(q, e, "ffn_conv_w", l * 3 * FT, m, FT)
                            dve.wait_ge(block_done, n + 4)
                            dve.wait_ge(silu_done, p["up_unit"] + m + 1)
                            times_tile(e, 1, t0 // 2 + 2 * it + e + 2)
                            split_hidden(e, m)
                        assert step[0] == PER
                    after_loop(b, s, PER, p["iters"])
                elif p["kind"] in ("out", "down"):
                    link(dve.memset(csb[:, 0, :], 0.0))
                    b, s = base[0], step[0]
                    with dve.Fori(0, p["iters"]) as it:
                        loop_steps(4, it)
                        for e in range(2):
                            dve.wait_ge(tile_free[e], t0 // 2 + it + 2)
                            o = p["proj"][:, ds(2 * it + e, 1), :].rearrange("p a t -> p (a t)")
                            link(dve.tensor_tensor(csb[:, 1, :], o, o, ALU.mult))
                            link(dve.tensor_tensor(csb[:, 0, :], csb[:, 0, :], csb[:, 1, :], ALU.add))
                    after_loop(b, s, 4, p["iters"])
                    dve.sem_inc(sum_ready, 1)
                    if p["kind"] == "down" and l + 1 < depth:
                        modulation(l + 1, 0, mod_m)
            for k in range(5):
                dve.wait_ge(y_turned, 2 * k + 2)
                n = P if k < 4 else NS
                dve.tensor_copy(y_rows[0:n, k, 512:1024], bank[(2 * k + 1) % 8][0:n, :]).then_inc(y_right, 1)


_INS = ['x_prompt', 'x_sample', 'state_conv_a', 'state_shift_b', 'state_wkv_b', 'state_gla_c', 'state_conv_ffn',
        'c_prompt', 'c_sample', 'ada_w', 'ada_b', 'norm_g', 'sconv_w_in', 'sconv_conv_w', 'sconv_w_out',
        'rwkv_mu', 'rwkv_w_rkv', 'rwkv_w0', 'rwkv_w1', 'rwkv_w2', 'rwkv_a0', 'rwkv_a1', 'rwkv_a2', 'rwkv_g1',
        'rwkv_g2', 'rwkv_k_k', 'rwkv_k_a', 'rwkv_r_k', 'rwkv_lnx_w', 'rwkv_lnx_b', 'rwkv_w_o',
        'gla_w_in', 'gla_wa1', 'gla_wa2', 'gla_ba', 'gla_onorm_g', 'gla_w_o',
        'ffn_w_up', 'ffn_conv_w', 'ffn_conv_b', 'ffn_w_down']
_OUTS = [('y_prompt', (1, 512, 1024)), ('y_sample', (8, 1, 1024)),
         ('conv_a_prompt', (2, 1, 2, 1024)), ('conv_a_sample', (2, 8, 2, 1024)),
         ('shift_b_prompt', (1, 1, 1024)), ('shift_b_sample', (1, 8, 1024)),
         ('wkv_b_prompt', (1, 1, 16, 64, 64)), ('wkv_b_sample', (1, 8, 16, 64, 64)),
         ('gla_c_prompt', (1, 1, 4, 128, 256)), ('gla_c_sample', (1, 8, 4, 128, 256)),
         ('conv_ffn_prompt', (4, 1, 2, 2816)), ('conv_ffn_sample', (4, 8, 2, 2816))]


def kernel(**inputs):
    import numpy as _np
    import concourse.bacc as _bacc
    from concourse.bass_utils import run_bass_kernel_spmd as _run

    nc = _bacc.Bacc("TRN2", target_bir_lowering=False, num_devices=1)
    arrays, ins, outs = {}, {}, {}
    for name in _INS:
        a = _np.ascontiguousarray(inputs[name])
        arrays[f"in_{name}_dram"] = a
        ins[name] = nc.dram_tensor(f"in_{name}_dram", a.shape, F32, kind="ExternalInput").ap()
    for name, shape in _OUTS:
        outs[name] = nc.dram_tensor(f"out_{name}_dram", shape, F32, kind="ExternalOutput").ap()
    trunk_kernel(nc, ins, outs, 4)
    r = _run(nc, [arrays], core_ids=[0])
    return tuple(r.results[0][f"out_{name}_dram"] for name, _ in _OUTS)
```
